# Optimizing a Trainium2 kernel written in Bass

```python
import jax, jax.numpy as jnp
from jax import lax
import numpy as np
import math

D_MODEL = 1024
BATCH = 1
SEQ = 256
DEPTH = 1

HEAD_DIM = 64
N_HEADS_MOBA = 8
N_HEADS_SB = 8
D_MOBA = N_HEADS_MOBA * HEAD_DIM
D_SB = N_HEADS_SB * HEAD_DIM
MOBA_BLOCK = 256
MOBA_TOP_K = 3
Q_CHUNK = 128
ROPE_THETA = 500000.0
ROPE_DIM = HEAD_DIM // 4
D_FF = 2816
FFN_RES = 0.5
EPS = 1e-6
D_IN = 3 * D_MOBA + 3 * D_SB + 2 * D_MODEL
NEG = -1e30


def rms_norm(x, g):
    x32 = x.astype(jnp.float32)
    y = x32 * lax.rsqrt(jnp.mean(x32 * x32, axis=-1, keepdims=True) + EPS)
    return y.astype(x.dtype) * g

def swiglu(x, w_gate, w_up, w_down):
    return (jax.nn.silu(x @ w_gate) * (x @ w_up)) @ w_down

def partial_rotary(x, positions):
    half = ROPE_DIM // 2
    inv_freq = ROPE_THETA ** (-jnp.arange(half, dtype=jnp.float32) * 2.0 / ROPE_DIM)
    ang = positions.astype(jnp.float32)[:, None, :, None] * inv_freq
    cos = jnp.cos(ang).astype(x.dtype)
    sin = jnp.sin(ang).astype(x.dtype)
    x1, x2, rest = x[..., :half], x[..., half:ROPE_DIM], x[..., ROPE_DIM:]
    return jnp.concatenate([x1 * cos - x2 * sin, x2 * cos + x1 * sin, rest], axis=-1)

def split_heads(x, n):
    b, t, _ = x.shape
    return x.reshape(b, t, n, HEAD_DIM).transpose(0, 2, 1, 3)

def merge_heads(x):
    b, h, t, d = x.shape
    return x.transpose(0, 2, 1, 3).reshape(b, t, h * d)

def moba_attention(q, k, v):
    B, H, T, hd = q.shape
    nb = -(-T // MOBA_BLOCK)
    pad = nb * MOBA_BLOCK - T
    k_pad = jnp.pad(k, ((0, 0), (0, 0), (0, pad), (0, 0)))
    v_pad = jnp.pad(v, ((0, 0), (0, 0), (0, pad), (0, 0)))
    kb = k_pad.reshape(B, H, nb, MOBA_BLOCK, hd)
    vb = v_pad.reshape(B, H, nb, MOBA_BLOCK, hd)
    k_mean = jnp.mean(kb.astype(jnp.float32), axis=3)
    k_sel = min(MOBA_TOP_K, nb)
    scale = hd ** -0.5
    bi = jnp.arange(B)[:, None, None, None]
    hi = jnp.arange(H)[None, :, None, None]
    offs = jnp.arange(MOBA_BLOCK)
    blk_ids = jnp.arange(nb)

    def chunk(c):
        start = c * Q_CHUNK
        qc = lax.dynamic_slice_in_dim(q, start, Q_CHUNK, axis=2)
        t = start + jnp.arange(Q_CHUNK)
        own = start // MOBA_BLOCK
        gate = jnp.einsum('bhqd,bhnd->bhqn', qc.astype(jnp.float32), k_mean)
        gate = jnp.where(blk_ids < own, gate, NEG)
        _, idx = lax.top_k(gate, k_sel)
        valid = idx < own
        ks = kb[bi, hi, idx]
        vs = vb[bi, hi, idx]
        s_sel = jnp.einsum('bhqd,bhqkld->bhqkl', qc, ks).astype(jnp.float32) * scale
        s_sel = jnp.where(valid[..., None], s_sel, NEG).reshape(B, H, Q_CHUNK, k_sel * MOBA_BLOCK)
        k_own = lax.dynamic_index_in_dim(kb, own, axis=2, keepdims=False)
        v_own = lax.dynamic_index_in_dim(vb, own, axis=2, keepdims=False)
        s_own = jnp.einsum('bhqd,bhld->bhql', qc, k_own).astype(jnp.float32) * scale
        pos_own = own * MOBA_BLOCK + offs
        s_own = jnp.where(pos_own[None, :] <= t[:, None], s_own, NEG)
        p = jax.nn.softmax(jnp.concatenate([s_sel, s_own], axis=-1), axis=-1).astype(v.dtype)
        p_sel = p[..., :k_sel * MOBA_BLOCK].reshape(B, H, Q_CHUNK, k_sel, MOBA_BLOCK)
        p_own = p[..., k_sel * MOBA_BLOCK:]
        return (jnp.einsum('bhqkl,bhqkld->bhqd', p_sel, vs)
                + jnp.einsum('bhql,bhld->bhqd', p_own, v_own))

    out = lax.map(chunk, jnp.arange(T // Q_CHUNK))
    return out.transpose(1, 2, 0, 3, 4).reshape(B, H, T, hd)

def stick_breaking_attention(q, k, v):
    B, H, T, hd = q.shape
    scale = hd ** -0.5
    s_pos = jnp.arange(T)

    def chunk(c):
        start = c * Q_CHUNK
        qc = lax.dynamic_slice_in_dim(q, start, Q_CHUNK, axis=2)
        t = start + jnp.arange(Q_CHUNK)
        z = jnp.einsum('bhqd,bhsd->bhqs', qc, k).astype(jnp.float32) * scale
        past = s_pos[None, :] < t[:, None]
        log_fail = jnp.where(past, jax.nn.log_sigmoid(-z), 0.0)
        later = lax.cumsum(log_fail, axis=3, reverse=True) - log_fail
        w = jnp.where(past, jnp.exp(jax.nn.log_sigmoid(z) + later), 0.0)
        return jnp.einsum('bhqs,bhsd->bhqd', w.astype(v.dtype), v)

    out = lax.map(chunk, jnp.arange(T // Q_CHUNK))
    return out.transpose(1, 2, 0, 3, 4).reshape(B, H, T, hd)

def hybrid_mixer(u, positions, w_in, b_gate, w_branch_moba, w_branch_sb, w_out):
    proj = u @ w_in
    cuts = [D_MOBA, 2 * D_MOBA, 3 * D_MOBA, 3 * D_MOBA + D_SB, 3 * D_MOBA + 2 * D_SB,
            3 * D_MOBA + 3 * D_SB, 3 * D_MOBA + 3 * D_SB + D_MODEL]
    q_a, k_a, v_a, q_b, k_b, v_b, g_a, g_b = jnp.split(proj, cuts, axis=-1)
    q_a = partial_rotary(split_heads(q_a, N_HEADS_MOBA), positions)
    k_a = partial_rotary(split_heads(k_a, N_HEADS_MOBA), positions)
    y_a = merge_heads(moba_attention(q_a, k_a, split_heads(v_a, N_HEADS_MOBA)))
    y_b = merge_heads(stick_breaking_attention(split_heads(q_b, N_HEADS_SB),
                                               split_heads(k_b, N_HEADS_SB),
                                               split_heads(v_b, N_HEADS_SB)))
    gates = jax.nn.sigmoid(jnp.concatenate([g_a, g_b], axis=-1) + b_gate)
    gate_a, gate_b = gates[..., :D_MODEL], gates[..., D_MODEL:]
    merged = gate_a * (y_a @ w_branch_moba) + gate_b * (y_b @ w_branch_sb)
    return merged @ w_out

def first_inputs(seed: int = 0) -> dict:
    key = jax.random.key(seed)
    ks = jax.random.split(key, 18)

    def w(k, shape, fan_in):
        return jax.random.normal(k, shape, jnp.float32) * fan_in ** -0.5

    def gain(k):
        return 1.0 + 0.05 * jax.random.normal(k, (DEPTH, D_MODEL), jnp.float32)

    return {
        "x": jax.random.normal(ks[0], (BATCH, SEQ, D_MODEL), jnp.float32),
        "positions": jnp.broadcast_to(jnp.arange(SEQ, dtype=jnp.int32), (BATCH, SEQ)),
        "ffn1_norm": gain(ks[1]),
        "ffn1_w_gate": w(ks[2], (DEPTH, D_MODEL, D_FF), D_MODEL),
        "ffn1_w_up": w(ks[3], (DEPTH, D_MODEL, D_FF), D_MODEL),
        "ffn1_w_down": w(ks[4], (DEPTH, D_FF, D_MODEL), D_FF),
        "mix_norm": gain(ks[5]),
        "w_in": w(ks[6], (DEPTH, D_MODEL, D_IN), D_MODEL),
        "b_gate": 0.02 * jax.random.normal(ks[7], (DEPTH, 2 * D_MODEL), jnp.float32),
        "w_branch_moba": w(ks[8], (DEPTH, D_MOBA, D_MODEL), D_MOBA),
        "w_branch_sb": w(ks[9], (DEPTH, D_SB, D_MODEL), D_SB),
        "w_out": w(ks[10], (DEPTH, D_MODEL, D_MODEL), D_MODEL),
        "ffn2_norm": gain(ks[11]),
        "ffn2_w_gate": w(ks[12], (DEPTH, D_MODEL, D_FF), D_MODEL),
        "ffn2_w_up": w(ks[13], (DEPTH, D_MODEL, D_FF), D_MODEL),
        "ffn2_w_down": w(ks[14], (DEPTH, D_FF, D_MODEL), D_FF),
        "final_norm": 1.0 + 0.05 * jax.random.normal(ks[15], (D_MODEL,), jnp.float32),
    }

def first_block(x, positions, ffn1_norm, ffn1_w_gate, ffn1_w_up, ffn1_w_down, mix_norm, w_in,
              b_gate, w_branch_moba, w_branch_sb, w_out, ffn2_norm, ffn2_w_gate, ffn2_w_up,
              ffn2_w_down, final_norm):
    h = x
    for l in range(DEPTH):
        h = h + FFN_RES * swiglu(rms_norm(h, ffn1_norm[l]), ffn1_w_gate[l], ffn1_w_up[l], ffn1_w_down[l])
        h = h + hybrid_mixer(rms_norm(h, mix_norm[l]), positions, w_in[l], b_gate[l],
                             w_branch_moba[l], w_branch_sb[l], w_out[l])
        h = h + FFN_RES * swiglu(rms_norm(h, ffn2_norm[l]), ffn2_w_gate[l], ffn2_w_up[l], ffn2_w_down[l])
    return rms_norm(h, final_norm)


N_HEADS_FOX = 8
N_HEADS_DSA = 8
N_IDX_HEADS = 8
IDX_DIM = 64
TOPK_MAX = 256
Q_BLOCK = 128
N_BUCKETS = 32
MAX_DISTANCE = 128
NEG_INF = -1e30

FOX_W = N_HEADS_FOX * HEAD_DIM
DSA_W = N_HEADS_DSA * HEAD_DIM
IDX_Q_W = N_IDX_HEADS * IDX_DIM
IN_SPLITS = (FOX_W, FOX_W, FOX_W, N_HEADS_FOX,
             DSA_W, HEAD_DIM, HEAD_DIM,
             IDX_Q_W, IDX_DIM, N_IDX_HEADS,
             D_MODEL, D_MODEL)
IN_WIDTH = 3 * FOX_W + N_HEADS_FOX + DSA_W + 2 * HEAD_DIM + IDX_Q_W + IDX_DIM + N_IDX_HEADS + 2 * D_MODEL


def rms_norm_2(x, g):
    xf = x.astype(jnp.float32)
    y = xf * lax.rsqrt(jnp.mean(xf * xf, axis=-1, keepdims=True) + EPS)
    return (y * g.astype(jnp.float32)).astype(x.dtype)

def swiglu_ffn(x, g, w_gate, w_up, w_down):
    h = rms_norm_2(x, g)
    return (jax.nn.silu(h @ w_gate) * (h @ w_up)) @ w_down

def t5_causal_bucket(rel):
    max_exact = N_BUCKETS // 2
    relf = jnp.maximum(rel, 1).astype(jnp.float32)
    large = max_exact + (jnp.log(relf / max_exact) / math.log(MAX_DISTANCE / max_exact)
                         * (N_BUCKETS - max_exact)).astype(jnp.int32)
    large = jnp.minimum(large, N_BUCKETS - 1)
    return jnp.where(rel < max_exact, rel, large)

def split_columns(z):
    outs, off = [], 0
    for w in IN_SPLITS:
        outs.append(z[..., off:off + w])
        off += w
    return outs

def fox_attention(q, k, v, log_f):
    S = q.shape[1]
    cum = jnp.cumsum(log_f, axis=1).transpose(0, 2, 1)
    scale = HEAD_DIM ** -0.5
    outs = []
    for start in range(0, S, Q_BLOCK):
        end = start + Q_BLOCK
        logits = jnp.einsum('bqhd,bkhd->bhqk', q[:, start:end], k[:, :end]).astype(jnp.float32) * scale
        logits = logits + cum[:, :, start:end, None] - cum[:, :, None, :end]
        qpos = jnp.arange(start, end)[:, None]
        kpos = jnp.arange(end)[None, :]
        logits = jnp.where(kpos <= qpos, logits, NEG_INF)
        p = jax.nn.softmax(logits, axis=-1).astype(v.dtype)
        outs.append(jnp.einsum('bhqk,bkhd->bqhd', p, v[:, :end]))
    return jnp.concatenate(outs, axis=1)

def dsa_attention(q, k, v, q_idx, k_idx, w_idx, rel_bias):
    S = q.shape[1]
    topk = min(TOPK_MAX, S // 4)
    scale = HEAD_DIM ** -0.5
    idx_scale = IDX_DIM ** -0.5
    w = w_idx.astype(jnp.float32) * (N_IDX_HEADS ** -0.5)
    gather = jax.vmap(lambda arr, ind: arr[ind])
    outs = []
    for start in range(0, S, Q_BLOCK):
        end = start + Q_BLOCK
        n_keys = min(S, max(end, topk))
        qpos = jnp.arange(start, end)
        kpos = jnp.arange(n_keys)
        causal = kpos[None, :] <= qpos[:, None]
        s_idx = jax.nn.relu(jnp.einsum('bqhd,bkd->bqhk', q_idx[:, start:end],
                                       k_idx[:, :n_keys]).astype(jnp.float32) * idx_scale)
        score = jnp.einsum('bqhk,bqh->bqk', s_idx, w[:, start:end])
        score = jnp.where(causal[None], score, NEG_INF)
        _, sel = lax.top_k(score, topk)
        valid = sel <= qpos[None, :, None]
        k_sel = gather(k, sel)
        v_sel = gather(v, sel)
        logits = jnp.einsum('bqhd,bqkd->bhqk', q[:, start:end], k_sel).astype(jnp.float32) * scale
        bucket = t5_causal_bucket(jnp.maximum(qpos[None, :, None] - sel, 0))
        bias = rel_bias.astype(jnp.float32)[bucket]
        logits = logits + bias.transpose(0, 3, 1, 2)
        logits = jnp.where(valid[:, None], logits, NEG_INF)
        p = jax.nn.softmax(logits, axis=-1).astype(v.dtype)
        outs.append(jnp.einsum('bhqk,bqkd->bqhd', p, v_sel))
    return jnp.concatenate(outs, axis=1)

def second_inputs(seed: int = 0) -> dict:
    key = jax.random.key(seed)
    ks = jax.random.split(key, 24)
    f32 = jnp.float32

    def dense(k, fan_in, fan_out):
        return jax.random.normal(k, (fan_in, fan_out), f32) * fan_in ** -0.5

    def gain(k, n):
        return 1.0 + 0.02 * jax.random.normal(k, (n,), f32)

    return {
        "x": jax.random.normal(ks[0], (BATCH, SEQ, D_MODEL), f32),
        "ffn1_norm": gain(ks[1], D_MODEL),
        "ffn1_w_gate": dense(ks[2], D_MODEL, D_FF),
        "ffn1_w_up": dense(ks[3], D_MODEL, D_FF),
        "ffn1_w_down": dense(ks[4], D_FF, D_MODEL),
        "mix_norm": gain(ks[5], D_MODEL),
        "w_in": dense(ks[6], D_MODEL, IN_WIDTH),
        "b_forget": 1.0 + 0.1 * jax.random.normal(ks[7], (N_HEADS_FOX,), f32),
        "fox_q_norm": gain(ks[8], HEAD_DIM),
        "fox_k_norm": gain(ks[9], HEAD_DIM),
        "dsa_q_norm": gain(ks[10], HEAD_DIM),
        "dsa_k_norm": gain(ks[11], HEAD_DIM),
        "rel_bias": 0.5 * jax.random.normal(ks[12], (N_BUCKETS, N_HEADS_DSA), f32),
        "w_branch_a": dense(ks[13], FOX_W, D_MODEL),
        "w_branch_b": dense(ks[14], DSA_W, D_MODEL),
        "w_out": dense(ks[15], D_MODEL, D_MODEL),
        "ffn2_norm": gain(ks[16], D_MODEL),
        "ffn2_w_gate": dense(ks[17], D_MODEL, D_FF),
        "ffn2_w_up": dense(ks[18], D_MODEL, D_FF),
        "ffn2_w_down": dense(ks[19], D_FF, D_MODEL),
    }

def second_block(x, ffn1_norm, ffn1_w_gate, ffn1_w_up, ffn1_w_down, mix_norm, w_in, b_forget,
              fox_q_norm, fox_k_norm, dsa_q_norm, dsa_k_norm, rel_bias,
              w_branch_a, w_branch_b, w_out, ffn2_norm, ffn2_w_gate, ffn2_w_up, ffn2_w_down):
    B, S, _ = x.shape
    for _layer in range(DEPTH):
        x = x + 0.5 * swiglu_ffn(x, ffn1_norm, ffn1_w_gate, ffn1_w_up, ffn1_w_down)

        h = rms_norm_2(x, mix_norm)
        (fq, fk, fv, ff, dq, dk, dv, iq, ik, iw, ga, gb) = split_columns(h @ w_in)

        fq = rms_norm_2(fq.reshape(B, S, N_HEADS_FOX, HEAD_DIM), fox_q_norm)
        fk = rms_norm_2(fk.reshape(B, S, N_HEADS_FOX, HEAD_DIM), fox_k_norm)
        fv = fv.reshape(B, S, N_HEADS_FOX, HEAD_DIM)
        log_f = jax.nn.log_sigmoid((ff + b_forget).astype(jnp.float32))
        o_a = fox_attention(fq, fk, fv, log_f).reshape(B, S, FOX_W)

        dq = rms_norm_2(dq.reshape(B, S, N_HEADS_DSA, HEAD_DIM), dsa_q_norm)
        dk = rms_norm_2(dk, dsa_k_norm)
        iq = iq.reshape(B, S, N_IDX_HEADS, IDX_DIM)
        o_b = dsa_attention(dq, dk, dv, iq, ik, iw, rel_bias).reshape(B, S, DSA_W)

        merged = jax.nn.sigmoid(ga) * (o_a @ w_branch_a) + jax.nn.sigmoid(gb) * (o_b @ w_branch_b)
        x = x + merged @ w_out

        x = x + 0.5 * swiglu_ffn(x, ffn2_norm, ffn2_w_gate, ffn2_w_up, ffn2_w_down)
    return x


def setup_inputs(seed=0):
    out = dict(first_inputs(seed))
    for name, value in second_inputs(seed + 1).items():
        if name != "x":
            out[name + "_2"] = value
    return out


def reference(
    x, positions, ffn1_norm, ffn1_w_gate, ffn1_w_up, ffn1_w_down, mix_norm, w_in, b_gate,
    w_branch_moba, w_branch_sb, w_out, ffn2_norm, ffn2_w_gate, ffn2_w_up, ffn2_w_down,
    final_norm, ffn1_norm_2, ffn1_w_gate_2, ffn1_w_up_2, ffn1_w_down_2, mix_norm_2, w_in_2,
    b_forget_2, fox_q_norm_2, fox_k_norm_2, dsa_q_norm_2, dsa_k_norm_2, rel_bias_2,
    w_branch_a_2, w_branch_b_2, w_out_2, ffn2_norm_2, ffn2_w_gate_2, ffn2_w_up_2, ffn2_w_down_2,
):
    x = first_block(
        x, positions, ffn1_norm, ffn1_w_gate, ffn1_w_up, ffn1_w_down, mix_norm, w_in, b_gate,
        w_branch_moba, w_branch_sb, w_out, ffn2_norm, ffn2_w_gate, ffn2_w_up, ffn2_w_down,
        final_norm,
    )
    return second_block(
        x, ffn1_norm_2, ffn1_w_gate_2, ffn1_w_up_2, ffn1_w_down_2, mix_norm_2, w_in_2,
        b_forget_2, fox_q_norm_2, fox_k_norm_2, dsa_q_norm_2, dsa_k_norm_2, rel_bias_2,
        w_branch_a_2, w_branch_b_2, w_out_2, ffn2_norm_2, ffn2_w_gate_2, ffn2_w_up_2,
        ffn2_w_down_2,
    )


_drawn_inputs = setup_inputs


def setup_inputs(seed=0):
    import zlib

    import numpy as np

    out = dict(_drawn_inputs(seed))
    spreads = {}
    factors = {'b_gate': 8.0,
     'ffn1_norm_2': 4.404,
     'mix_norm_2': 3.404,
     'b_forget_2': 41.151,
     'fox_q_norm_2': 8.0,
     'fox_k_norm_2': 8.0,
     'dsa_q_norm_2': 8.0,
     'dsa_k_norm_2': 8.0,
     'ffn2_norm_2': 7.235,
     'rel_bias_2': 3.108}
    for name, (base, spread) in spreads.items():
        noise = np.random.default_rng([zlib.crc32(name.encode()), seed]).standard_normal(out[name].shape)
        drawn = base * np.exp(spread * noise) if base else spread * noise
        out[name] = __import__('jax').numpy.asarray(drawn.astype(out[name].dtype))
    for name, factor in factors.items():
        out[name] = (out[name] * factor).astype(out[name].dtype)
    return out
```

```python
from contextlib import ExitStack

import concourse.bass as bass
from concourse import mybir

F32 = mybir.dt.float32
F32R = mybir.dt.float32r
I32 = mybir.dt.int32
ALU = mybir.AluOpType
ACT = mybir.ActivationFunctionType
AX_X = mybir.AxisListType.X

P = 128
SEQ = 256
DM = 1024
FF = 2816
HD = 64
NH = 8
HW = NH * HD
KC = DM // P
TT = SEQ // P
NB = 512
CH = 256
NCH = FF // CH
EPS = 1e-6
NEG = -1e30
TOPK = min(256, SEQ // 4)
SC = 384

SLOTS = 4
UNIT = 2048
DMAS = 2

FFN_UNITS = 2 * NCH + NCH
PROJ = 10
MIX_UNITS = 2 * PROJ + 4 + 4
BASE = {}
_n = 0
for _ph, _k in (("F0", FFN_UNITS), ("M0", MIX_UNITS), ("F1", FFN_UNITS),
                ("F2", FFN_UNITS), ("M1", MIX_UNITS), ("F3", FFN_UNITS)):
    BASE[_ph] = _n
    _n += _k
UNITS = _n
TILES = {"F0": 0, "M0": 14, "F1": 30, "F2": 44, "M1": 58, "F3": 74}
FFN_OF = {"F0": 0, "F1": 1, "F2": 2, "F3": 3}
PREP_OF = {"F0": 0, "M0": 1, "F1": 2, "F2": 3, "M1": 4, "F3": 5}
NARROW = BASE["M1"] + 2
NW = 208


def steps_of(phase):
    b = BASE[phase]
    if phase[0] == "F":
        s = [[b + 2 * c, b + 2 * c + 1] for c in range(NCH)]
        d = b + 2 * NCH
        return s + [[u for u in (d + i, d + i + 1) if u < d + NCH] for i in range(0, NCH, 2)]
    return [[b + 2 * j, b + 2 * j + 1] for j in range(MIX_UNITS // 2)]


PHASES = ("F0", "M0", "F1", "F2", "M1", "F3")
STEPS = [(ph, i, us) for ph in PHASES for i, us in enumerate(steps_of(ph))]


def next_units(phase, i):
    n = next(k for k, s in enumerate(STEPS) if s[:2] == (phase, i)) + 1
    return STEPS[n][2] if n < len(STEPS) else []


def landed(u):
    n = sum(DMAS + (v in (NARROW, NARROW + 1)) for v in range(u % SLOTS, u + 1, SLOTS))
    return 16 * n


def items_of(b):
    if b == 0:
        out = [(11, "TR", ("qa", 0)), (11, "TR", ("qa", 1)), (12, "TR", ("ka", 0)), (12, "TR", ("ka", 1))]
        out += [(t, "SM", ("moba", h)) for h, t in enumerate((14, 15, 17, 18, 19, 21, 22, 23))]
        out += [(18, "TR", ("qb", 0)), (19, "TR", ("qb", 1)), (22, "TR", ("kb", 0)), (23, "TR", ("kb", 1))]
        out += [(t, "SB", ("sb", h)) for h, t in enumerate((25, 27, 28, 30, 31, 33, 34, 36))]
        out += [(39, "TY", (0, 0)), (39, "TY", (0, 1)), (44, "TY", (1, 0)), (44, "TY", (1, 1))]
    else:
        out = [(6, "TR", ("iq", 0)), (7, "TR", ("iq", 1)), (11, "TR", ("kk", 0)), (11, "TR", ("kk", 1)),
               (11, "CU", ())]
        out += [(12 + h, "IX", h) for h in range(NH)]
        out += [(15, "TR", ("fq", 0)), (15, "TR", ("fq", 1)), (19, "TR", ("fk", 0)), (19, "TR", ("fk", 1))]
        out += [(t, "SM", ("fox", h)) for h, t in enumerate((21, 22, 23, 25, 26, 27, 28, 29))]
        out += [(27, "TR", ("dq", 0)), (27, "TR", ("dq", 1))]
        out += [(t, "SM", ("dsa", h)) for h, t in enumerate((31, 32, 34, 35, 36, 37, 38, 39))]
        out += [(39, "TY", (0, 0)), (39, "TY", (0, 1)), (44, "TY", (1, 0)), (44, "TY", (1, 1))]
    return sorted(out, key=lambda x: x[0])


class Item:
    pass


def plan():
    items, i, m, reads = {0: [], 1: []}, 0, 0, {"a": 0, "d": 0}
    turned = ix = softs = sbs = 0
    flat = []
    for b in (0, 1):
        for slot, kind, what in items_of(b):
            it = Item()
            it.b, it.slot, it.kind, it.what, it.i, it.m = b, slot, kind, what, i, m
            it.reader = "a" if kind in ("TR", "IX", "CU") else "d"
            reads[it.reader] += 1
            it.read = reads[it.reader]
            if kind in ("TR", "CU"):
                turned += 1
                it.turned = turned
            if kind == "IX":
                it.ix = ix
                ix += 1
            if kind == "SM":
                it.softs = softs
                softs += 1
            if kind == "SB":
                it.sbs = sbs
                sbs += 1
            if kind in ("SM", "SB"):
                m += 1
            i += 1
            items[b].append(it)
            flat.append(it)
    return items, flat


ITEMS, FLAT = plan()
HEADS = [it for it in FLAT if it.kind in ("SM", "SB")]


def turned_after(b, name):
    return max(it.turned for it in ITEMS[b] if it.kind in ("TR", "CU") and (it.what[:1] or ("cu",))[0] == name)


SM_AT = dict(soft=1, turn=2, out=3, norm=4)
SB_AT = dict(clamp=1, keep=2, sum=3, weigh=4, out=5, norm=6)
LAST_SLOT = 48

INV_FREQ = [500000.0 ** (-k * 2.0 / 16) for k in range(8)]
C_ID, C_CAUSAL, C_PAST, C_GE, C_ONE, C_LE, C_END = 0, 128, 512, 896, 1024, 1152, 1280


def build(nc, a, out):
    ctx = ExitStack()
    with ctx:
        def sb(name, shape, dt=F32):
            return ctx.enter_context(nc.sbuf_tensor(name, shape, dt))

        def sem(name):
            return ctx.enter_context(nc.semaphore(name))

        bank = [ctx.enter_context(nc.psum_tensor(f"bank{i}", [P, NB], F32)) for i in range(8)]

        raw = [sb(f"raw{i}", [P, UNIT]) for i in range(SLOTS)]
        w_hi = [sb(f"w_hi{i}", [P, UNIT], F32R) for i in range(SLOTS)]
        w_lo = [sb(f"w_lo{i}", [P, UNIT], F32R) for i in range(SLOTS)]
        x = sb("x", [P, TT, DM])
        xg = sb("xg", [P, TT, DM])
        xT_hi = sb("xT_hi", [P, KC, SEQ], F32R)
        xT_lo = sb("xT_lo", [P, KC, SEQ], F32R)
        gain = [sb(f"gain{i}", [P, DM]) for i in range(2)]
        gate = sb("gate", [P, TT, 2 * DM])
        const = sb("const", [P, C_END])
        small = sb("small", [P, 256])
        hid = ExitStack()
        with hid:
            hT_hi = hid.enter_context(nc.sbuf_tensor("hT_hi", [P, FF // P, SEQ], F32R))
            hT_lo = hid.enter_context(nc.sbuf_tensor("hT_lo", [P, FF // P, SEQ], F32R))
        mix = ctx.enter_context(ExitStack())

        def mb(name, shape, dt=F32):
            return mix.enter_context(nc.sbuf_tensor(name, shape, dt))

        v_a = mb("v_a", [P, TT, HW])
        y = [mb("y_a", [P, TT, HW]), mb("y_b", [P, TT, HW])]
        qT_a = mb("qT_a", [P, HW // P, SEQ])
        kT_a = mb("kT_a", [P, HW // P, SEQ])
        qT_b = mb("qT_b", [P, HW // P, SEQ])
        score = [mb(f"score{i}", [P, SC]) for i in range(2)]
        prob = [mb(f"prob{i}", [P, SC]) for i in range(2)]
        probT = [mb(f"probT{i}", [P, SC]) for i in range(2)]
        soft = [mb(f"soft{i}", [P, SC]) for i in range(2)]
        late = ExitStack()
        with late:
            kT_b = late.enter_context(nc.sbuf_tensor("kT_b", [P, HW // P, SEQ], F32))
            v_b = late.enter_context(nc.sbuf_tensor("v_b", [P, TT, HW], F32))
            b_row = [late.enter_context(nc.sbuf_tensor(f"b_row{i}", [P, NB], F32)) for i in range(2)]
        ikT = mb("ikT", [P, SEQ])
        dkT = mb("dkT", [P, SEQ])
        dv = mb("dv", [P, TT, HD])
        index, work = gate[:, 1, DM:DM + SC], gate[:, 0, DM:DM + SC]
        sel = mb("sel", [P, SC])
        toep = mb("toep", [P, NH, SEQ])
        hg = mb("hg", [P, 4])
        ncum = mb("ncum", [NH, SEQ])

        at = [0]

        def cols(n):
            at[0] += n
            return small[:, at[0] - n:at[0]]

        ss = cols(14)
        rstd = cols(14)
        nv, ny, nt = cols(16), cols(16), cols(16)
        hss = cols(16)
        rowmax = cols(16)
        rowsum = cols(16)
        rowinv = cols(16)
        ifw = cols(16)
        lgf = cols(16)
        lgt = cols(16)
        m8 = cols(16)
        ngt = cols(2)
        freq = cols(8)
        cosr = cols(16)
        sinr = cols(16)
        posf = cols(2)
        bfor = cols(8)
        posi = sb("posi", [P, 2], I32)
        nyi = sb("nyi", [P, 16], I32)
        ki = sb("ki", [P, 16], I32)
        hs = [[gate[:, 1, DM + (2 * i + t) * CH:DM + (2 * i + t + 1) * CH] for t in range(TT)] for i in range(2)]
        gsil = [gate[:, 0, DM + t * CH:DM + (t + 1) * CH] for t in range(TT)]
        onehot = gate[:, 1, 0:SC]

        raw_in = [sem(f"raw_in{i}") for i in range(SLOTS)]
        hi_done = sem("hi_done")
        lo_done = sem("lo_done")
        unit_used = sem("unit_used")
        tile_done = sem("tile_done")
        x_in = sem("x_in")
        const_in = sem("const_in")
        gain_in = sem("gain_in")
        gained = sem("gained")
        x_turned = sem("x_turned")
        xT_hi_done = sem("xT_hi_done")
        xT_lo_done = sem("xT_lo_done")
        squared = sem("squared")
        rstd_done = sem("rstd_done")
        silu_done = sem("silu_done")
        h_done = sem("h_done")
        h_turned = sem("h_turned")
        hT_hi_done = sem("hT_hi_done")
        hT_lo_done = sem("hT_lo_done")
        evac_act = sem("evac_act")
        evac_dve = sem("evac_dve")
        rows_ready = sem("rows_ready")
        scored = sem("scored")
        read_a = sem("read_a")
        read_d = sem("read_d")
        maxed = sem("maxed")
        exped = sem("exped")
        turned = sem("turned")
        copied = sem("copied")
        weighed = sem("weighed")
        clamped = sem("clamped")
        softplus = sem("softplus")
        kept = sem("kept")
        w_done = sem("w_done")
        head_out = sem("head_out")
        head_read = sem("head_read")
        indexed = sem("indexed")
        y_hi = sem("y_hi")
        y_lo = sem("y_lo")
        gated = sem("gated")
        sigmoid = sem("sigmoid")
        merged = sem("merged")
        m_turned = sem("m_turned")
        mT_hi = sem("mT_hi")
        mT_lo = sem("mT_lo")
        logf = sem("logf")
        lnf = sem("lnf")
        vrow_mm = sem("vrow_mm")
        vrow_sb = sem("vrow_sb")
        vrow_out = sem("vrow_out")
        table_in = sem("table_in")
        b_row_in = [sem("b_row_in0"), sem("b_row_in1")]
        pos_in = sem("pos_in")
        freq_set = sem("freq_set")
        ang_done = sem("ang_done")
        sin_done = sem("sin_done")
        mix_in = sem("mix_in")
        dve_chain = sem("dve_chain")
        act_chain = sem("act_chain")
        stored = sem("stored")

        ident = const[:, C_ID:C_ID + P]
        causal = const[:, C_CAUSAL:C_CAUSAL + SC]
        past = const[:, C_PAST:C_PAST + SC]
        tri_ge = const[:, C_GE:C_GE + P]
        ones = const[:, C_ONE:C_ONE + P]
        tri_le = const[:, C_LE:C_LE + P]

        bias_rows = nc.dram_tensor("bias_rows", [NH, P, SC], F32).ap()

        ffn_w = [("ffn1_w_gate", "ffn1_w_up", "ffn1_w_down"), ("ffn2_w_gate", "ffn2_w_up", "ffn2_w_down"),
                 ("ffn1_w_gate_2", "ffn1_w_up_2", "ffn1_w_down_2"),
                 ("ffn2_w_gate_2", "ffn2_w_up_2", "ffn2_w_down_2")]
        branch_w = [("w_branch_moba", "w_branch_sb"), ("w_branch_a_2", "w_branch_b_2")]
        out_w = ["w_out", "w_out_2"]
        proj_at = [[512 * j for j in range(PROJ)],
                   [2184, None, 0, 512, 1024, 1544, 2768, 3280, 3792, 4304]]
        gains = ["ffn1_norm", "mix_norm", "ffn2_norm", "final_norm",
                 "ffn1_norm_2", "mix_norm_2", "ffn2_norm_2"]
        GAIN_OF = {"F0": 0, "M0": 1, "F1": 2, "Z": 3, "F2": 4, "M1": 5, "F3": 6}
        Q_FFN = [(0, 0), (0, 1), (1, 0), (1, 1)]
        Q_MIX = [(0, 0), (1, 0), (0, 1), (1, 1)]
        PREV = {"M0": "F0", "F1": "M0", "F2": "F1", "M1": "F2", "F3": "M1"}

        def quarters(ph):
            return Q_MIX if ph in ("F1", "F3") else Q_FFN

        def turn_banks(ph):
            return [4, 5, 6, 7] if ph in ("F0", "F1", "F3") else [0, 1, 6, 7]

        def acc_bank(ph, tt, n):
            return bank[2 + 2 * tt + n] if ph[0] == "F" else bank[2 * n + tt]

        def wait_quarter(eng, ph, q):
            if ph[0] == "F":
                if q < 3:
                    eng.wait_ge(tile_done, TILES[ph] + NCH + q + 1)
                else:
                    eng.wait_ge(unit_used, BASE[ph] + FFN_UNITS)
            elif q % 2 == 0:
                eng.wait_ge(tile_done, TILES[ph] + PROJ + 4 + q // 2 + 1)
            else:
                eng.wait_ge(unit_used, BASE[ph] + MIX_UNITS - 2 + 2 * (q // 2))

        def wait_chunk(eng, ph, j, tt):
            if tt == 0:
                eng.wait_ge(tile_done, TILES[ph] + j + 1)
            else:
                eng.wait_ge(unit_used, BASE[ph] + 2 * j + 2)

        def head_bank(it):
            return bank[6 + it.m % 2]

        block = ctx.enter_context(nc.Block())

        @block.sync
        def _(sp):
            sp.dma_start(x[:, 0, :], a["x"][0, 0:P, :]).then_inc(x_in, 16)
            sp.dma_start(x[:, 1, :], a["x"][0, P:SEQ, :]).then_inc(x_in, 16)

            def free(u, i=0, k=0):
                if u >= SLOTS:
                    sp.wait_ge(lo_done, u + k * i - SLOTS + 1)

            def put(u, dst, src):
                sp.dma_start(dst, src).then_inc(raw_in[u % SLOTS], 16)

            def load_gate_up(f, c, hf, u, i=0, k=0):
                free(u, i, k)
                slot = raw[u % SLOTS][:].rearrange("p (k n) -> p k n", k=4)
                for s in range(2):
                    w = a[ffn_w[f][s]].rearrange("(k p) (c n) -> p k c n", p=P, n=CH)
                    put(u, slot[:, :, s * CH:(s + 1) * CH], w[:, 4 * hf:4 * hf + 4, c, :])

            def load_rows(w, u, r0, rows, c0, width):
                free(u)
                slot = raw[u % SLOTS][:, 0:rows * width].rearrange("p (k n) -> p k n", k=rows)
                w = w.rearrange("(k p) n -> p k n", p=P)
                h = rows // 2
                for s in range(2):
                    put(u, slot[:, s * h:(s + 1) * h, :], w[:, r0 + s * h:r0 + (s + 1) * h, c0:c0 + width])

            def load_narrow(u, hf):
                free(u)
                slot = raw[u % SLOTS][:, 0:4 * NW].rearrange("p (k n) -> p k n", k=4)
                w = a["w_in_2"].rearrange("(k p) n -> p k n", p=P)[:, 4 * hf:4 * hf + 4, :]
                put(u, slot[:, :, 0:8], w[:, :, 1536:1544])
                put(u, slot[:, :, 8:136], w[:, :, 2056:2184])
                put(u, slot[:, :, 136:208], w[:, :, 2696:2768])

            for ph in PHASES:
                u0 = BASE[ph]
                if ph[0] == "F":
                    f = FFN_OF[ph]
                    for c in range(1):
                        for hf in range(2):
                            load_gate_up(f, c, hf, u0 + 2 * c + hf)
                    if ph == "F0":
                        load_gate_up(f, 1, 0, u0 + 2)
                        load_gate_up(f, 1, 1, u0 + 3)
                        load_gate_up(f, 2, 0, u0 + 4)
                        load_gate_up(f, 2, 1, u0 + 5)
                        first = 3
                    else:
                        first = 1
                    n = (NCH - first) // 2
                    with sp.Fori(0, n) as i:
                        for j in range(4):
                            load_gate_up(f, first + j // 2 + 2 * i, j % 2, u0 + 2 * first + j, i, 4)
                    for d in range(NCH):
                        load_rows(a[ffn_w[f][2]], u0 + 2 * NCH + d, 2 * d, 2, 0, DM)
                    continue
                b = int(ph[1])
                w_in = a[("w_in", "w_in_2")[b]]
                for j in range(PROJ):
                    for hf in range(2):
                        if proj_at[b][j] is None:
                            load_narrow(u0 + 2 * j + hf, hf)
                        else:
                            load_rows(w_in, u0 + 2 * j + hf, 4 * hf, 4, proj_at[b][j], NB)
                for s in range(2):
                    for n in range(2):
                        load_rows(a[branch_w[b][s]], u0 + 20 + 2 * s + n, 0, 4, n * NB, NB)
                for n in range(2):
                    for hf in range(2):
                        load_rows(a[out_w[b]], u0 + 24 + 2 * n + hf, 4 * hf, 4, n * NB, NB)
            for q, (tt, n) in enumerate(Q_FFN):
                sp.wait_ge(gained, 4 * 7 + q + 1)
                sp.dma_start(out[0, tt * P:(tt + 1) * P, n * NB:(n + 1) * NB],
                             x[:, tt, n * NB:(n + 1) * NB]).then_inc(stored, 16)
            sp.wait_ge(stored, 16 * 4)

        @block.gpsimd
        def _(pool):
            pool.dma_start(gain[0][:], a[gains[0]].partition_broadcast(P)).then_inc(gain_in, 16)
            pool.dma_start(const[:], a["consts"]).then_inc(const_in, 16)
            pool.dma_start(onehot[0:32, :], a["onehot"]).then_inc(table_in, 16)
            pool.dma_start(lgt[0:32, 0:NH], a["rel_bias_2"]).then_inc(table_in, 16)
            for t in range(TT):
                pool.dma_start(posi[:, t:t + 1], a["positions"][0, t * P:(t + 1) * P]
                               .rearrange("(p o) -> p o", o=1)).then_inc(pos_in, 16)
            for k in range(8):
                m = nc.gpsimd.memset(freq[:, k:k + 1], INV_FREQ[k])
            m.then_inc(freq_set, 1)
            for g in range(2):
                pool.wait_ge(vrow_sb, 4 * g + 4)
                src = gate[:, 0, 0:4 * SC] if g == 0 else gate[:, 1, SC:5 * SC]
                pool.dma_start(bias_rows[4 * g:4 * g + 4].rearrange("h p c -> p h c"),
                               src.rearrange("p (h c) -> p h c", h=4)).then_inc(vrow_out, 16)
            pool.wait_ge(vrow_out, 32)
            for m in range(1, 7):
                pool.wait_ge(gain_in, 16 * m)
                if m >= 2:
                    pool.wait_ge(gained, 4 * (m - 1))
                pool.dma_start(gain[m % 2][:], a[gains[m]].partition_broadcast(P)).then_inc(gain_in, 16)
                if m == 1:
                    pool.wait_ge(unit_used, BASE["F0"] + FFN_UNITS)
                    for g in range(4):
                        if g >= 2:
                            pool.wait_ge(evac_dve, 2 * (g - 1))
                        pool.dma_start(b_row[g % 2][:], a["b_gate"][g * NB:(g + 1) * NB].partition_broadcast(P))\
                            .then_inc(b_row_in[g % 2], 16)
                if m == 5:
                    pool.wait_ge(unit_used, BASE["F2"] + FFN_UNITS)
                    skew = bass.AP(bias_rows.tensor, P - 1, [[SC - 1, P], [P * SC, NH], [1, SEQ]])
                    pool.dma_start(toep[:], skew).then_inc(mix_in, 16)
                    for k, name in enumerate(("fox_q_norm_2", "fox_k_norm_2", "dsa_q_norm_2", "dsa_k_norm_2")):
                        for r in range(2):
                            pool.dma_start(hg[r * HD:(r + 1) * HD, k:k + 1],
                                           a[name].rearrange("(d o) -> d o", o=1)).then_inc(mix_in, 16)
                    pool.dma_start(bfor, a["b_forget_2"].partition_broadcast(P)).then_inc(mix_in, 16)

        MIX_IN = 16 * 10

        @block.scalar
        def _(act):
            chain = [0]

            def link(ins):
                chain[0] += 1
                ins.then_inc(act_chain, 1)
                act.wait_ge(act_chain, chain[0])

            def split_hi(u, i=0, k=0):
                n = 4 * NW if u in (NARROW, NARROW + 1) else UNIT
                act.wait_ge(raw_in[u % SLOTS], landed(u) + 16 * DMAS * (k // SLOTS) * i)
                if u >= SLOTS:
                    act.wait_ge(unit_used, u + k * i - SLOTS + 1)
                act.activation(w_hi[u % SLOTS][:, 0:n], raw[u % SLOTS][:, 0:n], ACT.Copy).then_inc(hi_done, 1)

            def prep(ph):
                p = PREP_OF[ph]
                for q, (tt, n) in enumerate(quarters(ph)):
                    act.wait_ge(x_turned, 4 * p + q + 1)
                    act.activation(xT_hi[:, 4 * n:4 * n + 4, tt * P:(tt + 1) * P],
                                   bank[turn_banks(ph)[q]][:].rearrange("p (k t) -> p k t", k=4),
                                   ACT.Copy).then_inc(xT_hi_done, 1)
                square(GAIN_OF[ph])

            def square(g):
                for tt in range(TT):
                    act.wait_ge(gained, 4 * (g + 1) if g != 3 else 13)
                    act.activation(gate[:, tt, 0:DM], x[:, tt, :], ACT.Square,
                                   accum_out=ss[:, 2 * g + tt:2 * g + tt + 1]).then_inc(squared, 1)

            def silu(ph, c, i=0):
                for tt in range(TT):
                    if tt == 0:
                        act.wait_ge(tile_done, TILES[ph] + c + 2 * i + 1)
                    else:
                        act.wait_ge(unit_used, BASE[ph] + 2 * c + 2 + 4 * i)
                    g = GAIN_OF[ph]
                    act.activation(gsil[tt], bank[2 * (c % 2) + tt][:, 0:CH], ACT.Silu,
                                   scale=rstd[:, 2 * g + tt:2 * g + tt + 1]).then_inc(silu_done, 1)

            def hidden_hi(ph, c, i=0):
                act.wait_ge(h_turned, NCH * FFN_OF[ph] + c + 2 * i + 1)
                act.activation(hT_hi[:, bass.ds(2 * c + 4 * i, 2), :],
                               bank[6 + c % 2][:].rearrange("p (k t) -> p k t", k=2), ACT.Copy).then_inc(hT_hi_done, 1)

            def ffn(ph):
                u0 = BASE[ph]
                prep(ph)
                for u in next_units(ph, 0):
                    split_hi(u)
                act.wait_ge(rstd_done, GAIN_OF[ph] + 1)
                with act.Fori(0, (NCH - 1) // 2) as i:
                    for j in range(2):
                        silu(ph, j, i)
                        split_hi(u0 + 4 + 2 * j, i, 4)
                        hidden_hi(ph, j, i)
                        split_hi(u0 + 5 + 2 * j, i, 4)
                for s in range(NCH, NCH + 6):
                    us = next_units(ph, s)
                    if s == NCH:
                        silu(ph, NCH - 1)
                    for u in us[:1]:
                        split_hi(u)
                    if s == NCH:
                        hidden_hi(ph, NCH - 1)
                    for u in us[1:]:
                        split_hi(u)

            def mixer(b):
                ph = ("M0", "M1")[b]
                g = GAIN_OF[ph]
                prep(ph)

                def r(tt):
                    return rstd[:, 2 * g + tt:2 * g + tt + 1]

                def evac(j):
                    def mv(dst, src, last=False):
                        ins = act.activation(dst, src, ACT.Copy, scale=r(tt))
                        if last:
                            ins.then_inc(evac_act, 1)

                    if j == 0:
                        act.wait_ge(rstd_done, g + 1)
                    for tt in range(TT):
                        src = bank[2 * (j % 2) + tt]
                        wait_chunk(act, ph, j, tt)
                        if b == 0:
                            if j in (2, 5):
                                mv((v_a, v_b)[j // 3][:, tt, :], src[:], True)
                            else:
                                c0 = HW * (j % 3)
                                mv(xg[:, tt, c0:c0 + HW], src[:], True)
                        elif j == 1:
                            mv(lgf[:, 8 * tt:8 * tt + 8], src[:, 0:8])
                            mv(xg[:, tt, 512:576], src[:, 8:72])
                            mv(dv[:, tt, :], src[:, 72:136])
                            mv(xg[:, tt, 640:704], src[:, 136:200])
                            mv(xg[:, tt, 704:768], src[:, 136:200])
                            mv(ifw[:, 8 * tt:8 * tt + 8], src[:, 200:208], True)
                        elif j == 4:
                            mv(v_a[:, tt, :], src[:], True)
                        else:
                            c0 = {0: 0, 2: 0, 3: 512, 5: 0}[j]
                            mv(xg[:, tt, c0:c0 + HW], src[:], True)

                def gate_rows(j):
                    for tt in range(TT):
                        wait_chunk(act, ph, j, tt)
                        act.activation(gate[:, tt, (j - 6) * NB:(j - 5) * NB], bank[2 * (j % 2) + tt][:], ACT.Copy,
                                       scale=r(tt)).then_inc(gated, 1)

                def turn(it):
                    name, tt = it.what if it.kind == "TR" else ("cu", 0)
                    act.wait_ge(scored, it.i + 1)
                    S = bank[4 + it.i % 2]
                    t = slice(tt * P, (tt + 1) * P)
                    full = S[:].rearrange("p (k t) -> p k t", k=4)
                    if name == "cu":
                        ins = act.activation(ncum[:], S[0:NH, 0:SEQ], ACT.Copy, scale=-1.0)
                    elif name == "kk":
                        act.activation(dkT[:, t], S[:, 0:P], ACT.Copy, scale=hg[:, 3:4])
                        ins = act.activation(ikT[:, t], S[:, P:2 * P], ACT.Copy)
                    else:
                        dst = {"qa": qT_a, "ka": kT_a, "qb": qT_b, "kb": kT_b, "iq": None,
                               "fq": qT_a, "fk": kT_a, "dq": qT_b}[name]
                        dst = y[1][:].rearrange("p t (k n) -> p (t k) n", k=2) if name == "iq" else dst[:]
                        scale = {"qa": HD ** -0.5, "qb": HD ** -0.5, "ka": 1.0, "kb": 1.0, "iq": 1.0,
                                 "fq": hg[:, 0:1], "fk": hg[:, 1:2], "dq": hg[:, 2:3]}[name]
                        ins = act.activation(dst[:, :, t], full, ACT.Copy, scale=scale)
                    ins.then_inc(read_a, 1)

                def exps(it):
                    act.wait_ge(maxed, it.softs + 1)
                    if it.m >= 2:
                        act.wait_ge(head_out if HEADS[it.m - 2].kind == "SB" else turned, it.m - 1)
                    k = 2 * (it.m % 8)
                    s, e = score[it.m % 2], prob[it.m % 2]
                    act.activation(e[:, 0:P], s[:, 0:P], ACT.Exp, bias=rowmax[:, k:k + 1],
                                   accum_out=rowsum[:, k:k + 1])
                    act.activation(e[:, P:SC], s[:, P:SC], ACT.Exp, bias=rowmax[:, k + 1:k + 2],
                                   accum_out=rowsum[:, k + 1:k + 2]).then_inc(exped, 1)

                def copy_turned(it):
                    act.wait_ge(turned, it.m + 1)
                    if it.m >= 2:
                        act.wait_ge(head_out, it.m - 1)
                    act.activation(probT[it.m % 2][:], head_bank(it)[:, 0:SC], ACT.Copy).then_inc(copied, 1)

                def sb_softplus(it):
                    act.wait_ge(clamped, it.sbs + 1)
                    t = soft[it.m % 2]
                    link(act.activation(t[:], t[:], ACT.Exp))
                    act.activation(t[:], t[:], ACT.Ln, bias=1.0).then_inc(softplus, 1)

                def sb_weights(it):
                    act.wait_ge(weighed, it.sbs + 1)
                    e = prob[it.m % 2]
                    act.activation(e[:], e[:], ACT.Exp).then_inc(w_done, 1)

                def relu(it):
                    act.wait_ge(scored, it.i + 1)
                    if it.ix >= 2:
                        act.wait_ge(indexed, it.ix - 1)
                    act.activation(soft[it.ix % 2][:], bank[4 + it.i % 2][:, 0:SC], ACT.Relu,
                                   scale=HD ** -0.5).then_inc(read_a, 1)

                def y_turned(it):
                    br, tt = it.what
                    act.wait_ge(scored, it.i + 1)
                    if br == 0:
                        act.wait_ge(unit_used, BASE[ph] + 2 * PROJ)
                    act.activation(xT_hi[:, 4 * br:4 * br + 4, tt * P:(tt + 1) * P],
                                   bank[4 + it.i % 2][:].rearrange("p (k t) -> p k t", k=4),
                                   ACT.Copy).then_inc(y_hi, 1)

                for slot in range(LAST_SLOT):
                    j, q = divmod(slot, 4)
                    if q in (0, 2):
                        for u in next_units(ph, j)[q // 2:q // 2 + 1]:
                            split_hi(u)
                    for it in ITEMS[b]:
                        if it.kind == "TY" and slot - it.slot == 1:
                            y_turned(it)
                    if q == 0 and 1 <= j <= 6:
                        evac(j - 1)
                    if b == 1 and q == 0 and 7 <= j <= 10:
                        gate_rows(j - 1)
                    if b == 1 and slot == 9:
                        act.wait_ge(logf, 1)
                        link(act.activation(lgt, lgt, ACT.Exp, scale=-1.0))
                        act.activation(lgt, lgt, ACT.Ln, bias=1.0).then_inc(lnf, 1)
                    for it in ITEMS[b]:
                        d = slot - it.slot
                        if it.kind in ("TR", "CU") and d == 1:
                            turn(it)
                        if it.kind == "IX" and d == 1:
                            relu(it)
                        if it.kind == "SM" and d == SM_AT["turn"]:
                            copy_turned(it)
                        if it.kind == "SM" and d == SM_AT["soft"]:
                            exps(it)
                        if it.kind == "SB" and d == SB_AT["weigh"]:
                            sb_weights(it)
                        if it.kind == "SB" and d == SB_AT["clamp"]:
                            sb_softplus(it)
                    if slot == 42:
                        act.wait_ge(gated if b == 1 else evac_dve, 8)
                        for br in range(2):
                            act.activation(gate[:, :, br * DM:(br + 1) * DM], gate[:, :, br * DM:(br + 1) * DM],
                                           ACT.Sigmoid).then_inc(sigmoid, 1)
                for u in next_units(ph, 12)[:]:
                    split_hi(u)
                for q, (tt, n) in enumerate(Q_MIX):
                    act.wait_ge(m_turned, 4 * b + q + 1)
                    act.activation(xT_hi[:, 4 * n:4 * n + 4, tt * P:(tt + 1) * P],
                                   bank[4 + q][:].rearrange("p (k t) -> p k t", k=4), ACT.Copy).then_inc(mT_hi, 1)
                for u in next_units(ph, 13):
                    split_hi(u)

            for g in range(2):
                for h in range(4):
                    act.wait_ge(vrow_mm, 4 * g + h + 1)
                    dst = gate[:, 0, h * SC:(h + 1) * SC] if g == 0 else gate[:, 1, (h + 1) * SC:(h + 2) * SC]
                    act.activation(dst, bank[h][:, 0:SC], ACT.Copy).then_inc(vrow_sb, 1)
            act.wait_ge(ang_done, 1)
            act.activation(sinr, sinr, ACT.Sin).then_inc(sin_done, 1)
            act.activation(cosr, cosr, ACT.Sin).then_inc(sin_done, 1)
            for u in STEPS[0][2]:
                split_hi(u)
            act.wait_ge(vrow_out, 32)
            ffn("F0")
            mixer(0)
            ffn("F1")
            square(3)
            ffn("F2")
            mixer(1)
            ffn("F3")

        @block.vector
        def _(dve):
            chain = [0]

            def link(ins):
                chain[0] += 1
                ins.then_inc(dve_chain, 1)
                dve.wait_ge(dve_chain, chain[0])

            def split_lo(u, i=0, k=0):
                n = 4 * NW if u in (NARROW, NARROW + 1) else UNIT
                dve.wait_ge(hi_done, u + k * i + 1)
                s = u % SLOTS
                dve.tensor_tensor(w_lo[s][:, 0:n], raw[s][:, 0:n], w_hi[s][:, 0:n], ALU.subtract).then_inc(lo_done, 1)

            def rsqrt(dst, src, n, mean):
                link(dve.tensor_scalar(nv[:, 0:n], src, mean, EPS, ALU.mult, ALU.add))
                link(dve.tensor_scalar(nyi[:, 0:n], nv[:, 0:n].bitcast(I32), 1, None, ALU.logical_shift_right))
                link(dve.tensor_scalar(nyi[:, 0:n], nyi[:, 0:n], -1.0, float(0x5F3759DF), ALU.mult, ALU.add))
                y0 = nyi[:, 0:n].bitcast(F32)
                for k in range(4):
                    y1 = dst if k == 3 else ny[:, 0:n]
                    link(dve.tensor_tensor(nt[:, 0:n], y0, y0, ALU.mult))
                    link(dve.tensor_tensor(nt[:, 0:n], nt[:, 0:n], nv[:, 0:n], ALU.mult))
                    link(dve.tensor_scalar(nt[:, 0:n], nt[:, 0:n], -0.5, 1.5, ALU.mult, ALU.add))
                    ins = dve.tensor_tensor(y1, y0, nt[:, 0:n], ALU.mult)
                    if k < 3:
                        link(ins)
                    y0 = y1
                return ins

            def residual(ph, scale):
                prev = PREV.get(ph)
                g = GAIN_OF[ph]
                dve.wait_ge(gain_in, 16 * (g + 1))
                for q, (tt, n) in enumerate(quarters(ph)):
                    c = slice(n * NB, (n + 1) * NB)
                    if prev and ph != "F2":
                        wait_quarter(dve, prev, q)
                        link(dve.scalar_tensor_tensor(x[:, tt, c], acc_bank(prev, tt, n)[:], scale, x[:, tt, c],
                                                      ALU.mult, ALU.add))
                    dve.tensor_tensor(xg[:, tt, c], x[:, tt, c], gain[g % 2][:, c], ALU.mult).then_inc(gained, 1)

            def prep(ph):
                p, g = PREP_OF[ph], GAIN_OF[ph]
                for q, (tt, n) in enumerate(quarters(ph)):
                    dve.wait_ge(xT_hi_done, 4 * p + q + 1)
                    t = slice(tt * P, (tt + 1) * P)
                    dve.tensor_tensor(xT_lo[:, 4 * n:4 * n + 4, t],
                                      bank[turn_banks(ph)[q]][:].rearrange("p (k t) -> p k t", k=4),
                                      xT_hi[:, 4 * n:4 * n + 4, t], ALU.subtract).then_inc(xT_lo_done, 1)
                rms(g)

            def rms(g):
                dve.wait_ge(squared, 2 * (g + 1))
                rsqrt(rstd[:, 2 * g:2 * g + 2], ss[:, 2 * g:2 * g + 2], 2, 1.0 / DM).then_inc(rstd_done, 1)
                dve.wait_ge(rstd_done, g + 1)

            def hidden(ph, c, i=0):
                g = GAIN_OF[ph]
                for tt in range(TT):
                    dve.wait_ge(silu_done, 2 * NCH * FFN_OF[ph] + 2 * c + tt + 1 + 4 * i)
                    dve.scalar_tensor_tensor(hs[c % 2][tt], bank[2 * (c % 2) + tt][:, CH:2 * CH],
                                             rstd[:, 2 * g + tt:2 * g + tt + 1], gsil[tt],
                                             ALU.mult, ALU.mult).then_inc(h_done, 1)

            def hidden_lo(ph, c, i=0):
                dve.wait_ge(hT_hi_done, NCH * FFN_OF[ph] + c + 2 * i + 1)
                k = bass.ds(2 * c + 4 * i, 2)
                dve.tensor_tensor(hT_lo[:, k, :], bank[6 + c % 2][:].rearrange("p (k t) -> p k t", k=2),
                                  hT_hi[:, k, :], ALU.subtract).then_inc(hT_lo_done, 1)

            def ffn(ph):
                u0 = BASE[ph]
                prep(ph)
                for u in next_units(ph, 0):
                    split_lo(u)
                with dve.Fori(0, (NCH - 1) // 2) as i:
                    for j in range(2):
                        hidden(ph, j, i)
                        split_lo(u0 + 4 + 2 * j, i, 4)
                        hidden_lo(ph, j, i)
                        split_lo(u0 + 5 + 2 * j, i, 4)
                for s in range(NCH, NCH + 6):
                    us = next_units(ph, s)
                    if s == NCH:
                        hidden(ph, NCH - 1)
                    for u in us[:1]:
                        split_lo(u)
                    if s == NCH:
                        hidden_lo(ph, NCH - 1)
                    for u in us[1:]:
                        split_lo(u)

            def head_norm(src, dst, n):
                tmp = gate[:, :, 3 * NB:3 * NB + n * HD]
                link(dve.tensor_tensor(tmp, src, src, ALU.mult))
                v = hss[:, 0:TT * n].rearrange("p (t h) -> p t h", t=TT)
                link(dve.tensor_reduce(v, tmp.rearrange("p t (h d) -> p t h d", d=HD), AX_X, ALU.add))
                link(rsqrt(hss[:, 0:TT * n], hss[:, 0:TT * n], TT * n, 1.0 / HD))
                for tt in range(TT):
                    ins = dve.tensor_tensor(dst[:, tt, :].rearrange("p (h d) -> p h d", d=HD),
                                            src[:, tt, :].rearrange("p (h d) -> p h d", d=HD),
                                            hss[:, tt * n:(tt + 1) * n].rearrange("p (h o) -> p h o", o=1)
                                            .to_broadcast([P, n, HD]), ALU.mult)
                return ins

            def mixer(b):
                ph = ("M0", "M1")[b]
                g = GAIN_OF[ph]
                prep(ph)

                def rotate():
                    dve.wait_ge(evac_act, 4)
                    dve.wait_ge(sin_done, 2)
                    v = xg[:].rearrange("p t (h d) -> p t h d", d=HD)
                    tmp = y[1][:].rearrange("p t (k h d) -> p t k h d", k=4, d=8)
                    for tt in range(TT):
                        x1, x2 = v[:, tt, :, 0:8], v[:, tt, :, 8:16]
                        c = cosr[:, 8 * tt:8 * tt + 8].rearrange("p (o d) -> p o d", o=1).to_broadcast([P, 2 * NH, 8])
                        s = sinr[:, 8 * tt:8 * tt + 8].rearrange("p (o d) -> p o d", o=1).to_broadcast([P, 2 * NH, 8])
                        t = [tmp[:, tt, k] for k in range(4)]
                        dve.tensor_tensor(t[0], x1, c, ALU.mult)
                        dve.tensor_tensor(t[1], x2, s, ALU.mult)
                        dve.tensor_tensor(t[2], x2, c, ALU.mult)
                        link(dve.tensor_tensor(t[3], x1, s, ALU.mult))
                        dve.tensor_tensor(x1, t[0], t[1], ALU.subtract)
                        dve.tensor_tensor(x2, t[2], t[3], ALU.add).then_inc(rows_ready, 1)

                def norm_rows(c0, evacs):
                    dve.wait_ge(evac_act, evacs)
                    v = xg[:, :, c0:c0 + HW]
                    head_norm(v, v, NH).then_inc(rows_ready, 1)

                def narrow():
                    dve.wait_ge(evac_act, 16)
                    dve.wait_ge(mix_in, MIX_IN)
                    v = xg[:, :, 512:576]
                    link(head_norm(v, v, 1))
                    dve.tensor_copy(xg[:, :, 576:640], v).then_inc(rows_ready, 1)
                    dve.tensor_scalar(ifw, ifw, NH ** -0.5, None, ALU.mult)
                    for tt in range(TT):
                        ins = dve.tensor_tensor(lgf[:, 8 * tt:8 * tt + 8], lgf[:, 8 * tt:8 * tt + 8], bfor, ALU.add)
                    link(ins)
                    dve.scalar_tensor_tensor(lgt, lgf, -1.0, lgf, ALU.mult, ALU.max).then_inc(logf, 1)
                    dve.tensor_scalar(hg[:, 0:1], hg[:, 0:1], HD ** -0.5, None, ALU.mult)
                    link(dve.tensor_scalar(hg[:, 2:3], hg[:, 2:3], HD ** -0.5, None, ALU.mult))

                def log_f():
                    dve.wait_ge(lnf, 1)
                    dve.scalar_tensor_tensor(lgf, lgf, 0.0, lgt, ALU.min, ALU.subtract).then_inc(rows_ready, 1)

                def gate_rows(j):
                    for tt in range(TT):
                        wait_chunk(dve, ph, j, tt)
                        if tt == 0:
                            dve.wait_ge(b_row_in[j % 2], 16 * ((j - 6) // 2 + 1))
                        dve.scalar_tensor_tensor(gate[:, tt, (j - 6) * NB:(j - 5) * NB], bank[2 * (j % 2) + tt][:],
                                                 rstd[:, 2 * g + tt:2 * g + tt + 1], b_row[j % 2][:],
                                                 ALU.mult, ALU.add).then_inc(evac_dve, 1)

                def soften(it):
                    dve.wait_ge(scored, it.i + 1)
                    if it.softs >= 2:
                        dve.wait_ge(exped, it.softs - 1)
                    S, s = bank[4 + it.i % 2], score[it.m % 2]
                    kind, h = it.what
                    ins = dve.tensor_tensor(s[:], S[:, 0:SC], sel[:] if kind == "dsa" else causal, ALU.add)
                    ins.then_inc(read_d, 1)
                    dve.wait_ge(read_d, it.read)
                    if kind == "dsa":
                        dve.tensor_tensor(s[:, 0:P], s[:, 0:P], toep[:, h, P:2 * P], ALU.add)
                        link(dve.tensor_tensor(s[:, P:SC], s[:, P:SC], toep[:, h, :], ALU.add))
                    k = 2 * (it.m % 8)
                    dve.tensor_reduce(rowmax[:, k:k + 1], s[:, 0:P], AX_X, ALU.max)
                    link(dve.tensor_reduce(rowmax[:, k + 1:k + 2], s[:, P:SC], AX_X, ALU.max))
                    dve.tensor_scalar(rowmax[:, k:k + 2], rowmax[:, k:k + 2], -1.0, None, ALU.mult).then_inc(maxed, 1)

                def finish_head(it):
                    br = 0 if it.what[0] in ("moba", "fox") else 1
                    h = it.what[1]
                    O = head_bank(it)[:, SC:NB]
                    c = slice(h * HD, (h + 1) * HD)
                    if it.kind == "SM":
                        k = 2 * (it.m % 8)
                        dve.wait_ge(exped, it.softs + 1)
                        link(dve.reciprocal(rowinv[:, k:k + 2], rowsum[:, k:k + 2]))
                        dve.wait_ge(head_out, it.m + 1)
                        dve.tensor_scalar(y[br][:, 0, c], O[:, 0:HD], rowinv[:, k:k + 1], None, ALU.mult)
                        dve.tensor_scalar(y[br][:, 1, c], O[:, HD:P], rowinv[:, k + 1:k + 2], None, ALU.mult)\
                            .then_inc(head_read, 1)
                    else:
                        dve.wait_ge(head_out, it.m + 1)
                        dve.tensor_copy(y[br][:, :, c], O.rearrange("p (t d) -> p t d", t=TT)).then_inc(head_read, 1)

                def sb_clamp(it):
                    dve.wait_ge(scored, it.i + 1)
                    if HEADS[it.m - 2].kind == "SM":
                        dve.wait_ge(exped, HEADS[it.m - 2].softs + 1)
                    else:
                        dve.wait_ge(weighed, it.sbs - 1)
                    s = score[it.m % 2]
                    dve.tensor_tensor(s[:], bank[4 + it.i % 2][:, 0:SC], past, ALU.add).then_inc(read_d, 1)
                    dve.wait_ge(read_d, it.read)
                    dve.tensor_scalar(soft[it.m % 2][:], s[:], 30.0, None, ALU.min).then_inc(clamped, 1)

                def sb_keep(it):
                    dve.wait_ge(softplus, it.sbs + 1)
                    t = soft[it.m % 2]
                    dve.tensor_tensor(t[:], score[it.m % 2][:], t[:], ALU.max).then_inc(kept, 1)

                def sb_weigh(it):
                    dve.wait_ge(turned, it.m + 1)
                    dve.wait_ge(head_out, it.m - 1)
                    dve.tensor_tensor(prob[it.m % 2][:], score[it.m % 2][:], head_bank(it)[:, 0:SC], ALU.subtract)\
                        .then_inc(weighed, 1)

                def accumulate(it):
                    h = it.what
                    dve.wait_ge(read_a, it.read)
                    for tt, c in ((0, slice(0, P)), (1, slice(P, SC))):
                        wt = ifw[:, 8 * tt + h:8 * tt + h + 1]
                        src = soft[it.ix % 2][:, c]
                        if h == 0:
                            ins = dve.tensor_scalar(index[:, c], src, wt, None, ALU.mult)
                        else:
                            ins = dve.scalar_tensor_tensor(index[:, c], src, wt, index[:, c], ALU.mult, ALU.add)
                    ins.then_inc(indexed, 1)
                    dve.wait_ge(indexed, it.ix + 1)
                    if h == NH - 1:
                        link(dve.tensor_tensor(index, index, causal, ALU.add))

                def top_round(k):
                    for tt, c in ((0, slice(0, P)), (1, slice(P, SC))):
                        src = index if k == 0 else work
                        ins = dve.max(m8[:, 8 * tt:8 * tt + 8], src[:, c])
                    link(ins)
                    if k < TOPK // 8 - 1:
                        for tt, c in ((0, slice(0, P)), (1, slice(P, SC))):
                            ins = dve.match_replace(work[:, c], m8[:, 8 * tt:8 * tt + 8], src[:, c], -3e38)
                        link(ins)

                def select():
                    for tt, c in ((0, slice(0, P)), (1, slice(P, SC))):
                        thr = m8[:, 8 * tt + 7:8 * tt + 8]
                        n = ngt[:, tt:tt + 1]
                        link(dve.tensor_scalar(sel[:, c], index[:, c], thr, None, ALU.is_gt, ALU.add, accum_out=n))
                        link(dve.tensor_scalar(n, n, -1.0, float(TOPK), ALU.mult, ALU.add))
                        eq, cs = soft[0][:, c], soft[1][:, c]
                        link(dve.tensor_scalar(eq, index[:, c], thr, None, ALU.is_equal))
                        link(dve.tensor_tensor_scan(cs, eq, eq, 0.0, ALU.add, ALU.max))
                        link(dve.scalar_tensor_tensor(cs, cs, n, eq, ALU.is_le, ALU.mult))
                        link(dve.tensor_tensor(sel[:, c], sel[:, c], cs, ALU.add))
                        link(dve.tensor_scalar(sel[:, c], sel[:, c], -1.0, -NEG, ALU.add, ALU.mult))
                        link(dve.tensor_tensor(sel[:, c], sel[:, c], causal[:, c], ALU.add))

                def y_turned(it):
                    br, tt = it.what
                    dve.wait_ge(y_hi, 4 * b + 2 * br + tt + 1)
                    t = slice(tt * P, (tt + 1) * P)
                    k = slice(4 * br, 4 * br + 4)
                    dve.tensor_tensor(xT_lo[:, k, t], bank[4 + it.i % 2][:].rearrange("p (k t) -> p k t", k=4),
                                      xT_hi[:, k, t], ALU.subtract).then_inc(read_d, 1)

                def merge(br):
                    for q, (tt, n) in enumerate(Q_MIX):
                        if tt == 0:
                            dve.wait_ge(tile_done, TILES[ph] + PROJ + 2 * br + n + 1)
                        else:
                            dve.wait_ge(unit_used, BASE[ph] + 20 + 2 * br + n + 1)
                        if q == 0:
                            dve.wait_ge(sigmoid, 2 * b + br + 1)
                        c = slice(n * NB, (n + 1) * NB)
                        gt = gate[:, tt, br * DM + n * NB:br * DM + (n + 1) * NB]
                        dst = xg[:, tt, c] if br == 0 else gt
                        ins = dve.tensor_tensor(dst, gt, bank[2 * n + tt][:], ALU.mult)
                        if br == 1:
                            link(ins)
                            ins = dve.tensor_tensor(xg[:, tt, c], xg[:, tt, c], gt, ALU.add)
                        ins.then_inc(merged, 1)

                rounds = {21 + k: k for k in range(TOPK // 8)}
                for slot in range(LAST_SLOT):
                    j, q = divmod(slot, 4)
                    if b == 0 and slot == 9:
                        rotate()
                    if b == 0 and q == 0 and 7 <= j <= 10:
                        gate_rows(j - 1)
                    if b == 1:
                        if slot == 9:
                            narrow()
                        if slot == 10:
                            log_f()
                        if slot == 13:
                            norm_rows(0, 18)
                        if slot == 17:
                            norm_rows(512, 20)
                        if slot == 25:
                            norm_rows(0, 24)
                    for it in ITEMS[b]:
                        d = slot - it.slot
                        if (it.kind == "SM" and d == SM_AT["norm"]) or (it.kind == "SB" and d == SB_AT["norm"]):
                            finish_head(it)
                        if it.kind == "SB" and d == SB_AT["weigh"]:
                            sb_weigh(it)
                        if it.kind == "SB" and d == SB_AT["keep"]:
                            sb_keep(it)
                        if it.kind == "SB" and d == SB_AT["clamp"]:
                            sb_clamp(it)
                        if it.kind == "SM" and d == SM_AT["soft"]:
                            soften(it)
                        if it.kind == "IX" and d == 2:
                            accumulate(it)
                        if it.kind == "TY" and d == 1:
                            y_turned(it)
                    if b == 1 and slot in rounds:
                        top_round(rounds[slot])
                    if b == 1 and slot == 28:
                        select()
                    if q in (0, 2):
                        for u in next_units(ph, j)[q // 2:q // 2 + 1]:
                            split_lo(u)
                    if slot == 45:
                        merge(0)
                for u in next_units(ph, 12):
                    split_lo(u)
                merge(1)
                for q, (tt, n) in enumerate(Q_MIX):
                    dve.wait_ge(mT_hi, 4 * b + q + 1)
                    t = slice(tt * P, (tt + 1) * P)
                    dve.tensor_tensor(xT_lo[:, 4 * n:4 * n + 4, t],
                                      bank[4 + q][:].rearrange("p (k t) -> p k t", k=4),
                                      xT_hi[:, 4 * n:4 * n + 4, t], ALU.subtract).then_inc(mT_lo, 1)
                for u in next_units(ph, 13):
                    split_lo(u)

            dve.wait_ge(pos_in, 32)
            dve.wait_ge(freq_set, 1)
            link(dve.tensor_copy(posf, posi[:]))
            for tt in range(TT):
                ins = dve.tensor_scalar(sinr[:, 8 * tt:8 * tt + 8], freq, posf[:, tt:tt + 1], None, ALU.mult)
            link(ins)
            link(dve.tensor_scalar(ki[:], sinr, 0.15915494309189535, None, ALU.mult))
            link(dve.tensor_copy(cosr, ki[:]))
            for part in (-6.28125, -0.0019350051879882812, -3.0199159819567953e-07):
                link(dve.scalar_tensor_tensor(sinr, cosr, part, sinr, ALU.mult, ALU.add))
            link(dve.tensor_scalar(sinr, sinr, 3.1415925, -3.1415925, ALU.min, ALU.max))
            link(dve.scalar_tensor_tensor(cosr, sinr, -1.0, sinr, ALU.mult, ALU.max))
            dve.tensor_scalar(cosr, cosr, -1.0, 1.5707963267948966, ALU.mult, ALU.add).then_inc(ang_done, 1)

            dve.wait_ge(x_in, 32)
            residual("F0", 0.5)
            for u in STEPS[0][2]:
                split_lo(u)
            ffn("F0")
            residual("M0", 0.5)
            mixer(0)
            residual("F1", 1.0)
            ffn("F1")
            dve.wait_ge(gain_in, 16 * 4)
            for q, (tt, n) in enumerate(Q_FFN):
                c = slice(n * NB, (n + 1) * NB)
                wait_quarter(dve, "F1", q)
                ins = dve.scalar_tensor_tensor(x[:, tt, c], acc_bank("F1", tt, n)[:], 0.5, x[:, tt, c],
                                               ALU.mult, ALU.add)
            ins.then_inc(gained, 1)
            rms(3)
            dve.wait_ge(rstd_done, 4)
            for tt in range(TT):
                ins = dve.scalar_tensor_tensor(x[:, tt, :], x[:, tt, :], rstd[:, 6 + tt:7 + tt], gain[1][:],
                                               ALU.mult, ALU.mult)
            ins.then_inc(gained, 3)
            dve.wait_ge(gained, 16)
            residual("F2", 0.5)
            ffn("F2")
            residual("M1", 0.5)
            mixer(1)
            residual("F3", 1.0)
            ffn("F3")
            for q, (tt, n) in enumerate(Q_FFN):
                c = slice(n * NB, (n + 1) * NB)
                wait_quarter(dve, "F3", q)
                dve.scalar_tensor_tensor(x[:, tt, c], acc_bank("F3", tt, n)[:], 0.5, x[:, tt, c],
                                         ALU.mult, ALU.add).then_inc(gained, 1)

        @block.tensor
        def _(pe):
            def three(dst, st, hi, lo, mhi, mlo, start, stop):
                pe.matmul(dst, st(hi), mhi, start=start, stop=False)
                pe.matmul(dst, st(hi), mlo, start=False, stop=False)
                return pe.matmul(dst, st(lo), mhi, start=False, stop=stop)

            def rows(u, width, k4, col=0, n=NB):
                o = k4 * width + col
                return w_hi[u % SLOTS][:, o:o + n], w_lo[u % SLOTS][:, o:o + n]

            def four(u, tt, dst, k0, first, last, n=NB):
                for k4 in range(4):
                    mh, ml = rows(u, n, k4, 0, n)
                    m = three(dst, lambda z, k=k0 + k4: z[:, k, tt * P:(tt + 1) * P], xT_hi, xT_lo, mh, ml,
                              first and k4 == 0, last and k4 == 3)
                return m

            def prep(ph):
                p = PREP_OF[ph]
                for q, (tt, n) in enumerate(quarters(ph)):
                    pe.wait_ge(gained, 4 * GAIN_OF[ph] + q + 1)
                    for k in range(4):
                        ins = pe.transpose(bank[turn_banks(ph)[q]][:, k * P:(k + 1) * P],
                                           xg[:, tt, n * NB + k * P:n * NB + (k + 1) * P], ident)
                    ins.then_inc(x_turned, 1)

            def chunk(ph, c, hf, i=0, first=False):
                u = BASE[ph] + 2 * c + hf
                pe.wait_ge(lo_done, u + 1 + 4 * i)
                for tt in range(TT):
                    if first:
                        pe.wait_ge(xT_lo_done, 4 * PREP_OF[ph] + quarters(ph).index((tt, hf)) + 1)
                    m = four(u, tt, bank[2 * (c % 2) + tt][:], 4 * hf, hf == 0, hf == 1)
                    if tt == 0 and hf == 1:
                        m.then_inc(tile_done, 1)
                m.then_inc(unit_used, 1)

            def turn_hidden(ph, c, i=0):
                for tt in range(TT):
                    pe.wait_ge(h_done, 2 * NCH * FFN_OF[ph] + 2 * c + tt + 1 + 4 * i)
                    for k in range(2):
                        ins = pe.transpose(bank[6 + c % 2][:, k * SEQ + tt * P:k * SEQ + (tt + 1) * P],
                                           hs[c % 2][tt][:, k * P:(k + 1) * P], ident)
                ins.then_inc(h_turned, 1)

            def ffn(ph):
                prep(ph)
                chunk(ph, 0, 0, first=True)
                chunk(ph, 0, 1, first=True)
                with pe.Fori(0, (NCH - 1) // 2) as i:
                    for j in range(2):
                        chunk(ph, 1 + j, 0, i)
                        turn_hidden(ph, j, i)
                        chunk(ph, 1 + j, 1, i)
                for d in range(NCH):
                    u = BASE[ph] + 2 * NCH + d
                    pe.wait_ge(lo_done, u + 1)
                    pe.wait_ge(hT_lo_done, NCH * FFN_OF[ph] + d + 1)
                    for q, (tt, n) in enumerate(Q_FFN):
                        for k in range(2):
                            mh, ml = rows(u, DM, k, n * NB)
                            m = three(acc_bank(ph, tt, n)[:], lambda z: z[:, 2 * d + k, tt * P:(tt + 1) * P],
                                      hT_hi, hT_lo, mh, ml, d == 0 and k == 0, d == NCH - 1 and k == 1)
                        if d == NCH - 1 and q < 3:
                            m.then_inc(tile_done, 1)
                    m.then_inc(unit_used, 1)
                    if d == 0:
                        turn_hidden(ph, NCH - 1)

            def mixer(b):
                ph = ("M0", "M1")[b]
                u0 = BASE[ph]
                prep(ph)

                def score_bank(it):
                    if it.i >= 2:
                        was = FLAT[it.i - 2]
                        pe.wait_ge(read_sem(was), was.read)
                    return bank[4 + it.i % 2]

                def read_sem(was):
                    return read_d if was.reader == "d" else read_a

                def turn(it):
                    name, tt = it.what if it.kind == "TR" else ("cu", 0)
                    if b == 0:
                        if name in ("qa", "ka"):
                            pe.wait_ge(rows_ready, 2)
                        else:
                            pe.wait_ge(evac_act, {"qb": 8, "kb": 10}[name])
                    elif name == "iq":
                        pe.wait_ge(evac_act, 14)
                    else:
                        if name == "kk":
                            pe.wait_ge(evac_act, 16)
                        pe.wait_ge(rows_ready, {"kk": 3, "cu": 4, "fq": 5, "fk": 6, "dq": 7}[name])
                    S = score_bank(it)
                    if name == "cu":
                        pe.matmul(S[0:NH, 0:P], lgf[:, 0:8], tri_le, start=True, stop=True)
                        pe.matmul(S[0:NH, P:SEQ], lgf[:, 0:8], ones, start=True, stop=False)
                        pe.matmul(S[0:NH, P:SEQ], lgf[:, 8:16], tri_le, start=False, stop=True).then_inc(scored, 1)
                        return
                    c0 = {"qa": 0, "ka": 512, "qb": 0, "kb": 512, "iq": 0, "kk": 512, "fq": 0, "fk": 512, "dq": 0}[name]
                    n = 2 if name == "kk" else 4
                    for k in range(n):
                        ins = pe.transpose(S[:, k * P:(k + 1) * P], xg[:, tt, c0 + k * P:c0 + (k + 1) * P], ident)
                    ins.then_inc(scored, 1)

                def operands(it):
                    kind, h = it.what if it.kind != "IX" else ("idx", it.what)
                    r = slice(HD * (h % 2), HD * (h % 2) + HD)
                    c = slice(h * HD, (h + 1) * HD)
                    iqT = y[1][:].rearrange("p t (k n) -> p (t k) n", k=2)
                    if kind in ("moba", "fox"):
                        return qT_a[r, h // 2, :], kT_a[r, h // 2, :], v_a[:, :, c]
                    if kind == "sb":
                        return qT_b[r, h // 2, :], kT_b[r, h // 2, :], v_b[:, :, c]
                    if kind == "dsa":
                        return qT_b[r, h // 2, :], dkT[r, :], dv[:]
                    return iqT[r, h // 2, :], ikT[r, :], None

                def scores(it):
                    kind, h = it.what if it.kind != "IX" else ("idx", it.what)
                    need = {"moba": "ka", "fox": "fk", "sb": "kb", "dsa": "dq", "idx": "kk"}[kind]
                    pe.wait_ge(read_a, max(t.read for t in ITEMS[b] if t.kind in ("TR", "CU") and
                                           (t.what[:1] or ("cu",))[0] in ((need, "cu") if kind == "fox" else (need,))))
                    S = score_bank(it)
                    q, k, _ = operands(it)
                    if kind == "fox":
                        pick = const[0:NH, C_ID + h:C_ID + h + 1].to_broadcast([NH, P])
                        pe.matmul(S[:, 0:P], q[:, 0:P], k[:, 0:P], start=True, stop=False)
                        pe.matmul(S[:, 0:P], pick, ncum[:, 0:P], start=False, stop=True)
                        pe.matmul(S[:, P:SC], q[:, P:SEQ], k, start=True, stop=False)
                        pe.matmul(S[:, P:SC], pick, ncum[:], start=False, stop=True).then_inc(scored, 1)
                    elif kind == "sb":
                        pe.matmul(S[:, 0:SEQ], k[:, 0:P], q, start=True, stop=True)
                        pe.matmul(S[:, SEQ:SC], k[:, P:SEQ], q[:, P:SEQ], start=True, stop=True).then_inc(scored, 1)
                    else:
                        pe.matmul(S[:, 0:P], q[:, 0:P], k[:, 0:P], start=True, stop=True)
                        pe.matmul(S[:, P:SC], q[:, P:SEQ], k, start=True, stop=True).then_inc(scored, 1)

                def turn_free(it):
                    if it.m >= 2:
                        pe.wait_ge(head_read, it.m - 1)
                    return head_bank(it)

                def turn_probs(it):
                    pe.wait_ge(exped, it.softs + 1)
                    B = turn_free(it)
                    for k in range(3):
                        ins = pe.transpose(B[:, k * P:(k + 1) * P], prob[it.m % 2][:, k * P:(k + 1) * P], ident)
                    ins.then_inc(turned, 1)

                def sb_sum(it):
                    pe.wait_ge(kept, it.sbs + 1)
                    B = turn_free(it)
                    t = soft[it.m % 2]
                    pe.matmul(B[:, 0:P], tri_ge, t[:, 0:P], start=True, stop=True)
                    pe.matmul(B[:, P:SEQ], tri_ge, t[:, P:SEQ], start=True, stop=False)
                    pe.matmul(B[:, P:SEQ], ones, t[:, SEQ:SC], start=False, stop=True)
                    pe.matmul(B[:, SEQ:SC], tri_ge, t[:, SEQ:SC], start=True, stop=True).then_inc(turned, 1)

                def head(it):
                    if it.kind == "SM":
                        pe.wait_ge(copied, it.softs + 1)
                        w = probT[it.m % 2]
                    else:
                        pe.wait_ge(w_done, it.sbs + 1)
                        w = prob[it.m % 2]
                    _, _, v = operands(it)
                    O = head_bank(it)[:, SC:NB]
                    pe.matmul(O[:, 0:HD], w[:, 0:P], v[:, 0, :], start=True, stop=True)
                    pe.matmul(O[:, HD:P], w[:, P:SEQ], v[:, 0, :], start=True, stop=False)
                    pe.matmul(O[:, HD:P], w[:, SEQ:SC], v[:, 1, :], start=False, stop=True).then_inc(head_out, 1)

                def y_turn(it):
                    br, tt = it.what
                    last = max(t.m for t in HEADS if t.b == b and (t.what[0] in ("moba", "fox")) == (br == 0))
                    pe.wait_ge(head_read, last + 1)
                    S = score_bank(it)
                    for k in range(4):
                        ins = pe.transpose(S[:, k * P:(k + 1) * P], y[br][:, tt, k * P:(k + 1) * P], ident)
                    ins.then_inc(scored, 1)

                def project(j, q):
                    hf, tt = divmod(q, 2)
                    u = u0 + 2 * j + hf
                    pe.wait_ge(lo_done, u + 1)
                    n = NB if proj_at[b][j] is not None else NW
                    if j == 0:
                        pe.wait_ge(xT_lo_done, 4 * PREP_OF[ph] + quarters(ph).index((tt, hf)) + 1)
                    if j >= 2 and hf == 0 and tt == 0:
                        if j - 2 < 6:
                            pe.wait_ge(evac_act, 12 * b + 2 * (j - 1))
                        elif b == 0:
                            pe.wait_ge(evac_dve, 2 * (j - 7))
                        else:
                            pe.wait_ge(gated, 2 * (j - 7))
                    m = four(u, tt, bank[2 * (j % 2) + tt][:, 0:n], 4 * hf, hf == 0, hf == 1, n)
                    if tt == 1:
                        m.then_inc(unit_used, 1)
                    elif hf == 1:
                        m.then_inc(tile_done, 1)

                def branch(br, q):
                    n, tt = divmod(q, 2)
                    u = u0 + 20 + 2 * br + n
                    pe.wait_ge(lo_done, u + 1)
                    ty = [t for t in ITEMS[b] if t.kind == "TY" and t.what == (br, tt)][0]
                    pe.wait_ge(read_d, ty.read)
                    if br == 0:
                        pe.wait_ge(gated if b else evac_dve, 8)
                    else:
                        pe.wait_ge(merged, 8 * b + q + 1)
                    m = four(u, tt, bank[2 * n + tt][:], 4 * br, True, True)
                    m.then_inc(unit_used if tt else tile_done, 1)

                for slot in range(LAST_SLOT):
                    j, q = divmod(slot, 4)
                    if j < PROJ:
                        project(j, q)
                    elif slot < 44:
                        branch(0, q)
                    for it in ITEMS[b]:
                        d = slot - it.slot
                        if (it.kind == "SM" and d == SM_AT["out"]) or (it.kind == "SB" and d == SB_AT["out"]):
                            head(it)
                        if it.kind == "SB" and d == SB_AT["sum"]:
                            sb_sum(it)
                        if it.kind == "SM" and d == SM_AT["turn"]:
                            turn_probs(it)
                        if it.kind in ("TR", "CU") and d == 0:
                            turn(it)
                        if it.kind in ("SM", "SB", "IX") and d == 0:
                            scores(it)
                        if it.kind == "TY" and d == 0:
                            y_turn(it)
                for q in range(4):
                    branch(1, q)
                for q, (tt, n) in enumerate(Q_MIX):
                    pe.wait_ge(merged, 8 * b + 4 + q + 1)
                    for k in range(4):
                        ins = pe.transpose(bank[4 + q][:, k * P:(k + 1) * P],
                                           xg[:, tt, n * NB + k * P:n * NB + (k + 1) * P], ident)
                    ins.then_inc(m_turned, 1)
                for n in range(2):
                    for hf in range(2):
                        u = u0 + 24 + 2 * n + hf
                        pe.wait_ge(lo_done, u + 1)
                        for tt in range(TT):
                            pe.wait_ge(mT_lo, 4 * b + Q_MIX.index((tt, hf)) + 1)
                            m = four(u, tt, bank[2 * n + tt][:], 4 * hf, hf == 0, hf == 1)
                            if tt == 0 and hf == 1:
                                m.then_inc(tile_done, 1)
                        m.then_inc(unit_used, 1)

            pe.wait_ge(table_in, 32)
            for h in range(NH):
                if h >= 4:
                    pe.wait_ge(vrow_sb, h - 3)
                pe.matmul(bank[h % 4][:, 0:SC], lgt[0:32, h:h + 1].to_broadcast([32, P]), onehot[0:32, :],
                          start=True, stop=True).then_inc(vrow_mm, 1)
            pe.wait_ge(const_in, 16)
            for ph in PHASES:
                if ph[0] == "F":
                    ffn(ph)
                else:
                    mixer(int(ph[1]))


def lag_buckets(n_buckets, max_distance, lags):
    import numpy as np
    exact = n_buckets // 2
    rel = np.maximum(lags, 1).astype(np.float32)
    large = exact + (np.log(rel / np.float32(exact)) / np.float32(np.log(max_distance / exact))
                     * np.float32(n_buckets - exact)).astype(np.int32)
    return np.where(lags < exact, lags, np.minimum(large, n_buckets - 1))


def constants():
    import numpy as np
    c = np.zeros((P, C_END), np.float32)
    p, f = np.arange(P)[:, None], np.arange(P)[None, :]
    c[:, C_ID:C_ID + P] = p == f
    c[:, C_CAUSAL:C_CAUSAL + P] = c[:, C_CAUSAL + 2 * P:C_CAUSAL + 3 * P] = np.where(f <= p, 0, NEG)
    c[:, C_PAST:C_PAST + P] = c[:, C_PAST + 2 * P:C_PAST + 3 * P] = np.where(p < f, 0, NEG)
    c[:, C_GE:C_GE + P] = p >= f
    c[:, C_ONE:C_ONE + P] = 1
    c[:, C_LE:C_LE + P] = p <= f
    bucket = lag_buckets(32, 128, np.maximum(SEQ - 1 - np.arange(SC), 0))
    onehot = (np.arange(32)[:, None] == bucket[None, :]).astype(np.float32)
    return c, onehot


def kernel(**inputs):
    import numpy as np
    import concourse.bacc as bacc
    from concourse.bass_utils import run_bass_kernel_spmd

    nc = bacc.Bacc("TRN2", target_bir_lowering=False, num_devices=1)
    arrays, aps = {}, {}
    consts, onehot = constants()
    shape_only = {"consts": consts, "onehot": onehot}
    for name, v in {**inputs, **shape_only}.items():
        v = np.ascontiguousarray(v)
        if v.ndim > 1 and v.shape[0] == 1 and name not in ("x", "positions"):
            v = v[0]
        arrays["in_" + name] = v
        aps[name] = nc.dram_tensor("in_" + name, v.shape, mybir.dt.from_np(v.dtype), kind="ExternalInput").ap()
    o = nc.dram_tensor("result", (1, SEQ, DM), F32, kind="ExternalOutput").ap()
    build(nc, aps, o)
    r = run_bass_kernel_spmd(nc, [arrays], core_ids=[0])
    return r.results[0]["result"]
```

```python
from contextlib import ExitStack

import concourse.bass as bass
from concourse import mybir

F32 = mybir.dt.float32
F32R = mybir.dt.float32r
I32 = mybir.dt.int32
ALU = mybir.AluOpType
ACT = mybir.ActivationFunctionType
AX_X = mybir.AxisListType.X

P = 128
SEQ = 256
DM = 1024
FF = 2816
HD = 64
NH = 8
HW = NH * HD
KC = DM // P
TT = SEQ // P
NB = 512
CH = 256
NCH = FF // CH
EPS = 1e-6
NEG = -1e30
TOPK = min(256, SEQ // 4)
SC = 384

SLOTS = 4
UNIT = 2048
DMAS = 2

FFN_UNITS = 2 * NCH + NCH
PROJ = 10
MIX_UNITS = 2 * PROJ + 4 + 4
BASE = {}
_n = 0
for _ph, _k in (("F0", FFN_UNITS), ("M0", MIX_UNITS), ("F1", FFN_UNITS),
                ("F2", FFN_UNITS), ("M1", MIX_UNITS), ("F3", FFN_UNITS)):
    BASE[_ph] = _n
    _n += _k
UNITS = _n
TILES = {"F0": 0, "M0": 14, "F1": 30, "F2": 44, "M1": 58, "F3": 74}
FFN_OF = {"F0": 0, "F1": 1, "F2": 2, "F3": 3}
PREP_OF = {"F0": 0, "M0": 1, "F1": 2, "F2": 3, "M1": 4, "F3": 5}
NARROW = BASE["M1"] + 2
NW = 208


def steps_of(phase):
    b = BASE[phase]
    if phase[0] == "F":
        s = [[b + 2 * c, b + 2 * c + 1] for c in range(NCH)]
        d = b + 2 * NCH
        return s + [[u for u in (d + i, d + i + 1) if u < d + NCH] for i in range(0, NCH, 2)]
    return [[b + 2 * j, b + 2 * j + 1] for j in range(MIX_UNITS // 2)]


PHASES = ("F0", "M0", "F1", "F2", "M1", "F3")
STEPS = [(ph, i, us) for ph in PHASES for i, us in enumerate(steps_of(ph))]


def next_units(phase, i):
    n = next(k for k, s in enumerate(STEPS) if s[:2] == (phase, i)) + 1
    return STEPS[n][2] if n < len(STEPS) else []


def landed(u):
    n = sum(DMAS + (v in (NARROW, NARROW + 1)) for v in range(u % SLOTS, u + 1, SLOTS))
    return 16 * n


def items_of(b):
    if b == 0:
        out = [(11, "TR", ("qa", 0)), (11, "TR", ("qa", 1)), (12, "TR", ("ka", 0)), (12, "TR", ("ka", 1))]
        out += [(t, "SM", ("moba", h)) for h, t in enumerate((14, 15, 17, 18, 19, 21, 22, 23))]
        out += [(18, "TR", ("qb", 0)), (19, "TR", ("qb", 1)), (22, "TR", ("kb", 0)), (23, "TR", ("kb", 1))]
        out += [(t, "SB", ("sb", h)) for h, t in enumerate((25, 27, 28, 30, 31, 33, 34, 36))]
        out += [(39, "TY", (0, 0)), (39, "TY", (0, 1)), (44, "TY", (1, 0)), (44, "TY", (1, 1))]
    else:
        out = [(6, "TR", ("iq", 0)), (7, "TR", ("iq", 1)), (11, "TR", ("kk", 0)), (11, "TR", ("kk", 1)),
               (11, "CU", ())]
        out += [(12 + h, "IX", h) for h in range(NH)]
        out += [(15, "TR", ("fq", 0)), (15, "TR", ("fq", 1)), (19, "TR", ("fk", 0)), (19, "TR", ("fk", 1))]
        out += [(t, "SM", ("fox", h)) for h, t in enumerate((21, 22, 23, 25, 26, 27, 28, 29))]
        out += [(27, "TR", ("dq", 0)), (27, "TR", ("dq", 1))]
        out += [(t, "SM", ("dsa", h)) for h, t in enumerate((31, 32, 34, 35, 36, 37, 38, 39))]
        out += [(39, "TY", (0, 0)), (39, "TY", (0, 1)), (44, "TY", (1, 0)), (44, "TY", (1, 1))]
    return sorted(out, key=lambda x: x[0])


class Item:
    pass


def plan():
    items, i, m, reads = {0: [], 1: []}, 0, 0, {"a": 0, "d": 0}
    turned = ix = softs = sbs = 0
    flat = []
    for b in (0, 1):
        for slot, kind, what in items_of(b):
            it = Item()
            it.b, it.slot, it.kind, it.what, it.i, it.m = b, slot, kind, what, i, m
            it.reader = "a" if kind in ("TR", "IX", "CU") else "d"
            reads[it.reader] += 1
            it.read = reads[it.reader]
            if kind in ("TR", "CU"):
                turned += 1
                it.turned = turned
            if kind == "IX":
                it.ix = ix
                ix += 1
            if kind == "SM":
                it.softs = softs
                softs += 1
            if kind == "SB":
                it.sbs = sbs
                sbs += 1
            if kind in ("SM", "SB"):
                m += 1
            i += 1
            items[b].append(it)
            flat.append(it)
    return items, flat


ITEMS, FLAT = plan()
HEADS = [it for it in FLAT if it.kind in ("SM", "SB")]


def turned_after(b, name):
    return max(it.turned for it in ITEMS[b] if it.kind in ("TR", "CU") and (it.what[:1] or ("cu",))[0] == name)


SM_AT = dict(soft=1, turn=2, out=3, norm=4)
SB_AT = dict(clamp=1, keep=2, sum=3, weigh=4, out=5, norm=6)
LAST_SLOT = 48

INV_FREQ = [500000.0 ** (-k * 2.0 / 16) for k in range(8)]
C_ID, C_CAUSAL, C_PAST, C_GE, C_ONE, C_LE, C_END = 0, 128, 512, 896, 1024, 1152, 1280


def build(nc, a, out):
    ctx = ExitStack()
    with ctx:
        def sb(name, shape, dt=F32):
            return ctx.enter_context(nc.sbuf_tensor(name, shape, dt))

        def sem(name):
            return ctx.enter_context(nc.semaphore(name))

        bank = [ctx.enter_context(nc.psum_tensor(f"bank{i}", [P, NB], F32)) for i in range(8)]

        raw = [sb(f"raw{i}", [P, UNIT]) for i in range(SLOTS)]
        w_hi = [sb(f"w_hi{i}", [P, UNIT], F32R) for i in range(SLOTS)]
        w_lo = [sb(f"w_lo{i}", [P, UNIT], F32R) for i in range(SLOTS)]
        x = sb("x", [P, TT, DM])
        xg = sb("xg", [P, TT, DM])
        xT_hi = sb("xT_hi", [P, KC, SEQ], F32R)
        xT_lo = sb("xT_lo", [P, KC, SEQ], F32R)
        gain = [sb(f"gain{i}", [P, DM]) for i in range(2)]
        gate = sb("gate", [P, TT, 2 * DM])
        const = sb("const", [P, C_END])
        small = sb("small", [P, 256])
        hid = ExitStack()
        with hid:
            hT_hi = hid.enter_context(nc.sbuf_tensor("hT_hi", [P, FF // P, SEQ], F32R))
            hT_lo = hid.enter_context(nc.sbuf_tensor("hT_lo", [P, FF // P, SEQ], F32R))
        mix = ctx.enter_context(ExitStack())

        def mb(name, shape, dt=F32):
            return mix.enter_context(nc.sbuf_tensor(name, shape, dt))

        v_a = mb("v_a", [P, TT, HW])
        y = [mb("y_a", [P, TT, HW]), mb("y_b", [P, TT, HW])]
        qT_a = mb("qT_a", [P, HW // P, SEQ])
        kT_a = mb("kT_a", [P, HW // P, SEQ])
        qT_b = mb("qT_b", [P, HW // P, SEQ])
        score = [mb(f"score{i}", [P, SC]) for i in range(2)]
        prob = [mb(f"prob{i}", [P, SC]) for i in range(2)]
        probT = [mb(f"probT{i}", [P, SC]) for i in range(2)]
        soft = [mb(f"soft{i}", [P, SC]) for i in range(2)]
        late = ExitStack()
        with late:
            kT_b = late.enter_context(nc.sbuf_tensor("kT_b", [P, HW // P, SEQ], F32))
            v_b = late.enter_context(nc.sbuf_tensor("v_b", [P, TT, HW], F32))
            b_row = [late.enter_context(nc.sbuf_tensor(f"b_row{i}", [P, NB], F32)) for i in range(2)]
        ikT = mb("ikT", [P, SEQ])
        dkT = mb("dkT", [P, SEQ])
        dv = mb("dv", [P, TT, HD])
        index, work = gate[:, 1, DM:DM + SC], gate[:, 0, DM:DM + SC]
        sel = mb("sel", [P, SC])
        toep = mb("toep", [P, NH, SEQ])
        hg = mb("hg", [P, 4])
        ncum = mb("ncum", [NH, SEQ])

        at = [0]

        def cols(n):
            at[0] += n
            return small[:, at[0] - n:at[0]]

        ss = cols(14)
        rstd = cols(14)
        nv, ny, nt = cols(16), cols(16), cols(16)
        hss = cols(16)
        rowmax = cols(16)
        rowsum = cols(16)
        rowinv = cols(16)
        ifw = cols(16)
        lgf = cols(16)
        lgt = cols(16)
        m8 = cols(16)
        ngt = cols(2)
        freq = cols(8)
        cosr = cols(16)
        sinr = cols(16)
        posf = cols(2)
        bfor = cols(8)
        posi = sb("posi", [P, 2], I32)
        nyi = sb("nyi", [P, 16], I32)
        ki = sb("ki", [P, 16], I32)
        hs = [[gate[:, 1, DM + (2 * i + t) * CH:DM + (2 * i + t + 1) * CH] for t in range(TT)] for i in range(2)]
        gsil = [gate[:, 0, DM + t * CH:DM + (t + 1) * CH] for t in range(TT)]
        onehot = gate[0:32, 1, 0:SC]
        gain_zf = gate[:, 1, 0:DM]
        lag_rows = gate[0:NH, 1, SC:2 * SC]

        raw_in = [sem(f"raw_in{i}") for i in range(SLOTS)]
        hi_done = sem("hi_done")
        lo_done = sem("lo_done")
        unit_used = sem("unit_used")
        tile_done = sem("tile_done")
        x_in = [sem("x_in0"), sem("x_in1")]
        ident_in = sem("ident_in")
        const_in = sem("const_in")
        gain_in = sem("gain_in")
        gained = sem("gained")
        x_turned = sem("x_turned")
        xT_hi_done = sem("xT_hi_done")
        xT_lo_done = sem("xT_lo_done")
        squared = sem("squared")
        rstd_done = sem("rstd_done")
        silu_done = sem("silu_done")
        h_done = sem("h_done")
        h_turned = sem("h_turned")
        hT_hi_done = sem("hT_hi_done")
        hT_lo_done = sem("hT_lo_done")
        evac_act = sem("evac_act")
        evac_dve = sem("evac_dve")
        rows_ready = sem("rows_ready")
        scored = sem("scored")
        read_a = sem("read_a")
        read_d = sem("read_d")
        maxed = sem("maxed")
        exped = sem("exped")
        turned = sem("turned")
        copied = sem("copied")
        weighed = sem("weighed")
        clamped = sem("clamped")
        softplus = sem("softplus")
        kept = sem("kept")
        w_done = sem("w_done")
        head_out = sem("head_out")
        head_read = sem("head_read")
        indexed = sem("indexed")
        y_hi = sem("y_hi")
        y_lo = sem("y_lo")
        gated = sem("gated")
        sigmoid = sem("sigmoid")
        merged = sem("merged")
        m_turned = sem("m_turned")
        mT_hi = sem("mT_hi")
        mT_lo = sem("mT_lo")
        logf = sem("logf")
        lnf = sem("lnf")
        vrow_mm = sem("vrow_mm")
        vrow_sb = sem("vrow_sb")
        vrow_out = sem("vrow_out")
        table_in = sem("table_in")
        b_row_in = [sem("b_row_in0"), sem("b_row_in1")]
        pos_in = sem("pos_in")
        freq_set = sem("freq_set")
        ang_done = sem("ang_done")
        sin_done = sem("sin_done")
        mix_in = sem("mix_in")
        dve_chain = sem("dve_chain")
        act_chain = sem("act_chain")
        stored = sem("stored")

        ident = const[:, C_ID:C_ID + P]
        causal = const[:, C_CAUSAL:C_CAUSAL + SC]
        past = const[:, C_PAST:C_PAST + SC]
        tri_ge = const[:, C_GE:C_GE + P]
        ones = const[:, C_ONE:C_ONE + P]
        tri_le = const[:, C_LE:C_LE + P]

        bias_rows = nc.dram_tensor("bias_rows", [NH, P, SC], F32).ap()

        ffn_w = [("ffn1_w_gate", "ffn1_w_up", "ffn1_w_down"), ("ffn2_w_gate", "ffn2_w_up", "ffn2_w_down"),
                 ("ffn1_w_gate_2", "ffn1_w_up_2", "ffn1_w_down_2"),
                 ("ffn2_w_gate_2", "ffn2_w_up_2", "ffn2_w_down_2")]
        branch_w = [("w_branch_moba", "w_branch_sb"), ("w_branch_a_2", "w_branch_b_2")]
        out_w = ["w_out", "w_out_2"]
        proj_at = [[512 * j for j in range(PROJ)],
                   [2184, None, 0, 512, 1024, 1544, 2768, 3280, 3792, 4304]]
        gains = ["ffn1_norm", "mix_norm", "ffn2_norm", "final_norm",
                 "ffn1_norm_2", "mix_norm_2", "ffn2_norm_2"]
        GAIN_OF = {"F0": 0, "M0": 1, "F1": 2, "Z": 3, "F2": 4, "M1": 5, "F3": 6}
        Q_FFN = [(0, 0), (0, 1), (1, 0), (1, 1)]
        Q_MIX = [(0, 0), (1, 0), (0, 1), (1, 1)]
        PREV = dict(zip(PHASES[1:], PHASES))
        NEXT = dict(zip(PHASES, PHASES[1:]))
        EARLY = {"M0": 1, "F1": 2, "F2": 1, "M1": 1, "F3": 2}

        def quarters(ph):
            return Q_MIX if ph in ("F0", "F1", "F3") else Q_FFN

        def turn_banks(ph):
            return [4, 5, 6, 7] if ph in ("F0", "F1", "F3") else [0, 1, 6, 7]

        def acc_bank(ph, tt, n):
            return bank[2 + 2 * tt + n] if ph[0] == "F" else bank[2 * n + tt]

        def wait_quarter(eng, ph, q):
            if ph[0] == "F":
                if q < 3:
                    eng.wait_ge(tile_done, TILES[ph] + NCH + q + 1)
                else:
                    eng.wait_ge(unit_used, BASE[ph] + FFN_UNITS)
            elif q % 2 == 0:
                eng.wait_ge(tile_done, TILES[ph] + PROJ + 4 + q // 2 + 1)
            else:
                eng.wait_ge(unit_used, BASE[ph] + MIX_UNITS - 2 + 2 * (q // 2))

        def wait_chunk(eng, ph, j, tt):
            if tt == 0:
                eng.wait_ge(tile_done, TILES[ph] + j + 1)
            else:
                eng.wait_ge(unit_used, BASE[ph] + 2 * j + 2)

        def head_bank(it):
            return bank[6 + it.m % 2]

        block = ctx.enter_context(nc.Block())

        @block.sync
        def _(sp):
            def load_x(n):
                c = slice(n * NB, (n + 1) * NB)
                for tt in range(TT):
                    sp.dma_start(x[:, tt, c], a["x"][0, tt * P:(tt + 1) * P, c]).then_inc(x_in[n], 16)

            def free(u, i=0, k=0):
                if u >= SLOTS:
                    sp.wait_ge(lo_done, u + k * i - SLOTS + 1)

            def put(u, dst, src):
                sp.dma_start(dst, src).then_inc(raw_in[u % SLOTS], 16)

            def load_gate_up(f, c, hf, u, i=0, k=0):
                free(u, i, k)
                slot = raw[u % SLOTS][:].rearrange("p (k n) -> p k n", k=4)
                for s in range(2):
                    w = a[ffn_w[f][s]].rearrange("(k p) (c n) -> p k c n", p=P, n=CH)
                    put(u, slot[:, :, s * CH:(s + 1) * CH], w[:, 4 * hf:4 * hf + 4, c, :])

            def load_rows(w, u, r0, rows, c0, width):
                free(u)
                slot = raw[u % SLOTS][:, 0:rows * width].rearrange("p (k n) -> p k n", k=rows)
                w = w.rearrange("(k p) n -> p k n", p=P)
                h = rows // 2
                for s in range(2):
                    put(u, slot[:, s * h:(s + 1) * h, :], w[:, r0 + s * h:r0 + (s + 1) * h, c0:c0 + width])

            def load_narrow(u, hf):
                free(u)
                slot = raw[u % SLOTS][:, 0:4 * NW].rearrange("p (k n) -> p k n", k=4)
                w = a["w_in_2"].rearrange("(k p) n -> p k n", p=P)[:, 4 * hf:4 * hf + 4, :]
                put(u, slot[:, :, 0:8], w[:, :, 1536:1544])
                put(u, slot[:, :, 8:136], w[:, :, 2056:2184])
                put(u, slot[:, :, 136:208], w[:, :, 2696:2768])

            for ph in PHASES:
                u0 = BASE[ph]
                if ph[0] == "F":
                    f = FFN_OF[ph]
                    for c in range(1):
                        for hf in range(2):
                            if ph == "F0":
                                load_x(hf)
                            load_gate_up(f, c, hf, u0 + 2 * c + hf)
                    if ph == "F0":
                        load_gate_up(f, 1, 0, u0 + 2)
                        load_gate_up(f, 1, 1, u0 + 3)
                        load_gate_up(f, 2, 0, u0 + 4)
                        load_gate_up(f, 2, 1, u0 + 5)
                        first = 3
                    else:
                        first = 1
                    n = (NCH - first) // 2
                    with sp.Fori(0, n) as i:
                        for j in range(4):
                            load_gate_up(f, first + j // 2 + 2 * i, j % 2, u0 + 2 * first + j, i, 4)
                    for d in range(NCH):
                        load_rows(a[ffn_w[f][2]], u0 + 2 * NCH + d, 2 * d, 2, 0, DM)
                    continue
                b = int(ph[1])
                w_in = a[("w_in", "w_in_2")[b]]
                for j in range(PROJ):
                    for hf in range(2):
                        if proj_at[b][j] is None:
                            load_narrow(u0 + 2 * j + hf, hf)
                        else:
                            load_rows(w_in, u0 + 2 * j + hf, 4 * hf, 4, proj_at[b][j], NB)
                for s in range(2):
                    for n in range(2):
                        load_rows(a[branch_w[b][s]], u0 + 20 + 2 * s + n, 0, 4, n * NB, NB)
                for n in range(2):
                    for hf in range(2):
                        load_rows(a[out_w[b]], u0 + 24 + 2 * n + hf, 4 * hf, 4, n * NB, NB)
            for q, (tt, n) in enumerate(Q_FFN):
                sp.wait_ge(gained, 4 * 7 + q + 1)
                sp.dma_start(out[0, tt * P:(tt + 1) * P, n * NB:(n + 1) * NB],
                             x[:, tt, n * NB:(n + 1) * NB]).then_inc(stored, 16)
            sp.wait_ge(stored, 16 * 4)

        @block.gpsimd
        def _(pool):
            pool.dma_start(const[:, P:], a["consts"][:, P:]).then_inc(const_in, 16)
            for t in range(TT):
                pool.dma_start(posi[:, t:t + 1], a["positions"][0, t * P:(t + 1) * P]
                               .rearrange("(p o) -> p o", o=1)).then_inc(pos_in, 16)
            for k in range(8):
                m = nc.gpsimd.memset(freq[:, k:k + 1], INV_FREQ[k])
            m.then_inc(freq_set, 1)
            pool.dma_start(onehot, a["onehot"]).then_inc(table_in, 16)
            pool.dma_start(lgt[0:32, 0:NH], a["rel_bias_2"]).then_inc(table_in, 16)
            for m in range(1, 7):
                if m >= 2:
                    pool.wait_ge(gain_in, 16 * (m - 1))
                    pool.wait_ge(gained, 4 * (5 if m == 5 else m - 1))
                pool.dma_start(gain[m % 2][:], a[gains[m]].partition_broadcast(P)).then_inc(gain_in, 16)
                if m == 1:
                    pool.wait_ge(vrow_sb, 1)
                    pool.dma_start(bias_rows, lag_rows.rearrange("h (o c) -> h o c", o=1).to_broadcast([NH, P, SC]))\
                        .then_inc(vrow_out, 16)
                    pool.wait_ge(unit_used, BASE["F0"] + FFN_UNITS)
                    for g in range(4):
                        if g >= 2:
                            pool.wait_ge(evac_dve, 2 * (g - 1))
                        pool.dma_start(b_row[g % 2][:], a["b_gate"][g * NB:(g + 1) * NB].partition_broadcast(P))\
                            .then_inc(b_row_in[g % 2], 16)
                if m == 5:
                    pool.wait_ge(unit_used, BASE["F2"] + FFN_UNITS)
                    skew = bass.AP(bias_rows.tensor, P - 1, [[SC - 1, P], [P * SC, NH], [1, SEQ]])
                    pool.wait_ge(vrow_out, 16)
                    pool.dma_start(toep[:], skew).then_inc(mix_in, 16)
                    for k, name in enumerate(("fox_q_norm_2", "fox_k_norm_2", "dsa_q_norm_2", "dsa_k_norm_2")):
                        for r in range(2):
                            pool.dma_start(hg[r * HD:(r + 1) * HD, k:k + 1],
                                           a[name].rearrange("(d o) -> d o", o=1)).then_inc(mix_in, 16)
                    pool.dma_start(bfor, a["b_forget_2"].partition_broadcast(P)).then_inc(mix_in, 16)

        MIX_IN = 16 * 10

        @block.scalar
        def _(act):
            chain = [0]

            def link(ins):
                chain[0] += 1
                ins.then_inc(act_chain, 1)
                act.wait_ge(act_chain, chain[0])

            def split_hi(u, i=0, k=0):
                n = 4 * NW if u in (NARROW, NARROW + 1) else UNIT
                act.wait_ge(raw_in[u % SLOTS], landed(u) + 16 * DMAS * (k // SLOTS) * i)
                if u >= SLOTS:
                    act.wait_ge(unit_used, u + k * i - SLOTS + 1)
                act.activation(w_hi[u % SLOTS][:, 0:n], raw[u % SLOTS][:, 0:n], ACT.Copy).then_inc(hi_done, 1)

            def turned_hi(ph, qs):
                for q in qs:
                    tt, n = quarters(ph)[q]
                    act.wait_ge(x_turned, 4 * PREP_OF[ph] + q + 1)
                    act.activation(xT_hi[:, 4 * n:4 * n + 4, tt * P:(tt + 1) * P],
                                   bank[turn_banks(ph)[q]][:].rearrange("p (k t) -> p k t", k=4),
                                   ACT.Copy).then_inc(xT_hi_done, 1)

            def square(g, after):
                for tt in range(TT):
                    act.wait_ge(gained, after[tt])
                    if 2 * g + tt > 0:
                        act.wait_ge(squared, 2 * g + tt)
                    act.activation(gate[:, 0, 0:DM], x[:, tt, :], ACT.Square,
                                   accum_out=ss[:, 2 * g + tt:2 * g + tt + 1]).then_inc(squared, 1)

            def squares(ph):
                g = GAIN_OF[ph]
                if ph == "F2":
                    square(3, (14, 16))
                    square(4, (18, 20))
                elif quarters(ph) == Q_MIX:
                    square(g, (4 * g + 3, 4 * g + 4))
                else:
                    square(g, (4 * g + 2, 4 * g + 4))

            def silu(ph, c, i=0):
                for tt in range(TT):
                    if tt == 0:
                        act.wait_ge(tile_done, TILES[ph] + c + 2 * i + 1)
                    else:
                        act.wait_ge(unit_used, BASE[ph] + 2 * c + 2 + 4 * i)
                    g = GAIN_OF[ph]
                    act.activation(gsil[tt], bank[2 * (c % 2) + tt][:, 0:CH], ACT.Silu,
                                   scale=rstd[:, 2 * g + tt:2 * g + tt + 1]).then_inc(silu_done, 1)

            def hidden_hi(ph, c, i=0):
                act.wait_ge(h_turned, NCH * FFN_OF[ph] + c + 2 * i + 1)
                act.activation(hT_hi[:, bass.ds(2 * c + 4 * i, 2), :],
                               bank[6 + c % 2][:].rearrange("p (k t) -> p k t", k=2), ACT.Copy).then_inc(hT_hi_done, 1)

            def ffn(ph):
                u0 = BASE[ph]
                if ph == "F0":
                    split_hi(u0)
                    turned_hi(ph, (0, 1))
                    split_hi(u0 + 1)
                    turned_hi(ph, (2, 3))
                else:
                    turned_hi(ph, range(4))
                split_hi(u0 + 2)
                squares(ph)
                split_hi(u0 + 3)
                act.wait_ge(rstd_done, GAIN_OF[ph] + 1)
                with act.Fori(0, (NCH - 1) // 2) as i:
                    for j in range(2):
                        silu(ph, j, i)
                        split_hi(u0 + 4 + 2 * j, i, 4)
                        hidden_hi(ph, j, i)
                        split_hi(u0 + 5 + 2 * j, i, 4)
                for s in range(NCH, NCH + 6):
                    us = next_units(ph, s)
                    if s == NCH:
                        silu(ph, NCH - 1)
                    for u in us[:1]:
                        split_hi(u)
                    if s == NCH:
                        hidden_hi(ph, NCH - 1)
                    for u in us[1:]:
                        split_hi(u)
                    if ph == "F0" and s == NCH + 1:
                        act.wait_ge(vrow_mm, 1)
                        act.activation(lag_rows, bank[1][0:NH, 0:SC], ACT.Copy).then_inc(vrow_sb, 1)
                    if ph == "F0" and s == NCH + 2:
                        act.wait_ge(ang_done, 1)
                        act.activation(sinr, sinr, ACT.Sin).then_inc(sin_done, 1)
                        act.activation(cosr, cosr, ACT.Sin).then_inc(sin_done, 1)

            def mixer(b):
                ph = ("M0", "M1")[b]
                g = GAIN_OF[ph]
                turned_hi(ph, range(4))
                squares(ph)

                def r(tt):
                    return rstd[:, 2 * g + tt:2 * g + tt + 1]

                def evac(j):
                    def mv(dst, src, last=False):
                        ins = act.activation(dst, src, ACT.Copy, scale=r(tt))
                        if last:
                            ins.then_inc(evac_act, 1)

                    if j == 0:
                        act.wait_ge(rstd_done, g + 1)
                    for tt in range(TT):
                        src = bank[2 * (j % 2) + tt]
                        wait_chunk(act, ph, j, tt)
                        if b == 0:
                            if j in (2, 5):
                                mv((v_a, v_b)[j // 3][:, tt, :], src[:], True)
                            else:
                                c0 = HW * (j % 3)
                                mv(xg[:, tt, c0:c0 + HW], src[:], True)
                        elif j == 1:
                            mv(lgf[:, 8 * tt:8 * tt + 8], src[:, 0:8])
                            mv(xg[:, tt, 512:576], src[:, 8:72])
                            mv(dv[:, tt, :], src[:, 72:136])
                            mv(xg[:, tt, 640:704], src[:, 136:200])
                            mv(xg[:, tt, 704:768], src[:, 136:200])
                            mv(ifw[:, 8 * tt:8 * tt + 8], src[:, 200:208], True)
                        elif j == 4:
                            mv(v_a[:, tt, :], src[:], True)
                        else:
                            c0 = {0: 0, 2: 0, 3: 512, 5: 0}[j]
                            mv(xg[:, tt, c0:c0 + HW], src[:], True)

                def gate_rows(j):
                    for tt in range(TT):
                        wait_chunk(act, ph, j, tt)
                        act.activation(gate[:, tt, (j - 6) * NB:(j - 5) * NB], bank[2 * (j % 2) + tt][:], ACT.Copy,
                                       scale=r(tt)).then_inc(gated, 1)

                def turn(it):
                    name, tt = it.what if it.kind == "TR" else ("cu", 0)
                    act.wait_ge(scored, it.i + 1)
                    S = bank[4 + it.i % 2]
                    t = slice(tt * P, (tt + 1) * P)
                    full = S[:].rearrange("p (k t) -> p k t", k=4)
                    if name == "cu":
                        ins = act.activation(ncum[:], S[0:NH, 0:SEQ], ACT.Copy, scale=-1.0)
                    elif name == "kk":
                        act.activation(dkT[:, t], S[:, 0:P], ACT.Copy, scale=hg[:, 3:4])
                        ins = act.activation(ikT[:, t], S[:, P:2 * P], ACT.Copy)
                    else:
                        dst = {"qa": qT_a, "ka": kT_a, "qb": qT_b, "kb": kT_b, "iq": None,
                               "fq": qT_a, "fk": kT_a, "dq": qT_b}[name]
                        dst = y[1][:].rearrange("p t (k n) -> p (t k) n", k=2) if name == "iq" else dst[:]
                        scale = {"qa": HD ** -0.5, "qb": HD ** -0.5, "ka": 1.0, "kb": 1.0, "iq": 1.0,
                                 "fq": hg[:, 0:1], "fk": hg[:, 1:2], "dq": hg[:, 2:3]}[name]
                        ins = act.activation(dst[:, :, t], full, ACT.Copy, scale=scale)
                    ins.then_inc(read_a, 1)

                def exps(it):
                    act.wait_ge(maxed, it.softs + 1)
                    if it.m >= 2:
                        act.wait_ge(head_out if HEADS[it.m - 2].kind == "SB" else turned, it.m - 1)
                    k = 2 * (it.m % 8)
                    s, e = score[it.m % 2], prob[it.m % 2]
                    act.activation(e[:, 0:P], s[:, 0:P], ACT.Exp, bias=rowmax[:, k:k + 1],
                                   accum_out=rowsum[:, k:k + 1])
                    act.activation(e[:, P:SC], s[:, P:SC], ACT.Exp, bias=rowmax[:, k + 1:k + 2],
                                   accum_out=rowsum[:, k + 1:k + 2]).then_inc(exped, 1)

                def copy_turned(it):
                    act.wait_ge(turned, it.m + 1)
                    if it.m >= 2:
                        act.wait_ge(head_out, it.m - 1)
                    act.activation(probT[it.m % 2][:], head_bank(it)[:, 0:SC], ACT.Copy).then_inc(copied, 1)

                def sb_softplus(it):
                    act.wait_ge(clamped, it.sbs + 1)
                    t = soft[it.m % 2]
                    link(act.activation(t[:], t[:], ACT.Exp))
                    act.activation(t[:], t[:], ACT.Ln, bias=1.0).then_inc(softplus, 1)

                def sb_weights(it):
                    act.wait_ge(weighed, it.sbs + 1)
                    e = prob[it.m % 2]
                    act.activation(e[:], e[:], ACT.Exp).then_inc(w_done, 1)

                def relu(it):
                    act.wait_ge(scored, it.i + 1)
                    if it.ix >= 2:
                        act.wait_ge(indexed, it.ix - 1)
                    act.activation(soft[it.ix % 2][:], bank[4 + it.i % 2][:, 0:SC], ACT.Relu,
                                   scale=HD ** -0.5).then_inc(read_a, 1)

                def y_turned(it):
                    br, tt = it.what
                    act.wait_ge(scored, it.i + 1)
                    if br == 0:
                        act.wait_ge(unit_used, BASE[ph] + 2 * PROJ)
                    act.activation(xT_hi[:, 4 * br:4 * br + 4, tt * P:(tt + 1) * P],
                                   bank[4 + it.i % 2][:].rearrange("p (k t) -> p k t", k=4),
                                   ACT.Copy).then_inc(y_hi, 1)

                for slot in range(LAST_SLOT):
                    j, q = divmod(slot, 4)
                    if q in (0, 2):
                        for u in next_units(ph, j)[q // 2:q // 2 + 1]:
                            split_hi(u)
                    for it in ITEMS[b]:
                        if it.kind == "TY" and slot - it.slot == 1:
                            y_turned(it)
                    if q == 0 and 1 <= j <= 6:
                        evac(j - 1)
                    if b == 1 and q == 0 and 7 <= j <= 10:
                        gate_rows(j - 1)
                    if b == 1 and slot == 9:
                        act.wait_ge(logf, 1)
                        link(act.activation(lgt, lgt, ACT.Exp, scale=-1.0))
                        act.activation(lgt, lgt, ACT.Ln, bias=1.0).then_inc(lnf, 1)
                    for it in ITEMS[b]:
                        d = slot - it.slot
                        if it.kind in ("TR", "CU") and d == 1:
                            turn(it)
                        if it.kind == "IX" and d == 1:
                            relu(it)
                        if it.kind == "SM" and d == SM_AT["turn"]:
                            copy_turned(it)
                        if it.kind == "SM" and d == SM_AT["soft"]:
                            exps(it)
                        if it.kind == "SB" and d == SB_AT["weigh"]:
                            sb_weights(it)
                        if it.kind == "SB" and d == SB_AT["clamp"]:
                            sb_softplus(it)
                    if slot == 42:
                        act.wait_ge(gated if b == 1 else evac_dve, 8)
                        for br in range(2):
                            act.activation(gate[:, :, br * DM:(br + 1) * DM], gate[:, :, br * DM:(br + 1) * DM],
                                           ACT.Sigmoid).then_inc(sigmoid, 1)
                late_units = next_units(ph, 12)
                for q, (tt, n) in enumerate(Q_MIX):
                    act.wait_ge(m_turned, 4 * b + q + 1)
                    act.activation(xT_hi[:, 4 * n:4 * n + 4, tt * P:(tt + 1) * P],
                                   bank[4 + q][:].rearrange("p (k t) -> p k t", k=4), ACT.Copy).then_inc(mT_hi, 1)
                    if tt == 1:
                        split_hi(late_units[n])
                for u in next_units(ph, 13):
                    split_hi(u)

            act.dma_start(gain[0][:, 0:NB], a[gains[0]][0:NB].partition_broadcast(P)).then_inc(x_in[0], 16)
            act.dma_start(ident, a["consts"][:, 0:P]).then_inc(ident_in, 16)
            act.dma_start(gain[0][:, NB:], a[gains[0]][NB:].partition_broadcast(P)).then_inc(x_in[1], 16)
            ffn("F0")
            mixer(0)
            ffn("F1")
            ffn("F2")
            mixer(1)
            ffn("F3")

        @block.vector
        def _(dve):
            chain = [0]

            def link(ins):
                chain[0] += 1
                ins.then_inc(dve_chain, 1)
                dve.wait_ge(dve_chain, chain[0])

            def split_lo(u, i=0, k=0):
                n = 4 * NW if u in (NARROW, NARROW + 1) else UNIT
                dve.wait_ge(hi_done, u + k * i + 1)
                s = u % SLOTS
                dve.tensor_tensor(w_lo[s][:, 0:n], raw[s][:, 0:n], w_hi[s][:, 0:n], ALU.subtract).then_inc(lo_done, 1)

            def rsqrt(dst, src, n, mean):
                v, t, y0 = nv[:, 0:n], nt[:, 0:n], nyi[:, 0:n]
                link(dve.tensor_scalar(v, src, mean, EPS, ALU.mult, ALU.add))
                link(dve.tensor_scalar(y0, v.bitcast(I32), 1, None, ALU.logical_shift_right))
                dve.tensor_scalar(v, v, -0.5, None, ALU.mult)
                link(dve.tensor_scalar(y0, y0, -1.0, float(0x5F3759DF), ALU.mult, ALU.add))
                y0 = y0.bitcast(F32)
                for k in range(3):
                    y1 = dst if k == 2 else ny[:, 0:n]
                    link(dve.tensor_tensor(t, y0, y0, ALU.mult))
                    link(dve.tensor_tensor(t, t, v, ALU.mult))
                    ins = dve.scalar_tensor_tensor(y1, t, 1.5, y0, ALU.add, ALU.mult)
                    if k < 2:
                        link(ins)
                    y0 = y1
                return ins

            def residual(ph, q):
                prev = PREV.get(ph)
                g = 3 if ph == "F2" else GAIN_OF[ph]
                tt, n = quarters(ph)[q]
                c = slice(n * NB, (n + 1) * NB)
                if prev:
                    wait_quarter(dve, prev, q)
                    link(dve.scalar_tensor_tensor(x[:, tt, c], acc_bank(prev, tt, n)[:],
                                                  1.0 if prev[0] == "M" else 0.5, x[:, tt, c], ALU.mult, ALU.add))
                w = gain_zf if ph == "F2" else gain[g % 2][:]
                dve.tensor_tensor(xg[:, tt, c], x[:, tt, c], w[:, c], ALU.mult).then_inc(gained, 1)

            def turned_lo(ph, q):
                tt, n = quarters(ph)[q]
                dve.wait_ge(xT_hi_done, 4 * PREP_OF[ph] + q + 1)
                t = slice(tt * P, (tt + 1) * P)
                dve.tensor_tensor(xT_lo[:, 4 * n:4 * n + 4, t],
                                  bank[turn_banks(ph)[q]][:].rearrange("p (k t) -> p k t", k=4),
                                  xT_hi[:, 4 * n:4 * n + 4, t], ALU.subtract).then_inc(xT_lo_done, 1)

            def seam(ph):
                g = GAIN_OF[ph]
                if g:
                    dve.wait_ge(gain_in, 16 * g)
                if ph == "F2":
                    link(dve.tensor_tensor(gain_zf, gain[1][:], gain[0][:], ALU.mult))
                if ph == "F0":
                    for h in range(2):
                        dve.wait_ge(x_in[h], 16 * 3)
                        residual(ph, 2 * h)
                        residual(ph, 2 * h + 1)
                        split_lo(h)
                        turned_lo(ph, 2 * h)
                        turned_lo(ph, 2 * h + 1)
                    return
                order = ("r0", "r1", "r2", "l0", "l1", "r3", "l2", "l3") if quarters(ph) == Q_MIX else \
                        ("r0", "r1", "l0", "r2", "l1", "r3", "l2", "l3")
                for what in order:
                    (residual if what[0] == "r" else turned_lo)(ph, int(what[1]))

            def rms(g):
                dve.wait_ge(squared, 2 * (g + 1))
                rsqrt(rstd[:, 2 * g:2 * g + 2], ss[:, 2 * g:2 * g + 2], 2, 1.0 / DM).then_inc(rstd_done, 1)
                dve.wait_ge(rstd_done, g + 1)

            def two_norms():
                r3, r4 = rstd[:, 6:8], rstd[:, 8:10]
                for tt in range(TT):
                    dve.wait_ge(squared, 6 + tt + 1)
                    dve.tensor_tensor(x[:, tt, :], x[:, tt, :], gain[1][:], ALU.mult).then_inc(gained, 2)
                rms(3)
                dve.wait_ge(squared, 10)
                link(dve.tensor_tensor(ss[:, 8:10], ss[:, 8:10], r3, ALU.mult))
                link(dve.tensor_tensor(ss[:, 8:10], ss[:, 8:10], r3, ALU.mult))
                link(rsqrt(r4, ss[:, 8:10], 2, 1.0 / DM))
                dve.tensor_tensor(r4, r4, r3, ALU.mult).then_inc(rstd_done, 1)
                dve.wait_ge(rstd_done, 5)

            def scale_x():
                for tt in range(TT):
                    ins = dve.tensor_scalar(x[:, tt, :], x[:, tt, :], rstd[:, 6 + tt:7 + tt], None, ALU.mult)
                link(ins)

            def hidden(ph, c, i=0):
                g = GAIN_OF[ph]
                for tt in range(TT):
                    dve.wait_ge(silu_done, 2 * NCH * FFN_OF[ph] + 2 * c + tt + 1 + 4 * i)
                    dve.scalar_tensor_tensor(hs[c % 2][tt], bank[2 * (c % 2) + tt][:, CH:2 * CH],
                                             rstd[:, 2 * g + tt:2 * g + tt + 1], gsil[tt],
                                             ALU.mult, ALU.mult).then_inc(h_done, 1)

            def hidden_lo(ph, c, i=0):
                dve.wait_ge(hT_hi_done, NCH * FFN_OF[ph] + c + 2 * i + 1)
                k = bass.ds(2 * c + 4 * i, 2)
                dve.tensor_tensor(hT_lo[:, k, :], bank[6 + c % 2][:].rearrange("p (k t) -> p k t", k=2),
                                  hT_hi[:, k, :], ALU.subtract).then_inc(hT_lo_done, 1)

            def ffn(ph):
                u0 = BASE[ph]
                seam(ph)
                split_lo(u0 + 2)
                if ph == "F2":
                    two_norms()
                else:
                    rms(GAIN_OF[ph])
                split_lo(u0 + 3)
                with dve.Fori(0, (NCH - 1) // 2) as i:
                    for j in range(2):
                        hidden(ph, j, i)
                        split_lo(u0 + 4 + 2 * j, i, 4)
                        hidden_lo(ph, j, i)
                        split_lo(u0 + 5 + 2 * j, i, 4)
                for s in range(NCH, NCH + 6):
                    us = next_units(ph, s)
                    if s == NCH:
                        hidden(ph, NCH - 1)
                    for u in us[:1]:
                        split_lo(u)
                    if s == NCH:
                        hidden_lo(ph, NCH - 1)
                    for u in us[1:]:
                        split_lo(u)
                    if ph == "F0" and s == NCH + 1:
                        angles()
                    if ph == "F2" and s == NCH + 1:
                        scale_x()

            def angles():
                dve.wait_ge(pos_in, 32)
                dve.wait_ge(freq_set, 1)
                link(dve.tensor_copy(posf, posi[:]))
                for tt in range(TT):
                    ins = dve.tensor_scalar(sinr[:, 8 * tt:8 * tt + 8], freq, posf[:, tt:tt + 1], None, ALU.mult)
                link(ins)
                link(dve.tensor_scalar(ki[:], sinr, 0.15915494309189535, None, ALU.mult))
                link(dve.tensor_copy(cosr, ki[:]))
                for part in (-6.28125, -0.0019350051879882812, -3.0199159819567953e-07):
                    link(dve.scalar_tensor_tensor(sinr, cosr, part, sinr, ALU.mult, ALU.add))
                link(dve.tensor_scalar(sinr, sinr, 3.1415925, -3.1415925, ALU.min, ALU.max))
                link(dve.scalar_tensor_tensor(cosr, sinr, -1.0, sinr, ALU.mult, ALU.max))
                dve.tensor_scalar(cosr, cosr, -1.0, 1.5707963267948966, ALU.mult, ALU.add).then_inc(ang_done, 1)

            def head_norm(src, dst, n):
                tmp = gate[:, :, 3 * NB:3 * NB + n * HD]
                link(dve.tensor_tensor(tmp, src, src, ALU.mult))
                v = hss[:, 0:TT * n].rearrange("p (t h) -> p t h", t=TT)
                link(dve.tensor_reduce(v, tmp.rearrange("p t (h d) -> p t h d", d=HD), AX_X, ALU.add))
                link(rsqrt(hss[:, 0:TT * n], hss[:, 0:TT * n], TT * n, 1.0 / HD))
                for tt in range(TT):
                    ins = dve.tensor_tensor(dst[:, tt, :].rearrange("p (h d) -> p h d", d=HD),
                                            src[:, tt, :].rearrange("p (h d) -> p h d", d=HD),
                                            hss[:, tt * n:(tt + 1) * n].rearrange("p (h o) -> p h o", o=1)
                                            .to_broadcast([P, n, HD]), ALU.mult)
                return ins

            def mixer(b):
                ph = ("M0", "M1")[b]
                g = GAIN_OF[ph]
                seam(ph)
                rms(g)
                dve.wait_ge(const_in, 16)

                def rotate():
                    dve.wait_ge(evac_act, 4)
                    dve.wait_ge(sin_done, 2)
                    v = xg[:].rearrange("p t (h d) -> p t h d", d=HD)
                    tmp = y[1][:].rearrange("p t (k h d) -> p t k h d", k=4, d=8)
                    for tt in range(TT):
                        x1, x2 = v[:, tt, :, 0:8], v[:, tt, :, 8:16]
                        c = cosr[:, 8 * tt:8 * tt + 8].rearrange("p (o d) -> p o d", o=1).to_broadcast([P, 2 * NH, 8])
                        s = sinr[:, 8 * tt:8 * tt + 8].rearrange("p (o d) -> p o d", o=1).to_broadcast([P, 2 * NH, 8])
                        t = [tmp[:, tt, k] for k in range(4)]
                        dve.tensor_tensor(t[0], x1, c, ALU.mult)
                        dve.tensor_tensor(t[1], x2, s, ALU.mult)
                        dve.tensor_tensor(t[2], x2, c, ALU.mult)
                        link(dve.tensor_tensor(t[3], x1, s, ALU.mult))
                        dve.tensor_tensor(x1, t[0], t[1], ALU.subtract)
                        dve.tensor_tensor(x2, t[2], t[3], ALU.add).then_inc(rows_ready, 1)

                def norm_rows(c0, evacs):
                    dve.wait_ge(evac_act, evacs)
                    v = xg[:, :, c0:c0 + HW]
                    head_norm(v, v, NH).then_inc(rows_ready, 1)

                def narrow():
                    dve.wait_ge(evac_act, 16)
                    dve.wait_ge(mix_in, MIX_IN)
                    v = xg[:, :, 512:576]
                    link(head_norm(v, v, 1))
                    dve.tensor_copy(xg[:, :, 576:640], v).then_inc(rows_ready, 1)
                    dve.tensor_scalar(ifw, ifw, NH ** -0.5, None, ALU.mult)
                    for tt in range(TT):
                        ins = dve.tensor_tensor(lgf[:, 8 * tt:8 * tt + 8], lgf[:, 8 * tt:8 * tt + 8], bfor, ALU.add)
                    link(ins)
                    dve.scalar_tensor_tensor(lgt, lgf, -1.0, lgf, ALU.mult, ALU.max).then_inc(logf, 1)
                    dve.tensor_scalar(hg[:, 0:1], hg[:, 0:1], HD ** -0.5, None, ALU.mult)
                    link(dve.tensor_scalar(hg[:, 2:3], hg[:, 2:3], HD ** -0.5, None, ALU.mult))

                def log_f():
                    dve.wait_ge(lnf, 1)
                    dve.scalar_tensor_tensor(lgf, lgf, 0.0, lgt, ALU.min, ALU.subtract).then_inc(rows_ready, 1)

                def gate_rows(j):
                    for tt in range(TT):
                        wait_chunk(dve, ph, j, tt)
                        if tt == 0:
                            dve.wait_ge(b_row_in[j % 2], 16 * ((j - 6) // 2 + 1))
                        dve.scalar_tensor_tensor(gate[:, tt, (j - 6) * NB:(j - 5) * NB], bank[2 * (j % 2) + tt][:],
                                                 rstd[:, 2 * g + tt:2 * g + tt + 1], b_row[j % 2][:],
                                                 ALU.mult, ALU.add).then_inc(evac_dve, 1)

                def soften(it):
                    dve.wait_ge(scored, it.i + 1)
                    if it.softs >= 2:
                        dve.wait_ge(exped, it.softs - 1)
                    S, s = bank[4 + it.i % 2], score[it.m % 2]
                    kind, h = it.what
                    ins = dve.tensor_tensor(s[:], S[:, 0:SC], sel[:] if kind == "dsa" else causal, ALU.add)
                    ins.then_inc(read_d, 1)
                    dve.wait_ge(read_d, it.read)
                    if kind == "dsa":
                        dve.tensor_tensor(s[:, 0:P], s[:, 0:P], toep[:, h, P:2 * P], ALU.add)
                        link(dve.tensor_tensor(s[:, P:SC], s[:, P:SC], toep[:, h, :], ALU.add))
                    k = 2 * (it.m % 8)
                    dve.tensor_reduce(rowmax[:, k:k + 1], s[:, 0:P], AX_X, ALU.max)
                    link(dve.tensor_reduce(rowmax[:, k + 1:k + 2], s[:, P:SC], AX_X, ALU.max))
                    dve.tensor_scalar(rowmax[:, k:k + 2], rowmax[:, k:k + 2], -1.0, None, ALU.mult).then_inc(maxed, 1)

                def finish_head(it):
                    br = 0 if it.what[0] in ("moba", "fox") else 1
                    h = it.what[1]
                    O = head_bank(it)[:, SC:NB]
                    c = slice(h * HD, (h + 1) * HD)
                    if it.kind == "SM":
                        k = 2 * (it.m % 8)
                        dve.wait_ge(exped, it.softs + 1)
                        link(dve.reciprocal(rowinv[:, k:k + 2], rowsum[:, k:k + 2]))
                        dve.wait_ge(head_out, it.m + 1)
                        dve.tensor_scalar(y[br][:, 0, c], O[:, 0:HD], rowinv[:, k:k + 1], None, ALU.mult)
                        dve.tensor_scalar(y[br][:, 1, c], O[:, HD:P], rowinv[:, k + 1:k + 2], None, ALU.mult)\
                            .then_inc(head_read, 1)
                    else:
                        dve.wait_ge(head_out, it.m + 1)
                        dve.tensor_copy(y[br][:, :, c], O.rearrange("p (t d) -> p t d", t=TT)).then_inc(head_read, 1)

                def sb_clamp(it):
                    dve.wait_ge(scored, it.i + 1)
                    if HEADS[it.m - 2].kind == "SM":
                        dve.wait_ge(exped, HEADS[it.m - 2].softs + 1)
                    else:
                        dve.wait_ge(weighed, it.sbs - 1)
                    s = score[it.m % 2]
                    dve.tensor_tensor(s[:], bank[4 + it.i % 2][:, 0:SC], past, ALU.add).then_inc(read_d, 1)
                    dve.wait_ge(read_d, it.read)
                    dve.tensor_scalar(soft[it.m % 2][:], s[:], 30.0, None, ALU.min).then_inc(clamped, 1)

                def sb_keep(it):
                    dve.wait_ge(softplus, it.sbs + 1)
                    t = soft[it.m % 2]
                    dve.tensor_tensor(t[:], score[it.m % 2][:], t[:], ALU.max).then_inc(kept, 1)

                def sb_weigh(it):
                    dve.wait_ge(turned, it.m + 1)
                    dve.wait_ge(head_out, it.m - 1)
                    dve.tensor_tensor(prob[it.m % 2][:], score[it.m % 2][:], head_bank(it)[:, 0:SC], ALU.subtract)\
                        .then_inc(weighed, 1)

                def accumulate(it):
                    h = it.what
                    dve.wait_ge(read_a, it.read)
                    for tt, c in ((0, slice(0, P)), (1, slice(P, SC))):
                        wt = ifw[:, 8 * tt + h:8 * tt + h + 1]
                        src = soft[it.ix % 2][:, c]
                        if h == 0:
                            ins = dve.tensor_scalar(index[:, c], src, wt, None, ALU.mult)
                        else:
                            ins = dve.scalar_tensor_tensor(index[:, c], src, wt, index[:, c], ALU.mult, ALU.add)
                    ins.then_inc(indexed, 1)
                    dve.wait_ge(indexed, it.ix + 1)
                    if h == NH - 1:
                        link(dve.tensor_tensor(index, index, causal, ALU.add))

                def top_round(k):
                    for tt, c in ((0, slice(0, P)), (1, slice(P, SC))):
                        src = index if k == 0 else work
                        ins = dve.max(m8[:, 8 * tt:8 * tt + 8], src[:, c])
                    link(ins)
                    if k < TOPK // 8 - 1:
                        for tt, c in ((0, slice(0, P)), (1, slice(P, SC))):
                            ins = dve.match_replace(work[:, c], m8[:, 8 * tt:8 * tt + 8], src[:, c], -3e38)
                        link(ins)

                def select():
                    for tt, c in ((0, slice(0, P)), (1, slice(P, SC))):
                        thr = m8[:, 8 * tt + 7:8 * tt + 8]
                        n = ngt[:, tt:tt + 1]
                        link(dve.tensor_scalar(sel[:, c], index[:, c], thr, None, ALU.is_gt, ALU.add, accum_out=n))
                        link(dve.tensor_scalar(n, n, -1.0, float(TOPK), ALU.mult, ALU.add))
                        eq, cs = soft[0][:, c], soft[1][:, c]
                        link(dve.tensor_scalar(eq, index[:, c], thr, None, ALU.is_equal))
                        link(dve.tensor_tensor_scan(cs, eq, eq, 0.0, ALU.add, ALU.max))
                        link(dve.scalar_tensor_tensor(cs, cs, n, eq, ALU.is_le, ALU.mult))
                        link(dve.tensor_tensor(sel[:, c], sel[:, c], cs, ALU.add))
                        link(dve.tensor_scalar(sel[:, c], sel[:, c], -1.0, -NEG, ALU.add, ALU.mult))
                        link(dve.tensor_tensor(sel[:, c], sel[:, c], causal[:, c], ALU.add))

                def y_turned(it):
                    br, tt = it.what
                    dve.wait_ge(y_hi, 4 * b + 2 * br + tt + 1)
                    t = slice(tt * P, (tt + 1) * P)
                    k = slice(4 * br, 4 * br + 4)
                    dve.tensor_tensor(xT_lo[:, k, t], bank[4 + it.i % 2][:].rearrange("p (k t) -> p k t", k=4),
                                      xT_hi[:, k, t], ALU.subtract).then_inc(read_d, 1)

                def merge(br, qs=range(4)):
                    for q in qs:
                        tt, n = Q_MIX[q]
                        if tt == 0:
                            dve.wait_ge(tile_done, TILES[ph] + PROJ + 2 * br + n + 1)
                        else:
                            dve.wait_ge(unit_used, BASE[ph] + 20 + 2 * br + n + 1)
                        if q == 0:
                            dve.wait_ge(sigmoid, 2 * b + br + 1)
                        c = slice(n * NB, (n + 1) * NB)
                        gt = gate[:, tt, br * DM + n * NB:br * DM + (n + 1) * NB]
                        dst = xg[:, tt, c] if br == 0 else gt
                        ins = dve.tensor_tensor(dst, gt, bank[2 * n + tt][:], ALU.mult)
                        if br == 1:
                            link(ins)
                            ins = dve.tensor_tensor(xg[:, tt, c], xg[:, tt, c], gt, ALU.add)
                        ins.then_inc(merged, 1)

                rounds = {21 + k: k for k in range(TOPK // 8)}
                for slot in range(LAST_SLOT):
                    j, q = divmod(slot, 4)
                    if b == 0 and slot == 9:
                        rotate()
                    if b == 0 and q == 0 and 7 <= j <= 10:
                        gate_rows(j - 1)
                    if b == 1:
                        if slot == 9:
                            narrow()
                        if slot == 10:
                            log_f()
                        if slot == 13:
                            norm_rows(0, 18)
                        if slot == 17:
                            norm_rows(512, 20)
                        if slot == 25:
                            norm_rows(0, 24)
                    for it in ITEMS[b]:
                        d = slot - it.slot
                        if (it.kind == "SM" and d == SM_AT["norm"]) or (it.kind == "SB" and d == SB_AT["norm"]):
                            finish_head(it)
                        if it.kind == "SB" and d == SB_AT["weigh"]:
                            sb_weigh(it)
                        if it.kind == "SB" and d == SB_AT["keep"]:
                            sb_keep(it)
                        if it.kind == "SB" and d == SB_AT["clamp"]:
                            sb_clamp(it)
                        if it.kind == "SM" and d == SM_AT["soft"]:
                            soften(it)
                        if it.kind == "IX" and d == 2:
                            accumulate(it)
                        if it.kind == "TY" and d == 1:
                            y_turned(it)
                    if b == 1 and slot in rounds:
                        top_round(rounds[slot])
                    if b == 1 and slot == 28:
                        select()
                    if q in (0, 2):
                        for u in next_units(ph, j)[q // 2:q // 2 + 1]:
                            split_lo(u)
                    if slot == 45:
                        merge(0)
                def merged_lo(q):
                    tt, n = Q_MIX[q]
                    dve.wait_ge(mT_hi, 4 * b + q + 1)
                    t = slice(tt * P, (tt + 1) * P)
                    dve.tensor_tensor(xT_lo[:, 4 * n:4 * n + 4, t],
                                      bank[4 + q][:].rearrange("p (k t) -> p k t", k=4),
                                      xT_hi[:, 4 * n:4 * n + 4, t], ALU.subtract).then_inc(mT_lo, 1)

                late_units = next_units(ph, 12)
                merge(1, (0, 1))
                merged_lo(0)
                merged_lo(1)
                merge(1, (2, 3))
                split_lo(late_units[0])
                merged_lo(2)
                merged_lo(3)
                split_lo(late_units[1])
                for u in next_units(ph, 13):
                    split_lo(u)

            ffn("F0")
            mixer(0)
            ffn("F1")
            ffn("F2")
            mixer(1)
            ffn("F3")
            for q, (tt, n) in enumerate(Q_FFN):
                c = slice(n * NB, (n + 1) * NB)
                wait_quarter(dve, "F3", q)
                dve.scalar_tensor_tensor(x[:, tt, c], acc_bank("F3", tt, n)[:], 0.5, x[:, tt, c],
                                         ALU.mult, ALU.add).then_inc(gained, 1)

        @block.tensor
        def _(pe):
            def three(dst, st, hi, lo, mhi, mlo, start, stop):
                pe.matmul(dst, st(hi), mhi, start=start, stop=False)
                pe.matmul(dst, st(hi), mlo, start=False, stop=False)
                return pe.matmul(dst, st(lo), mhi, start=False, stop=stop)

            def rows(u, width, k4, col=0, n=NB):
                o = k4 * width + col
                return w_hi[u % SLOTS][:, o:o + n], w_lo[u % SLOTS][:, o:o + n]

            def four(u, tt, dst, k0, first, last, n=NB):
                for k4 in range(4):
                    mh, ml = rows(u, n, k4, 0, n)
                    m = three(dst, lambda z, k=k0 + k4: z[:, k, tt * P:(tt + 1) * P], xT_hi, xT_lo, mh, ml,
                              first and k4 == 0, last and k4 == 3)
                return m

            def turn_x(ph, q):
                tt, n = quarters(ph)[q]
                pe.wait_ge(gained, 4 * (3 if ph == "F2" else GAIN_OF[ph]) + q + 1)
                for k in range(4):
                    ins = pe.transpose(bank[turn_banks(ph)[q]][:, k * P:(k + 1) * P],
                                       xg[:, tt, n * NB + k * P:n * NB + (k + 1) * P], ident)
                ins.then_inc(x_turned, 1)

            def begin(ph, batch):
                if ph == "F0":
                    for hf in range(2):
                        turn_x(ph, 2 * hf)
                        turn_x(ph, 2 * hf + 1)
                        batch(0, hf)
                        batch(1, hf)
                    return
                turn_x(ph, EARLY[ph])
                batch(0, 0)
                for q in range(EARLY[ph] + 1, 4):
                    turn_x(ph, q)
                batch(0, 1)
                batch(1, 0)
                batch(1, 1)

            def chunk_tile(ph, c, hf, tt, i=0):
                m = four(BASE[ph] + 2 * c + hf, tt, bank[2 * (c % 2) + tt][:], 4 * hf, hf == 0, hf == 1)
                if tt == 1:
                    m.then_inc(unit_used, 1)
                elif hf == 1:
                    m.then_inc(tile_done, 1)

            def first_chunk(ph, tt, hf):
                pe.wait_ge(lo_done, BASE[ph] + hf + 1)
                pe.wait_ge(xT_lo_done, 4 * PREP_OF[ph] + quarters(ph).index((tt, hf)) + 1)
                chunk_tile(ph, 0, hf, tt)

            def chunk(ph, c, hf, i=0):
                pe.wait_ge(lo_done, BASE[ph] + 2 * c + hf + 1 + 4 * i)
                for tt in range(TT):
                    chunk_tile(ph, c, hf, tt, i)

            def turn_hidden(ph, c, i=0):
                for tt in range(TT):
                    pe.wait_ge(h_done, 2 * NCH * FFN_OF[ph] + 2 * c + tt + 1 + 4 * i)
                    for k in range(2):
                        ins = pe.transpose(bank[6 + c % 2][:, k * SEQ + tt * P:k * SEQ + (tt + 1) * P],
                                           hs[c % 2][tt][:, k * P:(k + 1) * P], ident)
                ins.then_inc(h_turned, 1)

            def ffn(ph):
                begin(ph, lambda tt, hf: first_chunk(ph, tt, hf))
                with pe.Fori(0, (NCH - 1) // 2) as i:
                    for j in range(2):
                        chunk(ph, 1 + j, 0, i)
                        turn_hidden(ph, j, i)
                        chunk(ph, 1 + j, 1, i)
                for d in range(NCH):
                    u = BASE[ph] + 2 * NCH + d
                    pe.wait_ge(lo_done, u + 1)
                    pe.wait_ge(hT_lo_done, NCH * FFN_OF[ph] + d + 1)
                    for q, (tt, n) in enumerate(Q_FFN):
                        if d == NCH - 1 and q == 3 and ph in NEXT:
                            turn_x(NEXT[ph], 0)
                        for k in range(2):
                            mh, ml = rows(u, DM, k, n * NB)
                            m = three(acc_bank(ph, tt, n)[:], lambda z: z[:, 2 * d + k, tt * P:(tt + 1) * P],
                                      hT_hi, hT_lo, mh, ml, d == 0 and k == 0, d == NCH - 1 and k == 1)
                        if d == NCH - 1 and q < 3:
                            m.then_inc(tile_done, 1)
                    m.then_inc(unit_used, 1)
                    if d == 0:
                        turn_hidden(ph, NCH - 1)
                    if ph == "F0" and d == 1:
                        pe.wait_ge(table_in, 32)
                        pe.matmul(bank[1][0:NH, 0:SC], lgt[0:32, 0:NH], onehot, start=True, stop=True)\
                            .then_inc(vrow_mm, 1)

            def mixer(b):
                ph = ("M0", "M1")[b]
                u0 = BASE[ph]
                if b == 0:
                    pe.wait_ge(const_in, 16)
                    pe.wait_ge(vrow_sb, 1)

                def score_bank(it):
                    if it.i >= 2:
                        was = FLAT[it.i - 2]
                        pe.wait_ge(read_sem(was), was.read)
                    return bank[4 + it.i % 2]

                def read_sem(was):
                    return read_d if was.reader == "d" else read_a

                def turn(it):
                    name, tt = it.what if it.kind == "TR" else ("cu", 0)
                    if b == 0:
                        if name in ("qa", "ka"):
                            pe.wait_ge(rows_ready, 2)
                        else:
                            pe.wait_ge(evac_act, {"qb": 8, "kb": 10}[name])
                    elif name == "iq":
                        pe.wait_ge(evac_act, 14)
                    else:
                        if name == "kk":
                            pe.wait_ge(evac_act, 16)
                        pe.wait_ge(rows_ready, {"kk": 3, "cu": 4, "fq": 5, "fk": 6, "dq": 7}[name])
                    S = score_bank(it)
                    if name == "cu":
                        pe.matmul(S[0:NH, 0:P], lgf[:, 0:8], tri_le, start=True, stop=True)
                        pe.matmul(S[0:NH, P:SEQ], lgf[:, 0:8], ones, start=True, stop=False)
                        pe.matmul(S[0:NH, P:SEQ], lgf[:, 8:16], tri_le, start=False, stop=True).then_inc(scored, 1)
                        return
                    c0 = {"qa": 0, "ka": 512, "qb": 0, "kb": 512, "iq": 0, "kk": 512, "fq": 0, "fk": 512, "dq": 0}[name]
                    n = 2 if name == "kk" else 4
                    for k in range(n):
                        ins = pe.transpose(S[:, k * P:(k + 1) * P], xg[:, tt, c0 + k * P:c0 + (k + 1) * P], ident)
                    ins.then_inc(scored, 1)

                def operands(it):
                    kind, h = it.what if it.kind != "IX" else ("idx", it.what)
                    r = slice(HD * (h % 2), HD * (h % 2) + HD)
                    c = slice(h * HD, (h + 1) * HD)
                    iqT = y[1][:].rearrange("p t (k n) -> p (t k) n", k=2)
                    if kind in ("moba", "fox"):
                        return qT_a[r, h // 2, :], kT_a[r, h // 2, :], v_a[:, :, c]
                    if kind == "sb":
                        return qT_b[r, h // 2, :], kT_b[r, h // 2, :], v_b[:, :, c]
                    if kind == "dsa":
                        return qT_b[r, h // 2, :], dkT[r, :], dv[:]
                    return iqT[r, h // 2, :], ikT[r, :], None

                def scores(it):
                    kind, h = it.what if it.kind != "IX" else ("idx", it.what)
                    need = {"moba": "ka", "fox": "fk", "sb": "kb", "dsa": "dq", "idx": "kk"}[kind]
                    pe.wait_ge(read_a, max(t.read for t in ITEMS[b] if t.kind in ("TR", "CU") and
                                           (t.what[:1] or ("cu",))[0] in ((need, "cu") if kind == "fox" else (need,))))
                    S = score_bank(it)
                    q, k, _ = operands(it)
                    if kind == "fox":
                        pick = const[0:NH, C_ID + h:C_ID + h + 1].to_broadcast([NH, P])
                        pe.matmul(S[:, 0:P], q[:, 0:P], k[:, 0:P], start=True, stop=False)
                        pe.matmul(S[:, 0:P], pick, ncum[:, 0:P], start=False, stop=True)
                        pe.matmul(S[:, P:SC], q[:, P:SEQ], k, start=True, stop=False)
                        pe.matmul(S[:, P:SC], pick, ncum[:], start=False, stop=True).then_inc(scored, 1)
                    elif kind == "sb":
                        pe.matmul(S[:, 0:SEQ], k[:, 0:P], q, start=True, stop=True)
                        pe.matmul(S[:, SEQ:SC], k[:, P:SEQ], q[:, P:SEQ], start=True, stop=True).then_inc(scored, 1)
                    else:
                        pe.matmul(S[:, 0:P], q[:, 0:P], k[:, 0:P], start=True, stop=True)
                        pe.matmul(S[:, P:SC], q[:, P:SEQ], k, start=True, stop=True).then_inc(scored, 1)

                def turn_free(it):
                    if it.m >= 2:
                        pe.wait_ge(head_read, it.m - 1)
                    return head_bank(it)

                def turn_probs(it):
                    pe.wait_ge(exped, it.softs + 1)
                    B = turn_free(it)
                    for k in range(3):
                        ins = pe.transpose(B[:, k * P:(k + 1) * P], prob[it.m % 2][:, k * P:(k + 1) * P], ident)
                    ins.then_inc(turned, 1)

                def sb_sum(it):
                    pe.wait_ge(kept, it.sbs + 1)
                    B = turn_free(it)
                    t = soft[it.m % 2]
                    pe.matmul(B[:, 0:P], tri_ge, t[:, 0:P], start=True, stop=True)
                    pe.matmul(B[:, P:SEQ], tri_ge, t[:, P:SEQ], start=True, stop=False)
                    pe.matmul(B[:, P:SEQ], ones, t[:, SEQ:SC], start=False, stop=True)
                    pe.matmul(B[:, SEQ:SC], tri_ge, t[:, SEQ:SC], start=True, stop=True).then_inc(turned, 1)

                def head(it):
                    if it.kind == "SM":
                        pe.wait_ge(copied, it.softs + 1)
                        w = probT[it.m % 2]
                    else:
                        pe.wait_ge(w_done, it.sbs + 1)
                        w = prob[it.m % 2]
                    _, _, v = operands(it)
                    O = head_bank(it)[:, SC:NB]
                    pe.matmul(O[:, 0:HD], w[:, 0:P], v[:, 0, :], start=True, stop=True)
                    pe.matmul(O[:, HD:P], w[:, P:SEQ], v[:, 0, :], start=True, stop=False)
                    pe.matmul(O[:, HD:P], w[:, SEQ:SC], v[:, 1, :], start=False, stop=True).then_inc(head_out, 1)

                def y_turn(it):
                    br, tt = it.what
                    last = max(t.m for t in HEADS if t.b == b and (t.what[0] in ("moba", "fox")) == (br == 0))
                    pe.wait_ge(head_read, last + 1)
                    S = score_bank(it)
                    for k in range(4):
                        ins = pe.transpose(S[:, k * P:(k + 1) * P], y[br][:, tt, k * P:(k + 1) * P], ident)
                    ins.then_inc(scored, 1)

                def project(j, hf, tt):
                    u = u0 + 2 * j + hf
                    pe.wait_ge(lo_done, u + 1)
                    n = NB if proj_at[b][j] is not None else NW
                    if j == 0:
                        pe.wait_ge(xT_lo_done, 4 * PREP_OF[ph] + quarters(ph).index((tt, hf)) + 1)
                    if j >= 2 and hf == 0 and tt == 0:
                        if j - 2 < 6:
                            pe.wait_ge(evac_act, 12 * b + 2 * (j - 1))
                        elif b == 0:
                            pe.wait_ge(evac_dve, 2 * (j - 7))
                        else:
                            pe.wait_ge(gated, 2 * (j - 7))
                    m = four(u, tt, bank[2 * (j % 2) + tt][:, 0:n], 4 * hf, hf == 0, hf == 1, n)
                    if tt == 1:
                        m.then_inc(unit_used, 1)
                    elif hf == 1:
                        m.then_inc(tile_done, 1)

                def branch(br, q):
                    n, tt = divmod(q, 2)
                    u = u0 + 20 + 2 * br + n
                    pe.wait_ge(lo_done, u + 1)
                    ty = [t for t in ITEMS[b] if t.kind == "TY" and t.what == (br, tt)][0]
                    pe.wait_ge(read_d, ty.read)
                    if br == 0:
                        pe.wait_ge(gated if b else evac_dve, 8)
                    else:
                        pe.wait_ge(merged, 8 * b + q + 1)
                    m = four(u, tt, bank[2 * n + tt][:], 4 * br, True, True)
                    m.then_inc(unit_used if tt else tile_done, 1)

                begin(ph, lambda tt, hf: project(0, hf, tt))
                for slot in range(4, LAST_SLOT):
                    j, q = divmod(slot, 4)
                    if j < PROJ:
                        project(j, q // 2, q % 2)
                    elif slot < 44:
                        branch(0, q)
                    for it in ITEMS[b]:
                        d = slot - it.slot
                        if (it.kind == "SM" and d == SM_AT["out"]) or (it.kind == "SB" and d == SB_AT["out"]):
                            head(it)
                        if it.kind == "SB" and d == SB_AT["sum"]:
                            sb_sum(it)
                        if it.kind == "SM" and d == SM_AT["turn"]:
                            turn_probs(it)
                        if it.kind in ("TR", "CU") and d == 0:
                            turn(it)
                        if it.kind in ("SM", "SB", "IX") and d == 0:
                            scores(it)
                        if it.kind == "TY" and d == 0:
                            y_turn(it)
                def turn_merged(q):
                    tt, n = Q_MIX[q]
                    pe.wait_ge(merged, 8 * b + 4 + q + 1)
                    for k in range(4):
                        ins = pe.transpose(bank[4 + q][:, k * P:(k + 1) * P],
                                           xg[:, tt, n * NB + k * P:n * NB + (k + 1) * P], ident)
                    ins.then_inc(m_turned, 1)

                def output(n, hf, tt):
                    u = u0 + 24 + 2 * n + hf
                    pe.wait_ge(lo_done, u + 1)
                    pe.wait_ge(mT_lo, 4 * b + Q_MIX.index((tt, hf)) + 1)
                    m = four(u, tt, bank[2 * n + tt][:], 4 * hf, hf == 0, hf == 1)
                    if tt == 1:
                        m.then_inc(unit_used, 1)
                    elif hf == 1:
                        m.then_inc(tile_done, 1)

                for q in range(3):
                    branch(1, q)
                turn_merged(0)
                turn_merged(1)
                branch(1, 3)
                output(0, 0, 0)
                turn_merged(2)
                turn_merged(3)
                output(0, 0, 1)
                for n, hf in ((0, 1), (1, 0), (1, 1)):
                    output(n, hf, 0)
                    if (n, hf) == (1, 1):
                        turn_x(NEXT[ph], 0)
                        turn_x(NEXT[ph], 1)
                    output(n, hf, 1)

            pe.wait_ge(ident_in, 16)
            for ph in PHASES:
                if ph[0] == "F":
                    ffn(ph)
                else:
                    mixer(int(ph[1]))


def lag_buckets(n_buckets, max_distance, lags):
    import numpy as np
    exact = n_buckets // 2
    rel = np.maximum(lags, 1).astype(np.float32)
    large = exact + (np.log(rel / np.float32(exact)) / np.float32(np.log(max_distance / exact))
                     * np.float32(n_buckets - exact)).astype(np.int32)
    return np.where(lags < exact, lags, np.minimum(large, n_buckets - 1))


def constants():
    import numpy as np
    c = np.zeros((P, C_END), np.float32)
    p, f = np.arange(P)[:, None], np.arange(P)[None, :]
    c[:, C_ID:C_ID + P] = p == f
    c[:, C_CAUSAL:C_CAUSAL + P] = c[:, C_CAUSAL + 2 * P:C_CAUSAL + 3 * P] = np.where(f <= p, 0, NEG)
    c[:, C_PAST:C_PAST + P] = c[:, C_PAST + 2 * P:C_PAST + 3 * P] = np.where(p < f, 0, NEG)
    c[:, C_GE:C_GE + P] = p >= f
    c[:, C_ONE:C_ONE + P] = 1
    c[:, C_LE:C_LE + P] = p <= f
    bucket = lag_buckets(32, 128, np.maximum(SEQ - 1 - np.arange(SC), 0))
    onehot = (np.arange(32)[:, None] == bucket[None, :]).astype(np.float32)
    return c, onehot


def kernel(**inputs):
    import numpy as np
    import concourse.bacc as bacc
    from concourse.bass_utils import run_bass_kernel_spmd

    nc = bacc.Bacc("TRN2", target_bir_lowering=False, num_devices=1)
    arrays, aps = {}, {}
    consts, onehot = constants()
    shape_only = {"consts": consts, "onehot": onehot}
    for name, v in {**inputs, **shape_only}.items():
        v = np.ascontiguousarray(v)
        if v.ndim > 1 and v.shape[0] == 1 and name not in ("x", "positions"):
            v = v[0]
        arrays["in_" + name] = v
        aps[name] = nc.dram_tensor("in_" + name, v.shape, mybir.dt.from_np(v.dtype), kind="ExternalInput").ap()
    o = nc.dram_tensor("result", (1, SEQ, DM), F32, kind="ExternalOutput").ap()
    build(nc, aps, o)
    r = run_bass_kernel_spmd(nc, [arrays], core_ids=[0])
    return r.results[0]["result"]
```

```python
from contextlib import ExitStack

import concourse.bass as bass
from concourse import mybir

F32 = mybir.dt.float32
F32R = mybir.dt.float32r
I32 = mybir.dt.int32
ALU = mybir.AluOpType
ACT = mybir.ActivationFunctionType
AX_X = mybir.AxisListType.X

P = 128
SEQ = 256
DM = 1024
FF = 2816
HD = 64
NH = 8
HW = NH * HD
KC = DM // P
TT = SEQ // P
NB = 512
CH = 256
NCH = FF // CH
EPS = 1e-6
NEG = -1e30
TOPK = min(256, SEQ // 4)
SC = 384

SLOTS = 4
UNIT = 2048
DMAS = 2

FFN_UNITS = 2 * NCH + NCH
PROJ = 10
MIX_UNITS = 2 * PROJ + 4 + 4
BASE = {}
_n = 0
for _ph, _k in (("F0", FFN_UNITS), ("M0", MIX_UNITS), ("F1", FFN_UNITS),
                ("F2", FFN_UNITS), ("M1", MIX_UNITS), ("F3", FFN_UNITS)):
    BASE[_ph] = _n
    _n += _k
UNITS = _n
TILES = {"F0": 0, "M0": 14, "F1": 30, "F2": 44, "M1": 58, "F3": 74}
FFN_OF = {"F0": 0, "F1": 1, "F2": 2, "F3": 3}
PREP_OF = {"F0": 0, "M0": 1, "F1": 2, "F2": 3, "M1": 4, "F3": 5}
NARROW = BASE["M1"] + 2
NW = 208


def steps_of(phase):
    b = BASE[phase]
    if phase[0] == "F":
        s = [[b + 2 * c, b + 2 * c + 1] for c in range(NCH)]
        d = b + 2 * NCH
        return s + [[u for u in (d + i, d + i + 1) if u < d + NCH] for i in range(0, NCH, 2)]
    return [[b + 2 * j, b + 2 * j + 1] for j in range(MIX_UNITS // 2)]


PHASES = ("F0", "M0", "F1", "F2", "M1", "F3")
STEPS = [(ph, i, us) for ph in PHASES for i, us in enumerate(steps_of(ph))]


def next_units(phase, i):
    n = next(k for k, s in enumerate(STEPS) if s[:2] == (phase, i)) + 1
    return STEPS[n][2] if n < len(STEPS) else []


def landed(u):
    n = sum(DMAS + (v in (NARROW, NARROW + 1)) for v in range(u % SLOTS, u + 1, SLOTS))
    return 16 * (n - (u % SLOTS == 0))


TY_AT = (38, 43)


def items_of(b):
    if b == 0:
        out = [(11, "TR", ("qa", 0)), (11, "TR", ("qa", 1)), (12, "TR", ("ka", 0)), (12, "TR", ("ka", 1))]
        out += [(t, "SM", ("moba", h)) for h, t in enumerate((14, 15, 17, 18, 19, 21, 22, 23))]
        out += [(20, "TR", ("qb", 0)), (20, "TR", ("qb", 1)), (24, "TR", ("kb", 0)), (24, "TR", ("kb", 1))]
        out += [(t, "SB", ("sb", h)) for h, t in enumerate((25, 27, 28, 30, 31, 33, 34, 36))]
    else:
        out = [(6, "TR", ("iq", 0)), (7, "TR", ("iq", 1)), (11, "TR", ("kk", 0)), (11, "TR", ("kk", 1)),
               (13, "CU", ())]
        out += [(12 + h, "IX", h) for h in range(NH)]
        out += [(15, "TR", ("fq", 0)), (15, "TR", ("fq", 1)), (19, "TR", ("fk", 0)), (19, "TR", ("fk", 1))]
        out += [(t, "SM", ("fox", h)) for h, t in enumerate((21, 22, 23, 25, 26, 27, 28, 29))]
        out += [(29, "TR", ("dq", 0)), (30, "TR", ("dq", 1))]
        out += [(t, "SM", ("dsa", h)) for h, t in enumerate(range(32, 40))]
    out += [(TY_AT[0], "TY", (0, 0)), (TY_AT[0] + 1, "TY", (0, 1)), (TY_AT[1], "TY", (1, 0)), (TY_AT[1], "TY", (1, 1))]
    return sorted(out, key=lambda x: x[0])


class Item:
    pass


def plan():
    items, i, m, reads = {0: [], 1: []}, 0, 0, {"a": 0, "d": 0}
    ix = softs = sbs = 0
    flat = []
    for b in (0, 1):
        for slot, kind, what in items_of(b):
            it = Item()
            it.b, it.slot, it.kind, it.what, it.i, it.m = b, slot, kind, what, i, m
            it.reader = "a" if kind in ("TR", "IX") else "d"
            reads[it.reader] += 1
            it.read = reads[it.reader]
            if kind == "IX":
                it.ix = ix
                ix += 1
            if kind == "SM":
                it.softs = softs
                softs += 1
            if kind == "SB":
                it.sbs = sbs
                sbs += 1
            if kind in ("SM", "SB"):
                m += 1
            i += 1
            items[b].append(it)
            flat.append(it)
    return items, flat


ITEMS, FLAT = plan()
HEADS = [it for it in FLAT if it.kind in ("SM", "SB")]


SM_AT = dict(soft=1, turn=2, out=3, norm=4)
SB_AT = dict(clamp=1, keep=2, sum=3, weigh=4, out=5, norm=6)
LAST_SLOT = 48

INV_FREQ = [500000.0 ** (-k * 2.0 / 16) for k in range(8)]
C_ID, C_CAUSAL, C_PAST, C_ONE, C_LE, C_GE, C_ALL = 0, 128, 512, 896, 1024, 1152, 1280


def build(nc, a, out):
    ctx = ExitStack()
    with ctx:
        def sb(name, shape, dt=F32):
            return ctx.enter_context(nc.sbuf_tensor(name, shape, dt))

        def sem(name):
            return ctx.enter_context(nc.semaphore(name))

        bank = [ctx.enter_context(nc.psum_tensor(f"bank{i}", [P, NB], F32)) for i in range(8)]

        raw = [sb(f"raw{i}", [P, UNIT]) for i in range(SLOTS)]
        w_hi = [sb(f"w_hi{i}", [P, UNIT], F32R) for i in range(SLOTS)]
        w_lo = [sb(f"w_lo{i}", [P, UNIT], F32R) for i in range(SLOTS)]
        x = sb("x", [P, TT, DM])
        xg = sb("xg", [P, TT, DM])
        xT_hi = sb("xT_hi", [P, KC, SEQ], F32R)
        xT_lo = sb("xT_lo", [P, KC, SEQ], F32R)
        gain = [sb(f"gain{i}", [P, DM]) for i in range(2)]
        gate = sb("gate", [P, TT, 2 * DM])
        const = sb("const", [P, C_GE])
        small = sb("small", [P, 258])
        hid = ExitStack()
        with hid:
            hT_hi = hid.enter_context(nc.sbuf_tensor("hT_hi", [P, FF // P, SEQ], F32R))
            hT_lo = hid.enter_context(nc.sbuf_tensor("hT_lo", [P, FF // P, SEQ], F32R))
        mix = ctx.enter_context(ExitStack())

        def mb(name, shape, dt=F32):
            return mix.enter_context(nc.sbuf_tensor(name, shape, dt))

        v_a = mb("v_a", [P, TT, HW])
        y = [mb("y_a", [P, TT, HW]), mb("y_b", [P, TT, HW])]
        turned_a = ExitStack()
        with turned_a:
            yT_a_hi, yT_a_lo = (turned_a.enter_context(nc.sbuf_tensor(n, [P, HW // P, SEQ], F32R))
                                for n in ("yT_a_hi", "yT_a_lo"))
        qT_a = mb("qT_a", [P, HW // P, SEQ])
        kT_a = mb("kT_a", [P, HW // P, SEQ])
        qT_b = mb("qT_b", [P, HW // P, SEQ])
        score = [mb(f"score{i}", [P, SC]) for i in range(2)]
        prob = [mb(f"prob{i}", [P, SC]) for i in range(2)]
        split_soft = ExitStack()
        with split_soft:
            soft_hi, soft_lo = ([split_soft.enter_context(nc.sbuf_tensor(f"{n}{i}", [P, SC], F32R)) for i in range(2)]
                                for n in ("soft_hi", "soft_lo"))
        probT = [mb(f"probT{i}", [P, SC]) for i in range(2)]
        soft = [mb(f"soft{i}", [P, SC]) for i in range(2)]
        late = ExitStack()
        with late:
            kT_b = late.enter_context(nc.sbuf_tensor("kT_b", [P, HW // P, SEQ], F32))
            v_b = late.enter_context(nc.sbuf_tensor("v_b", [P, TT, HW], F32))
            tri_r = late.enter_context(nc.sbuf_tensor("tri_r", [P, 2 * P], F32R))
            b_row = [late.enter_context(nc.sbuf_tensor(f"b_row{i}", [P, NB], F32)) for i in range(2)]
        yT_hi, yT_lo = [yT_a_hi[:], xT_hi[:, 4:8, :]], [yT_a_lo[:], xT_lo[:, 4:8, :]]
        ikT = mb("ikT", [P, SEQ])
        dkT = mb("dkT", [P, SEQ])
        dv = mb("dv", [P, TT, HD])
        index, work = gate[:, 1, DM:DM + SC], gate[:, 0, DM:DM + SC]
        sel = mb("sel", [P, SC])
        toep = mb("toep", [P, NH, SEQ])
        hg = mb("hg", [P, 4])
        ncum_hi, ncum_lo, pick = (mb(n, [NH, w], F32R) for n, w in (("ncum_hi", SEQ), ("ncum_lo", SEQ), ("pick", NH)))

        at = [0]

        def cols(n):
            at[0] += n
            return small[:, at[0] - n:at[0]]

        ss = cols(14)
        rstd = cols(14)
        pool_cols = gate[:, 1, DM + SC:DM + NB].rearrange("p (k n) -> p k n", n=16)
        newton = [[cols(16) for _ in range(3)], [pool_cols[:, k, :] for k in range(3)]]
        hss, hss_p = cols(16), pool_cols[:, 3, :]
        rowmax = cols(16)
        rowsum = cols(16)
        rowinv = cols(16)
        ifw = cols(16)
        lgf = cols(16)
        lgt = cols(16)
        m8 = cols(16)
        ngt = cols(2)
        mean_sq = cols(2)
        freq = cols(8)
        cosr = cols(16)
        sinr = cols(16)
        posf = cols(2)
        bfor = cols(8)
        guess = [sb("guess", [P, 16], I32), pool_cols[:, 4, :].bitcast(I32)]
        posi = gate[:, 1, 2 * SC:2 * SC + 2].bitcast(I32)
        ki = gate[:, 1, 2 * SC + 2:2 * SC + 18].bitcast(I32)
        hs = [[gate[:, 1, DM + (2 * i + t) * CH:DM + (2 * i + t + 1) * CH] for t in range(TT)] for i in range(2)]
        gsil = [gate[:, 0, DM + t * CH:DM + (t + 1) * CH] for t in range(TT)]
        onehot = gate[0:32, 1, 0:SC]
        gain_zf = gate[:, 1, 0:DM]
        tri_ge = gate[:, 1, DM:DM + P]
        lag_rows = gate[0:NH, 1, SC:2 * SC]

        raw_in = [sem(f"raw_in{i}") for i in range(SLOTS)]
        hi_done = sem("hi_done")
        lo_done = sem("lo_done")
        unit_used = sem("unit_used")
        tile_done = sem("tile_done")
        first_half = sem("first_half")
        first_half_hi = sem("first_half_hi")
        x_in = [sem("x_in0"), sem("x_in1")]
        ident_in = sem("ident_in")
        const_in = sem("const_in")
        gain_in = sem("gain_in")
        gained = sem("gained")
        x_turned = sem("x_turned")
        xT_hi_done = sem("xT_hi_done")
        xT_lo_done = sem("xT_lo_done")
        squared = sem("squared")
        rstd_done = sem("rstd_done")
        silu_done = sem("silu_done")
        h_done = sem("h_done")
        h_turned = sem("h_turned")
        hT_hi_done = sem("hT_hi_done")
        hT_lo_done = sem("hT_lo_done")
        evac_act = sem("evac_act")
        evac_dve = sem("evac_dve")
        rows_ready = sem("rows_ready")
        dq_ready = sem("dq_ready")
        selected = sem("selected")
        bias_ready = sem("bias_ready")
        pool_chain = sem("pool_chain")
        scored = sem("scored")
        read_a = sem("read_a")
        read_d = sem("read_d")
        maxed = sem("maxed")
        exped = sem("exped")
        turned = sem("turned")
        copied = sem("copied")
        weighed = sem("weighed")
        clamped = sem("clamped")
        softplus = sem("softplus")
        kept = sem("kept")
        w_done = sem("w_done")
        head_out = sem("head_out")
        head_read = sem("head_read")
        indexed = sem("indexed")
        y_hi = sem("y_hi")
        cum_hi = sem("cum_hi")
        tri_in = sem("tri_in")
        tri_done = sem("tri_done")
        gated = sem("gated")
        sigmoid = sem("sigmoid")
        merged = sem("merged")
        m_turned = sem("m_turned")
        mT_hi = sem("mT_hi")
        mT_lo = sem("mT_lo")
        logf = sem("logf")
        lnf = sem("lnf")
        vrow_mm = sem("vrow_mm")
        vrow_sb = sem("vrow_sb")
        vrow_out = sem("vrow_out")
        table_in = sem("table_in")
        b_row_in = [sem("b_row_in0"), sem("b_row_in1")]
        pos_in = sem("pos_in")
        freq_set = sem("freq_set")
        ang_done = sem("ang_done")
        sin_done = sem("sin_done")
        mix_in = sem("mix_in")
        dve_chain = sem("dve_chain")
        act_chain = sem("act_chain")
        stored = sem("stored")

        ident = const[:, C_ID:C_ID + P]
        causal = const[:, C_CAUSAL:C_CAUSAL + SC]
        past = const[:, C_PAST:C_PAST + SC]
        ones = const[:, C_ONE:C_ONE + P]
        tri_le = const[:, C_LE:C_LE + P]

        bias_rows = nc.dram_tensor("bias_rows", [NH, P, SC], F32).ap()

        ffn_w = [("ffn1_w_gate", "ffn1_w_up", "ffn1_w_down"), ("ffn2_w_gate", "ffn2_w_up", "ffn2_w_down"),
                 ("ffn1_w_gate_2", "ffn1_w_up_2", "ffn1_w_down_2"),
                 ("ffn2_w_gate_2", "ffn2_w_up_2", "ffn2_w_down_2")]
        branch_w = [("w_branch_moba", "w_branch_sb"), ("w_branch_a_2", "w_branch_b_2")]
        out_w = ["w_out", "w_out_2"]
        proj_at = [[512 * j for j in range(PROJ)],
                   [2184, None, 0, 512, 1024, 1544, 2768, 3280, 3792, 4304]]
        gains = ["ffn1_norm", "mix_norm", "ffn2_norm", "final_norm",
                 "ffn1_norm_2", "mix_norm_2", "ffn2_norm_2"]
        GAIN_OF = {"F0": 0, "M0": 1, "F1": 2, "Z": 3, "F2": 4, "M1": 5, "F3": 6}
        Q_FFN = [(0, 0), (0, 1), (1, 0), (1, 1)]
        Q_MIX = [(0, 0), (1, 0), (0, 1), (1, 1)]
        PREV = dict(zip(PHASES[1:], PHASES))
        NEXT = dict(zip(PHASES, PHASES[1:]))
        EARLY = {"M0": 1, "F1": 2, "F2": 1, "M1": 1, "F3": 2}

        def quarters(ph):
            return Q_MIX if ph in ("F0", "F1", "F3") else Q_FFN

        def turn_banks(ph):
            return [4, 5, 6, 7] if ph in ("F0", "F1", "F3") else [0, 1, 6, 7]

        def acc_bank(ph, tt, n):
            return bank[2 + 2 * tt + n] if ph[0] == "F" else bank[2 * n + tt]

        def wait_quarter(eng, ph, q):
            if ph[0] == "F":
                if q < 3:
                    eng.wait_ge(tile_done, TILES[ph] + NCH + q + 1)
                else:
                    eng.wait_ge(unit_used, BASE[ph] + FFN_UNITS)
            elif q % 2 == 0:
                eng.wait_ge(tile_done, TILES[ph] + PROJ + 4 + q // 2 + 1)
            else:
                eng.wait_ge(unit_used, BASE[ph] + MIX_UNITS - 2 + 2 * (q // 2))

        def wait_chunk(eng, ph, j, tt):
            if tt == 0:
                eng.wait_ge(tile_done, TILES[ph] + j + 1)
            else:
                eng.wait_ge(unit_used, BASE[ph] + 2 * j + 2)

        def gate_half(t):
            return t[:].rearrange("p (k n) -> p k n", k=4)[:, :, 0:CH]

        def up_half(t):
            return t[:].rearrange("p (k n) -> p k n", k=4)[:, :, CH:2 * CH]

        def head_bank(it):
            return bank[6 + it.m % 2]

        def rsqrt(eng, link, who, dst, src, n, mean):
            v, y, t = (z[:, 0:n] for z in newton[who])
            y0 = guess[who][:, 0:n]
            link(eng.tensor_scalar(v, src, mean, EPS, ALU.mult, ALU.add))
            link(eng.tensor_scalar(y0, v.bitcast(I32), -0.5, float(0x5F3759DF), ALU.mult, ALU.add))
            link(eng.tensor_scalar(v, v, -0.5, None, ALU.mult))
            y0 = y0.bitcast(F32)
            for k in range(3):
                y1 = dst if k == 2 else y
                link(eng.tensor_tensor(t, y0, y0, ALU.mult))
                link(eng.tensor_tensor(t, t, v, ALU.mult))
                if who == 0:
                    ins = eng.scalar_tensor_tensor(y1, t, 1.5, y0, ALU.add, ALU.mult)
                else:
                    link(eng.tensor_scalar(t, t, 1.5, None, ALU.add))
                    ins = eng.tensor_tensor(y1, t, y0, ALU.mult)
                if k < 2:
                    link(ins)
                y0 = y1
            return ins

        def head_norm(eng, link, who, src, dst, n):
            sums = (hss, hss_p)[who]
            tmp = gate[:, :, 3 * NB:3 * NB + n * HD]
            link(eng.tensor_tensor(tmp, src, src, ALU.mult))
            v = sums[:, 0:TT * n].rearrange("p (t h) -> p t h", t=TT)
            if who == 0:
                link(eng.tensor_reduce(v, tmp.rearrange("p t (h d) -> p t h d", d=HD), AX_X, ALU.add))
            else:
                w, rows4 = HD, tmp.rearrange("p t (h d) -> p t h d", d=HD)
                while w > 1:
                    w //= 2
                    dst4 = rows4[:, :, :, 0:w] if w > 1 else \
                        hss_p[:, 0:TT * n].rearrange("p (t h d) -> p t h d", t=TT, d=1)
                    link(eng.tensor_tensor(dst4, rows4[:, :, :, 0:w], rows4[:, :, :, w:2 * w], ALU.add))
            link(rsqrt(eng, link, who, sums[:, 0:TT * n], sums[:, 0:TT * n], TT * n, 1.0 / HD))
            for tt in range(TT):
                ins = eng.tensor_tensor(dst[:, tt, :].rearrange("p (h d) -> p h d", d=HD),
                                        src[:, tt, :].rearrange("p (h d) -> p h d", d=HD),
                                        sums[:, tt * n:(tt + 1) * n].rearrange("p (h o) -> p h o", o=1)
                                        .to_broadcast([P, n, HD]), ALU.mult)
            return ins

        block = ctx.enter_context(nc.Block())

        MIX_IN = 16 * 10

        @block.sync
        def _(sp):
            def load_x(n):
                c = slice(n * NB, (n + 1) * NB)
                for tt in range(TT):
                    sp.dma_start(x[:, tt, c], a["x"][0, tt * P:(tt + 1) * P, c]).then_inc(x_in[n], 16)

            def free(u, i=0, k=0):
                if u >= SLOTS:
                    sp.wait_ge(lo_done, u + k * i - SLOTS + 1)

            def put(u, dst, src, signal=None):
                sp.dma_start(dst, src).then_inc(signal or raw_in[u % SLOTS], 16)

            def load_gate_up(f, c, hf, u, i=0, k=0):
                free(u, i, k)
                slot = raw[u % SLOTS][:].rearrange("p (k n) -> p k n", k=4)
                for s in range(2):
                    w = a[ffn_w[f][s]].rearrange("(k p) (c n) -> p k c n", p=P, n=CH)
                    put(u, slot[:, :, s * CH:(s + 1) * CH], w[:, 4 * hf:4 * hf + 4, c, :],
                        first_half if u == 0 and s == 0 else None)

            def load_rows(w, u, r0, rows, c0, width):
                free(u)
                slot = raw[u % SLOTS][:, 0:rows * width].rearrange("p (k n) -> p k n", k=rows)
                w = w.rearrange("(k p) n -> p k n", p=P)
                h = rows // 2
                for s in range(2):
                    put(u, slot[:, s * h:(s + 1) * h, :], w[:, r0 + s * h:r0 + (s + 1) * h, c0:c0 + width])

            def load_narrow(u, hf):
                free(u)
                slot = raw[u % SLOTS][:, 0:4 * NW].rearrange("p (k n) -> p k n", k=4)
                w = a["w_in_2"].rearrange("(k p) n -> p k n", p=P)[:, 4 * hf:4 * hf + 4, :]
                put(u, slot[:, :, 0:8], w[:, :, 1536:1544])
                put(u, slot[:, :, 8:136], w[:, :, 2056:2184])
                put(u, slot[:, :, 136:208], w[:, :, 2696:2768])

            for ph in PHASES:
                u0 = BASE[ph]
                if ph[0] == "F":
                    f = FFN_OF[ph]
                    for c in range(1):
                        for hf in range(2):
                            if ph == "F0" and hf == 0:
                                load_x(0)
                            load_gate_up(f, c, hf, u0 + 2 * c + hf)
                            if ph == "F0" and hf == 0:
                                load_x(1)
                    if ph == "F0":
                        load_gate_up(f, 1, 0, u0 + 2)
                        load_gate_up(f, 1, 1, u0 + 3)
                        load_gate_up(f, 2, 0, u0 + 4)
                        load_gate_up(f, 2, 1, u0 + 5)
                        first = 3
                    else:
                        first = 1
                    n = (NCH - first) // 2
                    with sp.Fori(0, n) as i:
                        for j in range(4):
                            load_gate_up(f, first + j // 2 + 2 * i, j % 2, u0 + 2 * first + j, i, 4)
                    for d in range(NCH):
                        load_rows(a[ffn_w[f][2]], u0 + 2 * NCH + d, 2 * d, 2, 0, DM)
                    continue
                b = int(ph[1])
                w_in = a[("w_in", "w_in_2")[b]]
                for j in range(PROJ):
                    for hf in range(2):
                        if proj_at[b][j] is None:
                            load_narrow(u0 + 2 * j + hf, hf)
                        else:
                            load_rows(w_in, u0 + 2 * j + hf, 4 * hf, 4, proj_at[b][j], NB)
                for s in range(2):
                    for n in range(2):
                        load_rows(a[branch_w[b][s]], u0 + 20 + 2 * s + n, 0, 4, n * NB, NB)
                for n in range(2):
                    for hf in range(2):
                        load_rows(a[out_w[b]], u0 + 24 + 2 * n + hf, 4 * hf, 4, n * NB, NB)
            for q, (tt, n) in enumerate(Q_FFN):
                sp.wait_ge(gained, 4 * 7 + q + 1)
                sp.dma_start(out[0, tt * P:(tt + 1) * P, n * NB:(n + 1) * NB],
                             x[:, tt, n * NB:(n + 1) * NB]).then_inc(stored, 16)
            sp.wait_ge(stored, 16 * 4)

        @block.gpsimd
        def _(pool):
            for q, (tt, n) in enumerate(Q_MIX):
                if tt == 0:
                    pool.wait_ge(x_in[n], 16 * 3)
                c = slice(n * NB, (n + 1) * NB)
                pool.tensor_tensor(xg[:, tt, c], x[:, tt, c], gain[0][:, c], ALU.mult).then_inc(gained, 1)
            for t in range(TT):
                pool.dma_start(posi[:, t:t + 1], a["positions"][0, t * P:(t + 1) * P]
                               .rearrange("(p o) -> p o", o=1)).then_inc(pos_in, 16)
            for k in range(8):
                m = nc.gpsimd.memset(freq[:, k:k + 1], INV_FREQ[k])
            m.then_inc(freq_set, 1)
            pool.dma_start(onehot, a["onehot"]).then_inc(table_in, 16)
            pool.dma_start(lgt[0:32, 0:NH], a["rel_bias_2"]).then_inc(table_in, 16)
            pool.wait_ge(hi_done, 4)
            pool.dma_start(const[:, P:], a["consts"][:, P:C_GE]).then_inc(const_in, 16)
            for m in range(1, 7):
                if m >= 2:
                    pool.wait_ge(gain_in, 16 * (m - 1))
                    pool.wait_ge(gained, 4 * (5 if m == 5 else m - 1))
                pool.dma_start(gain[m % 2][:], a[gains[m]].partition_broadcast(P)).then_inc(gain_in, 16)
                if m == 1:
                    pool.wait_ge(vrow_sb, 1)
                    pool.dma_start(bias_rows, lag_rows.rearrange("h (o c) -> h o c", o=1).to_broadcast([NH, P, SC]))\
                        .then_inc(vrow_out, 16)
                    pool.wait_ge(unit_used, BASE["F0"] + FFN_UNITS)
                    pool.dma_start(tri_ge, a["consts"][:, C_GE:]).then_inc(tri_in, 16)
                    for g in range(4):
                        if g >= 2:
                            pool.wait_ge(evac_dve, 2 * (g - 1))
                        pool.dma_start(b_row[g % 2][:], a["b_gate"][g * NB:(g + 1) * NB].partition_broadcast(P))\
                            .then_inc(b_row_in[g % 2], 16)
                if m == 5:
                    pool.wait_ge(unit_used, BASE["F2"] + FFN_UNITS)
                    skew = bass.AP(bias_rows.tensor, P - 1, [[SC - 1, P], [P * SC, NH], [1, SEQ]])
                    pool.wait_ge(vrow_out, 16)
                    pool.dma_start(toep[:], skew).then_inc(mix_in, 16)
                    for k, name in enumerate(("fox_q_norm_2", "fox_k_norm_2", "dsa_q_norm_2", "dsa_k_norm_2")):
                        for r in range(2):
                            pool.dma_start(hg[r * HD:(r + 1) * HD, k:k + 1],
                                           a[name].rearrange("(d o) -> d o", o=1)).then_inc(mix_in, 16)
                    pool.dma_start(bfor, a["b_forget_2"].partition_broadcast(P)).then_inc(mix_in, 16)

            pool.wait_ge(evac_act, 24)
            chain = [0]

            def link(ins):
                chain[0] += 1
                ins.then_inc(pool_chain, 1)
                pool.wait_ge(pool_chain, chain[0])

            head_norm(pool, link, 1, xg[:, :, 0:HW], xg[:, :, 0:HW], NH).then_inc(dq_ready, 1)
            pool.wait_ge(selected, TT)
            dsa = [it for it in HEADS if it.b == 1 and it.what[0] == "dsa"]
            for h in range(NH):
                if h >= 2:
                    pool.wait_ge(read_d, dsa[h - 2].read)
                pool.tensor_tensor(soft[h % 2][:, 0:P], sel[:, 0:P], toep[:, h, P:2 * P], ALU.add)
                pool.tensor_tensor(soft[h % 2][:, P:SC], sel[:, P:SC], toep[:, h, :], ALU.add).then_inc(bias_ready, 1)

        @block.scalar
        def _(act):
            chain = [0]

            def link(ins):
                chain[0] += 1
                ins.then_inc(act_chain, 1)
                act.wait_ge(act_chain, chain[0])

            def split_hi(u, i=0, k=0):
                n = 4 * NW if u in (NARROW, NARROW + 1) else UNIT
                act.wait_ge(raw_in[u % SLOTS], landed(u) + 16 * DMAS * (k // SLOTS) * i)
                if u >= SLOTS:
                    act.wait_ge(unit_used, u + k * i - SLOTS + 1)
                act.activation(w_hi[u % SLOTS][:, 0:n], raw[u % SLOTS][:, 0:n], ACT.Copy).then_inc(hi_done, 1)

            def turned_hi(ph, qs):
                for q in qs:
                    tt, n = quarters(ph)[q]
                    act.wait_ge(x_turned, 4 * PREP_OF[ph] + q + 1)
                    act.activation(xT_hi[:, 4 * n:4 * n + 4, tt * P:(tt + 1) * P],
                                   bank[turn_banks(ph)[q]][:].rearrange("p (k t) -> p k t", k=4),
                                   ACT.Copy).then_inc(xT_hi_done, 1)

            def square(g, after):
                for tt in range(TT):
                    act.wait_ge(gained, after[tt])
                    if 2 * g + tt > 0:
                        act.wait_ge(squared, 2 * g + tt)
                    act.activation(gate[:, 0, 0:DM], x[:, tt, :], ACT.Square,
                                   accum_out=ss[:, 2 * g + tt:2 * g + tt + 1]).then_inc(squared, 1)

            def squares(ph):
                g = GAIN_OF[ph]
                if ph == "F2":
                    square(3, (14, 16))
                    square(4, (18, 20))
                elif quarters(ph) == Q_MIX:
                    square(g, (4 * g + 3, 4 * g + 4))
                else:
                    square(g, (4 * g + 2, 4 * g + 4))

            def silu(ph, c, i=0):
                for tt in range(TT):
                    if tt == 0:
                        act.wait_ge(tile_done, TILES[ph] + c + 2 * i + 1)
                    else:
                        act.wait_ge(unit_used, BASE[ph] + 2 * c + 2 + 4 * i)
                    g = GAIN_OF[ph]
                    act.activation(gsil[tt], bank[2 * (c % 2) + tt][:, 0:CH], ACT.Silu,
                                   scale=rstd[:, 2 * g + tt:2 * g + tt + 1]).then_inc(silu_done, 1)

            def hidden_hi(ph, c, i=0):
                act.wait_ge(h_turned, NCH * FFN_OF[ph] + c + 2 * i + 1)
                act.activation(hT_hi[:, bass.ds(2 * c + 4 * i, 2), :],
                               bank[6 + c % 2][:].rearrange("p (k t) -> p k t", k=2), ACT.Copy).then_inc(hT_hi_done, 1)

            def ffn(ph):
                u0 = BASE[ph]
                if ph == "F0":
                    act.wait_ge(first_half, 16)
                    act.activation(gate_half(w_hi[0]), gate_half(raw[0]), ACT.Copy).then_inc(first_half_hi, 1)
                    turned_hi(ph, (0, 1))
                    act.wait_ge(raw_in[0], landed(0))
                    act.activation(up_half(w_hi[0]), up_half(raw[0]), ACT.Copy).then_inc(hi_done, 1)
                    split_hi(u0 + 1)
                    turned_hi(ph, (2, 3))
                else:
                    turned_hi(ph, range(4))
                split_hi(u0 + 2)
                squares(ph)
                split_hi(u0 + 3)
                act.wait_ge(rstd_done, GAIN_OF[ph] + 1)
                with act.Fori(0, (NCH - 1) // 2) as i:
                    for j in range(2):
                        silu(ph, j, i)
                        split_hi(u0 + 4 + 2 * j, i, 4)
                        hidden_hi(ph, j, i)
                        split_hi(u0 + 5 + 2 * j, i, 4)
                for s in range(NCH, NCH + 6):
                    us = next_units(ph, s)
                    if s == NCH:
                        silu(ph, NCH - 1)
                    for u in us[:1]:
                        split_hi(u)
                    if s == NCH:
                        hidden_hi(ph, NCH - 1)
                    for u in us[1:]:
                        split_hi(u)
                    if ph == "F0" and s == NCH + 1:
                        act.wait_ge(vrow_mm, 1)
                        act.activation(lag_rows, bank[1][0:NH, 0:SC], ACT.Copy).then_inc(vrow_sb, 1)
                    if ph == "F0" and s == NCH + 2:
                        act.wait_ge(ang_done, 1)
                        act.activation(sinr, sinr, ACT.Sin).then_inc(sin_done, 1)
                        act.activation(cosr, cosr, ACT.Sin).then_inc(sin_done, 1)

            def mixer(b):
                ph = ("M0", "M1")[b]
                g = GAIN_OF[ph]
                turned_hi(ph, range(4))
                split_hi(BASE[ph] + 2)
                squares(ph)
                act.preload_act_table_set("natural_log_exp_and_others")

                def r(tt):
                    return rstd[:, 2 * g + tt:2 * g + tt + 1]

                def evac(j):
                    def mv(dst, src, last=False):
                        ins = act.activation(dst, src, ACT.Copy, scale=r(tt))
                        if last:
                            ins.then_inc(evac_act, 1)

                    if j == 0:
                        act.wait_ge(rstd_done, g + 1)
                    for tt in range(TT):
                        src = bank[2 * (j % 2) + tt]
                        wait_chunk(act, ph, j, tt)
                        if b == 0:
                            if j in (2, 5):
                                mv((v_a, v_b)[j // 3][:, tt, :], src[:], True)
                            else:
                                c0 = HW * (j % 3)
                                mv(xg[:, tt, c0:c0 + HW], src[:], True)
                        elif j == 1:
                            mv(lgf[:, 8 * tt:8 * tt + 8], src[:, 0:8])
                            mv(xg[:, tt, 512:576], src[:, 8:72])
                            mv(dv[:, tt, :], src[:, 72:136])
                            mv(xg[:, tt, 640:704], src[:, 136:200])
                            mv(xg[:, tt, 704:768], src[:, 136:200])
                            mv(ifw[:, 8 * tt:8 * tt + 8], src[:, 200:208], True)
                        elif j == 4:
                            mv(v_a[:, tt, :], src[:], True)
                        else:
                            c0 = {0: 0, 2: 0, 3: 512, 5: 0}[j]
                            mv(xg[:, tt, c0:c0 + HW], src[:], True)

                def gate_rows(j):
                    for tt in range(TT):
                        wait_chunk(act, ph, j, tt)
                        act.activation(gate[:, tt, (j - 6) * NB:(j - 5) * NB], bank[2 * (j % 2) + tt][:], ACT.Copy,
                                       scale=r(tt)).then_inc(gated, 1)

                def turn(it):
                    name, tt = it.what if it.kind == "TR" else ("cu", 0)
                    if name == "cu":
                        act.activation(pick[:], const[0:NH, C_ID:C_ID + NH], ACT.Copy)
                    act.wait_ge(scored, it.i + 1)
                    S = bank[4 + it.i % 2]
                    t = slice(tt * P, (tt + 1) * P)
                    full = S[:].rearrange("p (k t) -> p k t", k=4)
                    if name == "cu":
                        act.activation(ncum_hi[:], S[0:NH, 0:SEQ], ACT.Copy, scale=-1.0).then_inc(cum_hi, 1)
                        return
                    elif name == "kk":
                        act.activation(dkT[:, t], S[:, 0:P], ACT.Copy, scale=hg[:, 3:4])
                        ins = act.activation(ikT[:, t], S[:, P:2 * P], ACT.Copy)
                    else:
                        dst = {"qa": qT_a, "ka": kT_a, "qb": qT_b, "kb": kT_b, "iq": None,
                               "fq": qT_a, "fk": kT_a, "dq": qT_b}[name]
                        dst = y[1][:].rearrange("p t (k n) -> p (t k) n", k=2) if name == "iq" else dst[:]
                        scale = {"qa": HD ** -0.5, "qb": HD ** -0.5, "ka": 1.0, "kb": 1.0, "iq": 1.0,
                                 "fq": hg[:, 0:1], "fk": hg[:, 1:2], "dq": hg[:, 2:3]}[name]
                        ins = act.activation(dst[:, :, t], full, ACT.Copy, scale=scale)
                    ins.then_inc(read_a, 1)

                def exps(it):
                    act.wait_ge(maxed, it.softs + 1)
                    if it.m >= 2:
                        act.wait_ge(head_out if HEADS[it.m - 2].kind == "SB" else turned, it.m - 1)
                    k = 2 * (it.m % 8)
                    s, e = score[it.m % 2], prob[it.m % 2]
                    act.activation(e[:, 0:P], s[:, 0:P], ACT.Exp, bias=rowmax[:, k:k + 1],
                                   accum_out=rowsum[:, k:k + 1])
                    act.activation(e[:, P:SC], s[:, P:SC], ACT.Exp, bias=rowmax[:, k + 1:k + 2],
                                   accum_out=rowsum[:, k + 1:k + 2]).then_inc(exped, 1)

                def copy_turned(it):
                    act.wait_ge(turned, it.m + 1)
                    if it.m >= 2:
                        act.wait_ge(head_out, it.m - 1)
                    act.activation(probT[it.m % 2][:], head_bank(it)[:, 0:SC], ACT.Copy).then_inc(copied, 1)

                def sb_softplus(it):
                    act.wait_ge(clamped, it.sbs + 1)
                    t = soft[it.m % 2]
                    link(act.activation(t[:], t[:], ACT.Exp))
                    act.activation(t[:], t[:], ACT.Ln, bias=1.0).then_inc(softplus, 1)

                def sb_weights(it):
                    act.wait_ge(weighed, it.sbs + 1)
                    e = prob[it.m % 2]
                    act.activation(e[:], e[:], ACT.Exp).then_inc(w_done, 1)

                def relu(it):
                    act.wait_ge(scored, it.i + 1)
                    if it.ix >= 2:
                        act.wait_ge(indexed, it.ix - 1)
                    act.activation(soft[it.ix % 2][:], bank[4 + it.i % 2][:, 0:SC], ACT.Relu,
                                   scale=HD ** -0.5).then_inc(read_a, 1)

                def y_turned(it):
                    br, tt = it.what
                    act.wait_ge(scored, it.i + 1)
                    if br == 1:
                        act.wait_ge(unit_used, BASE[ph] + 2 * PROJ)
                    act.activation(yT_hi[br][:, :, tt * P:(tt + 1) * P],
                                   bank[4 + it.i % 2][:].rearrange("p (k t) -> p k t", k=4),
                                   ACT.Copy).then_inc(y_hi, 1)

                for slot in range(LAST_SLOT):
                    j, q = divmod(slot, 4)
                    for it in ITEMS[b]:
                        if it.kind == "TY" and slot - it.slot == 1:
                            y_turned(it)
                    if q in (0, 2) and slot > 0:
                        for u in next_units(ph, j)[q // 2:q // 2 + 1]:
                            split_hi(u)
                    if q == 0 and 1 <= j <= 6:
                        evac(j - 1)
                    if b == 1 and q == 0 and 7 <= j <= 10:
                        gate_rows(j - 1)
                    if b == 1 and slot == 11:
                        act.wait_ge(logf, 1)
                        link(act.activation(lgt, lgt, ACT.Exp, scale=-1.0))
                        act.activation(lgt, lgt, ACT.Ln, bias=1.0).then_inc(lnf, 1)
                    if b == 0 and slot == 13:
                        act.wait_ge(tri_in, 16)
                        act.activation(tri_r[:, P:2 * P], ones, ACT.Copy)
                        act.activation(tri_r[:, 0:P], tri_ge, ACT.Copy).then_inc(tri_done, 1)
                    for it in ITEMS[b]:
                        if slot - it.slot == 1 and it.kind in ("TR", "CU"):
                            turn(it)
                        if slot - it.slot == 1 and it.kind == "IX":
                            relu(it)
                    for it in ITEMS[b]:
                        d = slot - it.slot
                        if it.kind == "SM" and d == SM_AT["turn"]:
                            copy_turned(it)
                        if it.kind == "SM" and d == SM_AT["soft"]:
                            exps(it)
                        if it.kind == "SB" and d == SB_AT["weigh"]:
                            sb_weights(it)
                        if it.kind == "SB" and d == SB_AT["clamp"]:
                            sb_softplus(it)
                    if slot in (41, 42, 44, 45):
                        if slot == 41:
                            act.wait_ge(gated if b == 1 else evac_dve, 8)
                        g_rows = gate[:, (slot - 1) % 2 if slot < 44 else slot % 2, (slot // 44) * DM:(slot // 44 + 1) * DM]
                        act.activation(g_rows, g_rows, ACT.Sigmoid).then_inc(sigmoid, 1)
                    if slot == 40:
                        act.preload_act_table_set("sigmoid_and_others")
                    if slot == 45:
                        act.preload_act_table_set("silu_and_others")
                for q, (tt, n) in enumerate(Q_MIX):
                    act.wait_ge(m_turned, 4 * b + q + 1)
                    act.activation(xT_hi[:, 4 * n:4 * n + 4, tt * P:(tt + 1) * P],
                                   bank[4 + q][:].rearrange("p (k t) -> p k t", k=4), ACT.Copy).then_inc(mT_hi, 1)
                    if tt == 1:
                        split_hi(next_units(ph, 12)[n])
                for u in next_units(ph, 13):
                    split_hi(u)

            act.preload_act_table_set("silu_and_others")
            act.dma_start(gain[0][:, 0:NB], a[gains[0]][0:NB].partition_broadcast(P)).then_inc(x_in[0], 16)
            act.dma_start(ident, a["consts"][:, 0:P]).then_inc(ident_in, 16)
            act.dma_start(gain[0][:, NB:], a[gains[0]][NB:].partition_broadcast(P)).then_inc(x_in[1], 16)
            ffn("F0")
            mixer(0)
            ffn("F1")
            ffn("F2")
            mixer(1)
            ffn("F3")

        @block.vector
        def _(dve):
            chain = [0]

            def link(ins):
                chain[0] += 1
                ins.then_inc(dve_chain, 1)
                dve.wait_ge(dve_chain, chain[0])

            def split_lo(u, i=0, k=0):
                n = 4 * NW if u in (NARROW, NARROW + 1) else UNIT
                dve.wait_ge(hi_done, u + k * i + 1)
                s = u % SLOTS
                dve.tensor_tensor(w_lo[s][:, 0:n], raw[s][:, 0:n], w_hi[s][:, 0:n], ALU.subtract).then_inc(lo_done, 1)

            def residual(ph, q):
                prev = PREV.get(ph)
                g = 3 if ph == "F2" else GAIN_OF[ph]
                tt, n = quarters(ph)[q]
                c = slice(n * NB, (n + 1) * NB)
                if prev:
                    wait_quarter(dve, prev, q)
                    link(dve.scalar_tensor_tensor(x[:, tt, c], acc_bank(prev, tt, n)[:],
                                                  1.0 if prev[0] == "M" else 0.5, x[:, tt, c], ALU.mult, ALU.add))
                w = gain_zf if ph == "F2" else gain[g % 2][:]
                dve.tensor_tensor(xg[:, tt, c], x[:, tt, c], w[:, c], ALU.mult).then_inc(gained, 1)

            def turned_lo(ph, q):
                tt, n = quarters(ph)[q]
                dve.wait_ge(xT_hi_done, 4 * PREP_OF[ph] + q + 1)
                t = slice(tt * P, (tt + 1) * P)
                dve.tensor_tensor(xT_lo[:, 4 * n:4 * n + 4, t],
                                  bank[turn_banks(ph)[q]][:].rearrange("p (k t) -> p k t", k=4),
                                  xT_hi[:, 4 * n:4 * n + 4, t], ALU.subtract).then_inc(xT_lo_done, 1)

            def seam(ph):
                g = GAIN_OF[ph]
                if g:
                    dve.wait_ge(gain_in, 16 * g)
                if ph == "F2":
                    link(dve.tensor_tensor(gain_zf, gain[1][:], gain[0][:], ALU.mult))
                if ph == "F0":
                    for h in range(2):
                        if h == 0:
                            dve.wait_ge(first_half_hi, 1)
                            dve.tensor_tensor(gate_half(w_lo[0]), gate_half(raw[0]), gate_half(w_hi[0]), ALU.subtract)
                            turned_lo(ph, 0)
                            dve.wait_ge(hi_done, 1)
                            dve.tensor_tensor(up_half(w_lo[0]), up_half(raw[0]), up_half(w_hi[0]), ALU.subtract)\
                                .then_inc(lo_done, 1)
                            turned_lo(ph, 1)
                        else:
                            split_lo(1)
                            turned_lo(ph, 2)
                            turned_lo(ph, 3)
                    return
                order = ("r0", "r1", "r2", "l0", "l1", "r3", "l2", "l3") if quarters(ph) == Q_MIX else \
                        ("r0", "r1", "l0", "r2", "l1", "r3", "l2", "l3")
                for what in order:
                    (residual if what[0] == "r" else turned_lo)(ph, int(what[1]))

            def rms(g):
                dve.wait_ge(squared, 2 * (g + 1))
                rsqrt(dve, link, 0, rstd[:, 2 * g:2 * g + 2], ss[:, 2 * g:2 * g + 2], 2, 1.0 / DM).then_inc(rstd_done, 1)
                dve.wait_ge(rstd_done, g + 1)

            def two_norms():
                r3, r4 = rstd[:, 6:8], rstd[:, 8:10]
                for tt in range(TT):
                    dve.wait_ge(squared, 6 + tt + 1)
                    dve.tensor_tensor(x[:, tt, :], x[:, tt, :], gain[1][:], ALU.mult).then_inc(gained, 2)
                dve.wait_ge(squared, 8)
                link(dve.tensor_scalar(mean_sq, ss[:, 6:8], 1.0 / DM, EPS, ALU.mult, ALU.add))
                link(dve.reciprocal(mean_sq, mean_sq))
                dve.wait_ge(squared, 10)
                link(dve.tensor_tensor(ss[:, 8:10], ss[:, 8:10], mean_sq, ALU.mult))
                rsqrt(dve, link, 0, rstd[:, 6:10], ss[:, 6:10], 4, 1.0 / DM).then_inc(rstd_done, 1)
                dve.wait_ge(rstd_done, 4)
                dve.tensor_tensor(r4, r4, r3, ALU.mult).then_inc(rstd_done, 1)
                dve.wait_ge(rstd_done, 5)

            def scale_x():
                for tt in range(TT):
                    ins = dve.tensor_scalar(x[:, tt, :], x[:, tt, :], rstd[:, 6 + tt:7 + tt], None, ALU.mult)
                link(ins)

            def hidden(ph, c, i=0):
                g = GAIN_OF[ph]
                for tt in range(TT):
                    dve.wait_ge(silu_done, 2 * NCH * FFN_OF[ph] + 2 * c + tt + 1 + 4 * i)
                    dve.scalar_tensor_tensor(hs[c % 2][tt], bank[2 * (c % 2) + tt][:, CH:2 * CH],
                                             rstd[:, 2 * g + tt:2 * g + tt + 1], gsil[tt],
                                             ALU.mult, ALU.mult).then_inc(h_done, 1)

            def hidden_lo(ph, c, i=0):
                dve.wait_ge(hT_hi_done, NCH * FFN_OF[ph] + c + 2 * i + 1)
                k = bass.ds(2 * c + 4 * i, 2)
                dve.tensor_tensor(hT_lo[:, k, :], bank[6 + c % 2][:].rearrange("p (k t) -> p k t", k=2),
                                  hT_hi[:, k, :], ALU.subtract).then_inc(hT_lo_done, 1)

            def ffn(ph):
                u0 = BASE[ph]
                seam(ph)
                split_lo(u0 + 2)
                if ph == "F2":
                    two_norms()
                else:
                    rms(GAIN_OF[ph])
                split_lo(u0 + 3)
                with dve.Fori(0, (NCH - 1) // 2) as i:
                    for j in range(2):
                        hidden(ph, j, i)
                        split_lo(u0 + 4 + 2 * j, i, 4)
                        hidden_lo(ph, j, i)
                        split_lo(u0 + 5 + 2 * j, i, 4)
                for s in range(NCH, NCH + 6):
                    us = next_units(ph, s)
                    if s == NCH:
                        hidden(ph, NCH - 1)
                    for u in us[:1]:
                        split_lo(u)
                    if s == NCH:
                        hidden_lo(ph, NCH - 1)
                    for u in us[1:]:
                        split_lo(u)
                    if ph == "F0" and s == NCH + 1:
                        angles()
                    if ph == "F2" and s == NCH + 1:
                        scale_x()

            def angles():
                dve.wait_ge(pos_in, 32)
                dve.wait_ge(freq_set, 1)
                link(dve.tensor_copy(posf, posi))
                for tt in range(TT):
                    ins = dve.tensor_scalar(sinr[:, 8 * tt:8 * tt + 8], freq, posf[:, tt:tt + 1], None, ALU.mult)
                link(ins)
                link(dve.tensor_scalar(ki, sinr, 0.15915494309189535, None, ALU.mult))
                link(dve.tensor_copy(cosr, ki))
                for part in (-6.28125, -0.0019350051879882812, -3.0199159819567953e-07):
                    link(dve.scalar_tensor_tensor(sinr, cosr, part, sinr, ALU.mult, ALU.add))
                link(dve.tensor_scalar(sinr, sinr, 3.1415925, -3.1415925, ALU.min, ALU.max))
                link(dve.scalar_tensor_tensor(cosr, sinr, -1.0, sinr, ALU.mult, ALU.max))
                dve.tensor_scalar(cosr, cosr, -1.0, 1.5707963267948966, ALU.mult, ALU.add).then_inc(ang_done, 1)

            def mixer(b):
                ph = ("M0", "M1")[b]
                g = GAIN_OF[ph]
                u0 = BASE[ph]
                seam(ph)
                split_lo(u0 + 2)
                rms(g)
                dve.wait_ge(const_in, 16)

                def rotate():
                    dve.wait_ge(evac_act, 4)
                    dve.wait_ge(sin_done, 2)
                    v = xg[:].rearrange("p t (h d) -> p t h d", d=HD)
                    tmp = y[1][:].rearrange("p t (k h d) -> p t k h d", k=4, d=8)
                    for tt in range(TT):
                        x1, x2 = v[:, tt, :, 0:8], v[:, tt, :, 8:16]
                        c = cosr[:, 8 * tt:8 * tt + 8].rearrange("p (o d) -> p o d", o=1).to_broadcast([P, 2 * NH, 8])
                        s = sinr[:, 8 * tt:8 * tt + 8].rearrange("p (o d) -> p o d", o=1).to_broadcast([P, 2 * NH, 8])
                        t = [tmp[:, tt, k] for k in range(4)]
                        dve.tensor_tensor(t[0], x1, c, ALU.mult)
                        dve.tensor_tensor(t[1], x2, s, ALU.mult)
                        dve.tensor_tensor(t[2], x2, c, ALU.mult)
                        link(dve.tensor_tensor(t[3], x1, s, ALU.mult))
                        dve.tensor_tensor(x1, t[0], t[1], ALU.subtract)
                        dve.tensor_tensor(x2, t[2], t[3], ALU.add).then_inc(rows_ready, 1)

                def norm_rows(c0, evacs):
                    dve.wait_ge(evac_act, evacs)
                    v = xg[:, :, c0:c0 + HW]
                    head_norm(dve, link, 0, v, v, NH).then_inc(rows_ready, 1)

                def narrow():
                    dve.wait_ge(evac_act, 16)
                    dve.wait_ge(mix_in, MIX_IN)
                    v = xg[:, :, 512:576]
                    link(head_norm(dve, link, 0, v, v, 1))
                    dve.tensor_copy(xg[:, :, 576:640], v).then_inc(rows_ready, 1)
                    dve.tensor_scalar(ifw, ifw, NH ** -0.5, None, ALU.mult)
                    for tt in range(TT):
                        ins = dve.tensor_tensor(lgf[:, 8 * tt:8 * tt + 8], lgf[:, 8 * tt:8 * tt + 8], bfor, ALU.add)
                    link(ins)
                    dve.scalar_tensor_tensor(lgt, lgf, -1.0, lgf, ALU.mult, ALU.max).then_inc(logf, 1)
                    dve.tensor_scalar(hg[:, 0:1], hg[:, 0:1], HD ** -0.5, None, ALU.mult)
                    link(dve.tensor_scalar(hg[:, 2:3], hg[:, 2:3], HD ** -0.5, None, ALU.mult))

                def log_f():
                    dve.wait_ge(lnf, 1)
                    dve.scalar_tensor_tensor(lgf, lgf, 0.0, lgt, ALU.min, ALU.subtract).then_inc(rows_ready, 1)

                def gate_rows(j):
                    for tt in range(TT):
                        wait_chunk(dve, ph, j, tt)
                        if tt == 0:
                            dve.wait_ge(b_row_in[j % 2], 16 * ((j - 6) // 2 + 1))
                        dve.scalar_tensor_tensor(gate[:, tt, (j - 6) * NB:(j - 5) * NB], bank[2 * (j % 2) + tt][:],
                                                 rstd[:, 2 * g + tt:2 * g + tt + 1], b_row[j % 2][:],
                                                 ALU.mult, ALU.add).then_inc(evac_dve, 1)

                def soften(it):
                    dve.wait_ge(scored, it.i + 1)
                    if it.softs >= 2:
                        dve.wait_ge(exped, it.softs - 1)
                    S, s = bank[4 + it.i % 2], score[it.m % 2]
                    kind, h = it.what
                    if kind == "dsa":
                        dve.wait_ge(bias_ready, h + 1)
                    dve.tensor_tensor(s[:], S[:, 0:SC], soft[h % 2][:] if kind == "dsa" else causal, ALU.add)\
                        .then_inc(read_d, 1)
                    dve.wait_ge(read_d, it.read)
                    k = 2 * (it.m % 8)
                    dve.tensor_reduce(rowmax[:, k:k + 1], s[:, 0:P], AX_X, ALU.max)
                    link(dve.tensor_reduce(rowmax[:, k + 1:k + 2], s[:, P:SC], AX_X, ALU.max))
                    dve.tensor_scalar(rowmax[:, k:k + 2], rowmax[:, k:k + 2], -1.0, None, ALU.mult).then_inc(maxed, 1)

                def finish_head(it):
                    br = 0 if it.what[0] in ("moba", "fox") else 1
                    h = it.what[1]
                    O = head_bank(it)[:, SC:NB]
                    c = slice(h * HD, (h + 1) * HD)
                    if it.kind == "SM":
                        k = 2 * (it.m % 8)
                        dve.wait_ge(exped, it.softs + 1)
                        link(dve.reciprocal(rowinv[:, k:k + 2], rowsum[:, k:k + 2]))
                        dve.wait_ge(head_out, it.m + 1)
                        dve.tensor_scalar(y[br][:, 0, c], O[:, 0:HD], rowinv[:, k:k + 1], None, ALU.mult)
                        dve.tensor_scalar(y[br][:, 1, c], O[:, HD:P], rowinv[:, k + 1:k + 2], None, ALU.mult)\
                            .then_inc(head_read, 1)
                    else:
                        dve.wait_ge(head_out, it.m + 1)
                        dve.tensor_copy(y[br][:, :, c], O.rearrange("p (t d) -> p t d", t=TT)).then_inc(head_read, 1)

                def sb_clamp(it):
                    dve.wait_ge(scored, it.i + 1)
                    if HEADS[it.m - 2].kind == "SM":
                        dve.wait_ge(exped, HEADS[it.m - 2].softs + 1)
                    else:
                        dve.wait_ge(weighed, it.sbs - 1)
                    s = score[it.m % 2]
                    dve.tensor_tensor(s[:], bank[4 + it.i % 2][:, 0:SC], past, ALU.add).then_inc(read_d, 1)
                    dve.wait_ge(read_d, it.read)
                    dve.tensor_scalar(soft[it.m % 2][:], s[:], 30.0, None, ALU.min).then_inc(clamped, 1)

                def sb_keep(it):
                    dve.wait_ge(softplus, it.sbs + 1)
                    k = it.m % 2
                    t, hi, lo = soft[k], soft_hi[k], soft_lo[k]
                    link(dve.tensor_tensor(t[:], score[k][:], t[:], ALU.max))
                    dve.wait_ge(head_out if HEADS[it.m - 2].kind == "SM" else turned, it.m - 1)
                    link(dve.tensor_copy(hi[:], t[:]))
                    dve.tensor_tensor(lo[:], t[:], hi[:], ALU.subtract).then_inc(kept, 1)

                def sb_weigh(it):
                    dve.wait_ge(turned, it.m + 1)
                    dve.wait_ge(head_out, it.m - 1)
                    dve.tensor_tensor(prob[it.m % 2][:], score[it.m % 2][:], head_bank(it)[:, 0:SC], ALU.subtract)\
                        .then_inc(weighed, 1)

                def accumulate(it):
                    h = it.what
                    dve.wait_ge(read_a, it.read)
                    for tt, c in ((0, slice(0, P)), (1, slice(P, SC))):
                        wt = ifw[:, 8 * tt + h:8 * tt + h + 1]
                        src = soft[it.ix % 2][:, c]
                        if h == 0:
                            ins = dve.tensor_scalar(index[:, c], src, wt, None, ALU.mult)
                        else:
                            ins = dve.scalar_tensor_tensor(index[:, c], src, wt, index[:, c], ALU.mult, ALU.add)
                    ins.then_inc(indexed, 1)
                    dve.wait_ge(indexed, it.ix + 1)
                    if h == NH - 1:
                        link(dve.tensor_tensor(index, index, causal, ALU.add))

                def top_round(k):
                    for tt, c in ((0, slice(0, P)), (1, slice(P, SC))):
                        src = index if k == 0 else work
                        ins = dve.max(m8[:, 8 * tt:8 * tt + 8], src[:, c])
                    link(ins)
                    if k < TOPK // 8 - 1:
                        for tt, c in ((0, slice(0, P)), (1, slice(P, SC))):
                            ins = dve.match_replace(work[:, c], m8[:, 8 * tt:8 * tt + 8], src[:, c], -3e38)
                        link(ins)

                def select(tt):
                    c = (slice(0, P), slice(P, SC))[tt]
                    thr = m8[:, 8 * tt + 7:8 * tt + 8]
                    n = ngt[:, tt:tt + 1]
                    link(dve.tensor_scalar(sel[:, c], index[:, c], thr, None, ALU.is_gt, ALU.add, accum_out=n))
                    dve.tensor_scalar(n, n, -1.0, float(TOPK), ALU.mult, ALU.add)
                    eq, cs = soft[0][:, c], soft[1][:, c]
                    link(dve.tensor_scalar(eq, index[:, c], thr, None, ALU.is_equal))
                    link(dve.tensor_tensor_scan(cs, eq, eq, 0.0, ALU.add, ALU.max))
                    link(dve.scalar_tensor_tensor(cs, cs, n, eq, ALU.is_le, ALU.mult))
                    link(dve.tensor_tensor(sel[:, c], sel[:, c], cs, ALU.add))
                    link(dve.tensor_scalar(sel[:, c], sel[:, c], -1.0, -NEG, ALU.add, ALU.mult))
                    dve.tensor_tensor(sel[:, c], sel[:, c], causal[:, c], ALU.add).then_inc(selected, 1)

                def cum_lo(it):
                    dve.wait_ge(cum_hi, 1)
                    dve.scalar_tensor_tensor(ncum_lo[:], bank[4 + it.i % 2][0:NH, 0:SEQ], -1.0, ncum_hi[:],
                                             ALU.mult, ALU.subtract).then_inc(read_d, 1)

                def y_turned(it):
                    br, tt = it.what
                    dve.wait_ge(y_hi, 4 * b + 2 * br + tt + 1)
                    t = slice(tt * P, (tt + 1) * P)
                    dve.tensor_tensor(yT_lo[br][:, :, t], bank[4 + it.i % 2][:].rearrange("p (k t) -> p k t", k=4),
                                      yT_hi[br][:, :, t], ALU.subtract).then_inc(read_d, 1)

                def merge(br, qs=range(4)):
                    for q in qs:
                        tt, n = Q_MIX[q]
                        if tt == 0:
                            dve.wait_ge(tile_done, TILES[ph] + PROJ + 2 * br + n + 1)
                        else:
                            dve.wait_ge(unit_used, BASE[ph] + 20 + 2 * br + n + 1)
                        dve.wait_ge(sigmoid, 4 * b + 2 * br + tt + 1)
                        c = slice(n * NB, (n + 1) * NB)
                        gt = gate[:, tt, br * DM + n * NB:br * DM + (n + 1) * NB]
                        dst = xg[:, tt, c] if br == 0 else gt
                        ins = dve.tensor_tensor(dst, gt, bank[2 * n + tt][:], ALU.mult)
                        if br == 1:
                            link(ins)
                            ins = dve.tensor_tensor(xg[:, tt, c], xg[:, tt, c], gt, ALU.add)
                        ins.then_inc(merged, 1)

                rounds = {21 + k: k for k in range(TOPK // 8)}
                for slot in range(LAST_SLOT):
                    j, q = divmod(slot, 4)
                    if b == 0 and slot == 9:
                        rotate()
                    if b == 0 and q == 0 and 7 <= j <= 10:
                        dve.wait_ge(tri_done, 1)
                        gate_rows(j - 1)
                    if b == 1:
                        if slot == 9:
                            narrow()
                        if slot == 12:
                            log_f()
                        if slot == 13:
                            norm_rows(0, 18)
                        if slot == 17:
                            norm_rows(512, 20)
                    for it in ITEMS[b]:
                        d = slot - it.slot
                        if (it.kind == "SM" and d == SM_AT["norm"]) or (it.kind == "SB" and d == SB_AT["norm"]):
                            finish_head(it)
                        if it.kind == "SB" and d == SB_AT["weigh"]:
                            sb_weigh(it)
                        if it.kind == "SB" and d == SB_AT["keep"]:
                            sb_keep(it)
                        if it.kind == "SB" and d == SB_AT["clamp"]:
                            sb_clamp(it)
                        if it.kind == "SM" and d == SM_AT["soft"]:
                            soften(it)
                        if it.kind == "IX" and d == 2:
                            accumulate(it)
                        if it.kind == "CU" and d == 1:
                            cum_lo(it)
                        if it.kind == "TY" and d == 1:
                            y_turned(it)
                    if slot == 44:
                        merge(0, (2, 3))
                        split_lo(next_units(ph, 10)[1])
                    if slot == 45:
                        merge(1, (0, 1))
                    if b == 1 and slot in rounds:
                        top_round(rounds[slot])
                    if q in (0, 2) and 0 < slot < 42:
                        for u in next_units(ph, j)[q // 2:q // 2 + 1]:
                            split_lo(u)
                    if b == 1 and slot in (29, 30):
                        select(slot - 29)
                    if slot == 43:
                        merge(0, (0, 1))
                def merged_lo(q):
                    tt, n = Q_MIX[q]
                    dve.wait_ge(mT_hi, 4 * b + q + 1)
                    t = slice(tt * P, (tt + 1) * P)
                    dve.tensor_tensor(xT_lo[:, 4 * n:4 * n + 4, t],
                                      bank[4 + q][:].rearrange("p (k t) -> p k t", k=4),
                                      xT_hi[:, 4 * n:4 * n + 4, t], ALU.subtract).then_inc(mT_lo, 1)

                split_lo(u0 + 24)
                merged_lo(0)
                merged_lo(1)
                merge(1, (2, 3))
                split_lo(u0 + 25)
                merged_lo(2)
                merged_lo(3)
                split_lo(u0 + 26)
                split_lo(u0 + 27)
                for u in next_units(ph, 13):
                    split_lo(u)

            ffn("F0")
            mixer(0)
            ffn("F1")
            ffn("F2")
            mixer(1)
            ffn("F3")
            for q, (tt, n) in enumerate(Q_FFN):
                c = slice(n * NB, (n + 1) * NB)
                wait_quarter(dve, "F3", q)
                dve.scalar_tensor_tensor(x[:, tt, c], acc_bank("F3", tt, n)[:], 0.5, x[:, tt, c],
                                         ALU.mult, ALU.add).then_inc(gained, 1)

        @block.tensor
        def _(pe):
            def three(dst, st, hi, lo, mhi, mlo, start, stop):
                pe.matmul(dst, st(hi), mhi, start=start, stop=False)
                pe.matmul(dst, st(hi), mlo, start=False, stop=False)
                return pe.matmul(dst, st(lo), mhi, start=False, stop=stop)

            def rows(u, width, k4, col=0, n=NB):
                o = k4 * width + col
                return w_hi[u % SLOTS][:, o:o + n], w_lo[u % SLOTS][:, o:o + n]

            def four(u, tt, dst, k0, first, last, n=NB, hi=xT_hi, lo=xT_lo):
                for k4 in range(4):
                    mh, ml = rows(u, n, k4, 0, n)
                    m = three(dst, lambda z, k=k0 + k4: z[:, k, tt * P:(tt + 1) * P], hi, lo, mh, ml,
                              first and k4 == 0, last and k4 == 3)
                return m

            def turn_x(ph, q):
                tt, n = quarters(ph)[q]
                pe.wait_ge(gained, 4 * (3 if ph == "F2" else GAIN_OF[ph]) + q + 1)
                for k in range(4):
                    ins = pe.transpose(bank[turn_banks(ph)[q]][:, k * P:(k + 1) * P],
                                       xg[:, tt, n * NB + k * P:n * NB + (k + 1) * P], ident)
                ins.then_inc(x_turned, 1)

            def begin(ph, batch):
                if ph == "F0":
                    for hf in range(2):
                        if hf == 0:
                            turn_x(ph, 0)
                            turn_x(ph, 1)
                        batch(0, hf)
                        if hf == 0:
                            turn_x(ph, 2)
                            turn_x(ph, 3)
                        batch(1, hf)
                    return
                turn_x(ph, EARLY[ph])
                batch(0, 0)
                for q in range(EARLY[ph] + 1, 4):
                    turn_x(ph, q)
                batch(0, 1)
                batch(1, 0)
                batch(1, 1)

            def chunk_tile(ph, c, hf, tt, i=0):
                m = four(BASE[ph] + 2 * c + hf, tt, bank[2 * (c % 2) + tt][:], 4 * hf, hf == 0, hf == 1)
                if tt == 1:
                    m.then_inc(unit_used, 1)
                elif hf == 1:
                    m.then_inc(tile_done, 1)

            def first_chunk(ph, tt, hf):
                pe.wait_ge(lo_done, BASE[ph] + hf + 1)
                pe.wait_ge(xT_lo_done, 4 * PREP_OF[ph] + quarters(ph).index((tt, hf)) + 1)
                chunk_tile(ph, 0, hf, tt)

            def chunk(ph, c, hf, i=0):
                pe.wait_ge(lo_done, BASE[ph] + 2 * c + hf + 1 + 4 * i)
                for tt in range(TT):
                    chunk_tile(ph, c, hf, tt, i)

            def turn_hidden(ph, c, i=0):
                for tt in range(TT):
                    pe.wait_ge(h_done, 2 * NCH * FFN_OF[ph] + 2 * c + tt + 1 + 4 * i)
                    for k in range(2):
                        ins = pe.transpose(bank[6 + c % 2][:, k * SEQ + tt * P:k * SEQ + (tt + 1) * P],
                                           hs[c % 2][tt][:, k * P:(k + 1) * P], ident)
                ins.then_inc(h_turned, 1)

            def ffn(ph):
                begin(ph, lambda tt, hf: first_chunk(ph, tt, hf))
                with pe.Fori(0, (NCH - 1) // 2) as i:
                    for j in range(2):
                        chunk(ph, 1 + j, 0, i)
                        turn_hidden(ph, j, i)
                        chunk(ph, 1 + j, 1, i)
                for d in range(NCH):
                    u = BASE[ph] + 2 * NCH + d
                    pe.wait_ge(lo_done, u + 1)
                    pe.wait_ge(hT_lo_done, NCH * FFN_OF[ph] + d + 1)
                    for q, (tt, n) in enumerate(Q_FFN):
                        if d == NCH - 1 and q == 3 and ph in NEXT:
                            turn_x(NEXT[ph], 0)
                        for k in range(2):
                            mh, ml = rows(u, DM, k, n * NB)
                            m = three(acc_bank(ph, tt, n)[:], lambda z: z[:, 2 * d + k, tt * P:(tt + 1) * P],
                                      hT_hi, hT_lo, mh, ml, d == 0 and k == 0, d == NCH - 1 and k == 1)
                        if d == NCH - 1 and q < 3:
                            m.then_inc(tile_done, 1)
                    m.then_inc(unit_used, 1)
                    if d == 0:
                        turn_hidden(ph, NCH - 1)
                    if ph == "F0" and d == 1:
                        pe.wait_ge(table_in, 32)
                        pe.matmul(bank[1][0:NH, 0:SC], lgt[0:32, 0:NH], onehot, start=True, stop=True)\
                            .then_inc(vrow_mm, 1)

            def mixer(b):
                ph = ("M0", "M1")[b]
                u0 = BASE[ph]
                if b == 0:
                    pe.wait_ge(const_in, 16)
                    pe.wait_ge(vrow_sb, 1)

                def score_bank(it):
                    if it.i >= 2:
                        was = FLAT[it.i - 2]
                        pe.wait_ge(read_sem(was), was.read)
                    return bank[4 + it.i % 2]

                def read_sem(was):
                    return read_d if was.reader == "d" else read_a

                def turn(it):
                    name, tt = it.what if it.kind == "TR" else ("cu", 0)
                    if b == 0:
                        if name in ("qa", "ka"):
                            pe.wait_ge(rows_ready, 2)
                        else:
                            pe.wait_ge(evac_act, {"qb": 8, "kb": 10}[name])
                    elif name == "iq":
                        pe.wait_ge(evac_act, 14)
                    else:
                        if name == "kk":
                            pe.wait_ge(evac_act, 16)
                        if name == "dq":
                            pe.wait_ge(dq_ready, 1)
                        else:
                            pe.wait_ge(rows_ready, {"kk": 3, "cu": 4, "fq": 5, "fk": 6}[name])
                    S = score_bank(it)
                    if name == "cu":
                        pe.matmul(S[0:NH, 0:P], lgf[:, 0:8], tri_le, start=True, stop=True)
                        pe.matmul(S[0:NH, P:SEQ], lgf[:, 0:8], ones, start=True, stop=False)
                        pe.matmul(S[0:NH, P:SEQ], lgf[:, 8:16], tri_le, start=False, stop=True).then_inc(scored, 1)
                        return
                    c0 = {"qa": 0, "ka": 512, "qb": 0, "kb": 512, "iq": 0, "kk": 512, "fq": 0, "fk": 512, "dq": 0}[name]
                    n = 2 if name == "kk" else 4
                    for k in range(n):
                        ins = pe.transpose(S[:, k * P:(k + 1) * P], xg[:, tt, c0 + k * P:c0 + (k + 1) * P], ident)
                    ins.then_inc(scored, 1)

                def operands(it):
                    kind, h = it.what if it.kind != "IX" else ("idx", it.what)
                    r = slice(HD * (h % 2), HD * (h % 2) + HD)
                    c = slice(h * HD, (h + 1) * HD)
                    iqT = y[1][:].rearrange("p t (k n) -> p (t k) n", k=2)
                    if kind in ("moba", "fox"):
                        return qT_a[r, h // 2, :], kT_a[r, h // 2, :], v_a[:, :, c]
                    if kind == "sb":
                        return qT_b[r, h // 2, :], kT_b[r, h // 2, :], v_b[:, :, c]
                    if kind == "dsa":
                        return qT_b[r, h // 2, :], dkT[r, :], dv[:]
                    return iqT[r, h // 2, :], ikT[r, :], None

                def scores(it):
                    kind, h = it.what if it.kind != "IX" else ("idx", it.what)
                    need = {"moba": "ka", "fox": "fk", "sb": "kb", "dsa": "dq", "idx": "kk"}[kind]
                    pe.wait_ge(read_a, max(t.read for t in ITEMS[b] if t.kind == "TR" and t.what[0] == need))
                    S = score_bank(it)
                    q, k, _ = operands(it)
                    if kind == "fox":
                        pe.wait_ge(read_d, next(t.read for t in ITEMS[b] if t.kind == "CU"))
                        one = pick[:, h:h + 1].to_broadcast([NH, P])
                        pe.matmul(S[:, 0:P], q[:, 0:P], k[:, 0:P], start=True, stop=False)
                        pe.matmul(S[:, 0:P], one, ncum_hi[:, 0:P], start=False, stop=False)
                        pe.matmul(S[:, 0:P], one, ncum_lo[:, 0:P], start=False, stop=True)
                        pe.matmul(S[:, P:SC], q[:, P:SEQ], k, start=True, stop=False)
                        pe.matmul(S[:, P:SC], one, ncum_hi[:], start=False, stop=False)
                        pe.matmul(S[:, P:SC], one, ncum_lo[:], start=False, stop=True).then_inc(scored, 1)
                    elif kind == "sb":
                        pe.matmul(S[:, 0:SEQ], k[:, 0:P], q, start=True, stop=True)
                        pe.matmul(S[:, SEQ:SC], k[:, P:SEQ], q[:, P:SEQ], start=True, stop=True).then_inc(scored, 1)
                    else:
                        pe.matmul(S[:, 0:P], q[:, 0:P], k[:, 0:P], start=True, stop=True)
                        pe.matmul(S[:, P:SC], q[:, P:SEQ], k, start=True, stop=True).then_inc(scored, 1)

                def turn_free(it):
                    if it.m >= 2:
                        pe.wait_ge(head_read, it.m - 1)
                    return head_bank(it)

                def turn_probs(it):
                    pe.wait_ge(exped, it.softs + 1)
                    B = turn_free(it)
                    for k in range(3):
                        ins = pe.transpose(B[:, k * P:(k + 1) * P], prob[it.m % 2][:, k * P:(k + 1) * P], ident)
                    ins.then_inc(turned, 1)

                def sb_sum(it):
                    pe.wait_ge(tri_done, 1)
                    pe.wait_ge(kept, it.sbs + 1)
                    B = turn_free(it)
                    tri, one = tri_r[:, 0:P], tri_r[:, P:2 * P]
                    hi, lo = soft_hi[it.m % 2], soft_lo[it.m % 2]
                    pe.matmul(B[:, 0:SC], tri, hi[:], start=True, stop=False)
                    pe.matmul(B[:, 0:SC], tri, lo[:], start=False, stop=False)
                    pe.matmul(B[:, P:SEQ], one, hi[:, SEQ:SC], start=False, stop=False)
                    pe.matmul(B[:, P:SEQ], one, lo[:, SEQ:SC], start=False, stop=True).then_inc(turned, 1)

                def head(it):
                    if it.kind == "SM":
                        pe.wait_ge(copied, it.softs + 1)
                        w = probT[it.m % 2]
                    else:
                        pe.wait_ge(w_done, it.sbs + 1)
                        w = prob[it.m % 2]
                    _, _, v = operands(it)
                    O = head_bank(it)[:, SC:NB]
                    pe.matmul(O[:, 0:HD], w[:, 0:P], v[:, 0, :], start=True, stop=True)
                    pe.matmul(O[:, HD:P], w[:, P:SEQ], v[:, 0, :], start=True, stop=False)
                    pe.matmul(O[:, HD:P], w[:, SEQ:SC], v[:, 1, :], start=False, stop=True).then_inc(head_out, 1)

                def y_turn(it):
                    br, tt = it.what
                    last = max(t.m for t in HEADS if t.b == b and (t.what[0] in ("moba", "fox")) == (br == 0))
                    pe.wait_ge(head_read, last + 1)
                    S = score_bank(it)
                    for k in range(4):
                        ins = pe.transpose(S[:, k * P:(k + 1) * P], y[br][:, tt, k * P:(k + 1) * P], ident)
                    ins.then_inc(scored, 1)

                def project(j, hf, tt):
                    u = u0 + 2 * j + hf
                    pe.wait_ge(lo_done, u + 1)
                    n = NB if proj_at[b][j] is not None else NW
                    if j == 0:
                        pe.wait_ge(xT_lo_done, 4 * PREP_OF[ph] + quarters(ph).index((tt, hf)) + 1)
                    if j >= 2 and hf == 0 and tt == 0:
                        if j - 2 < 6:
                            pe.wait_ge(evac_act, 12 * b + 2 * (j - 1))
                        elif b == 0:
                            pe.wait_ge(evac_dve, 2 * (j - 7))
                        else:
                            pe.wait_ge(gated, 2 * (j - 7))
                    m = four(u, tt, bank[2 * (j % 2) + tt][:, 0:n], 4 * hf, hf == 0, hf == 1, n)
                    if tt == 1:
                        m.then_inc(unit_used, 1)
                    elif hf == 1:
                        m.then_inc(tile_done, 1)

                def branch(br, q):
                    n, tt = divmod(q, 2)
                    u = u0 + 20 + 2 * br + n
                    pe.wait_ge(lo_done, u + 1)
                    ty = [t for t in ITEMS[b] if t.kind == "TY" and t.what == (br, tt)][0]
                    pe.wait_ge(read_d, ty.read)
                    if br == 0:
                        pe.wait_ge(gated if b else evac_dve, 6 + 2 * n)
                    else:
                        pe.wait_ge(merged, 8 * b + q + 1)
                    m = four(u, tt, bank[2 * n + tt][:], 0, True, True, hi=yT_hi[br], lo=yT_lo[br])
                    m.then_inc(unit_used if tt else tile_done, 1)

                begin(ph, lambda tt, hf: project(0, hf, tt))
                for slot in range(4, LAST_SLOT):
                    j, q = divmod(slot, 4)
                    if slot == TY_AT[1]:
                        for it in ITEMS[b]:
                            if it.kind == "TY" and it.slot == slot:
                                y_turn(it)
                    if j < PROJ:
                        project(j, q // 2, q % 2)
                    elif slot < 44:
                        branch(0, q)
                    for it in ITEMS[b]:
                        d = slot - it.slot
                        if (it.kind == "SM" and d == SM_AT["out"]) or (it.kind == "SB" and d == SB_AT["out"]):
                            head(it)
                        if it.kind == "SB" and d == SB_AT["sum"]:
                            sb_sum(it)
                        if it.kind == "SM" and d == SM_AT["turn"]:
                            turn_probs(it)
                        if it.kind in ("TR", "CU") and d == 0:
                            turn(it)
                        if it.kind in ("SM", "SB", "IX") and d == 0:
                            scores(it)
                        if it.kind == "TY" and d == 0 and slot != TY_AT[1]:
                            y_turn(it)
                def turn_merged(q):
                    tt, n = Q_MIX[q]
                    pe.wait_ge(merged, 8 * b + 4 + q + 1)
                    for k in range(4):
                        ins = pe.transpose(bank[4 + q][:, k * P:(k + 1) * P],
                                           xg[:, tt, n * NB + k * P:n * NB + (k + 1) * P], ident)
                    ins.then_inc(m_turned, 1)

                def output(n, hf, tt):
                    u = u0 + 24 + 2 * n + hf
                    pe.wait_ge(lo_done, u + 1)
                    pe.wait_ge(mT_lo, 4 * b + Q_MIX.index((tt, hf)) + 1)
                    m = four(u, tt, bank[2 * n + tt][:], 4 * hf, hf == 0, hf == 1)
                    if tt == 1:
                        m.then_inc(unit_used, 1)
                    elif hf == 1:
                        m.then_inc(tile_done, 1)

                for q in range(3):
                    branch(1, q)
                turn_merged(0)
                turn_merged(1)
                branch(1, 3)
                output(0, 0, 0)
                turn_merged(2)
                turn_merged(3)
                output(0, 0, 1)
                for n, hf in ((0, 1), (1, 0), (1, 1)):
                    output(n, hf, 0)
                    if (n, hf) == (1, 1):
                        turn_x(NEXT[ph], 0)
                        turn_x(NEXT[ph], 1)
                    output(n, hf, 1)

            pe.wait_ge(ident_in, 16)
            for ph in PHASES:
                if ph[0] == "F":
                    ffn(ph)
                else:
                    mixer(int(ph[1]))


def lag_buckets(n_buckets, max_distance, lags):
    import numpy as np
    exact = n_buckets // 2
    rel = np.maximum(lags, 1).astype(np.float32)
    large = exact + (np.log(rel / np.float32(exact)) / np.float32(np.log(max_distance / exact))
                     * np.float32(n_buckets - exact)).astype(np.int32)
    return np.where(lags < exact, lags, np.minimum(large, n_buckets - 1))


def constants():
    import numpy as np
    c = np.zeros((P, C_ALL), np.float32)
    p, f = np.arange(P)[:, None], np.arange(P)[None, :]
    c[:, C_ID:C_ID + P] = p == f
    c[:, C_CAUSAL:C_CAUSAL + P] = c[:, C_CAUSAL + 2 * P:C_CAUSAL + 3 * P] = np.where(f <= p, 0, NEG)
    c[:, C_PAST:C_PAST + P] = c[:, C_PAST + 2 * P:C_PAST + 3 * P] = np.where(p < f, 0, NEG)
    c[:, C_GE:C_GE + P] = p >= f
    c[:, C_ONE:C_ONE + P] = 1
    c[:, C_LE:C_LE + P] = p <= f
    bucket = lag_buckets(32, 128, np.maximum(SEQ - 1 - np.arange(SC), 0))
    onehot = (np.arange(32)[:, None] == bucket[None, :]).astype(np.float32)
    return c, onehot


def kernel(**inputs):
    import numpy as np
    import concourse.bacc as bacc
    from concourse.bass_utils import run_bass_kernel_spmd

    nc = bacc.Bacc("TRN2", target_bir_lowering=False, num_devices=1)
    arrays, aps = {}, {}
    consts, onehot = constants()
    shape_only = {"consts": consts, "onehot": onehot}
    for name, v in {**inputs, **shape_only}.items():
        v = np.ascontiguousarray(v)
        if v.ndim > 1 and v.shape[0] == 1 and name not in ("x", "positions"):
            v = v[0]
        arrays["in_" + name] = v
        aps[name] = nc.dram_tensor("in_" + name, v.shape, mybir.dt.from_np(v.dtype), kind="ExternalInput").ap()
    o = nc.dram_tensor("result", (1, SEQ, DM), F32, kind="ExternalOutput").ap()
    build(nc, aps, o)
    r = run_bass_kernel_spmd(nc, [arrays], core_ids=[0])
    return r.results[0]["result"]
```
